# Optimizing a Trainium2 kernel written in Bass

```python
import jax, jax.numpy as jnp
from jax import lax
import numpy as np

D_MODEL = 1024
BATCH = 1
SEQ = 1024
DEPTH = 2

GRID_W = 64
CTX_LEN = 256
N_MIXERS = 2
POS_BASE = 10000.0
EPS = 1e-6
CONV_WIDTH = 31
CONV_PAD = CONV_WIDTH // 2
GLA_HEADS = 4
GLA_KEY_DIM = D_MODEL // 2
GLA_VAL_DIM = D_MODEL
GLA_HEAD_K = GLA_KEY_DIM // GLA_HEADS
GLA_HEAD_V = GLA_VAL_DIM // GLA_HEADS
GLA_GATE_RANK = 16
GLA_GATE_NORM = 16.0
GLA_CHUNK = 64
GLA_IN_DIM = 2 * GLA_KEY_DIM + 2 * GLA_VAL_DIM + 2 * GLA_GATE_RANK
MOE_GROUPS = 4
MOE_PER_GROUP = 8
MOE_EXPERTS = MOE_GROUPS * MOE_PER_GROUP
MOE_TOP_K = 2
MOE_FF = D_MODEL // 2
MOE_BLOCK = 128
N_CONV_LAYERS = (DEPTH + 1) // 2
N_GLA_LAYERS = DEPTH // 2

kernel_name = 'hybrid_conv_gla_hmoe_prefix_dit'

def rmsnorm(x, g):
    xf = x.astype(jnp.float32)
    y = xf * lax.rsqrt(jnp.mean(xf * xf, axis=-1, keepdims=True) + EPS)
    return (y * g).astype(x.dtype)

def layernorm(x, g, b):
    xf = x.astype(jnp.float32)
    mu = jnp.mean(xf, axis=-1, keepdims=True)
    var = jnp.mean(jnp.square(xf - mu), axis=-1, keepdims=True)
    return ((xf - mu) * lax.rsqrt(var + EPS) * g + b).astype(x.dtype)

def modulate(h, shift, scale):
    return h * (1 + scale) + shift

def sincos_2d(rows, width, dim):
    quarter = dim // 4
    omega = 1.0 / (POS_BASE ** (jnp.arange(quarter, dtype=jnp.float32) / quarter))
    r = jnp.broadcast_to(jnp.arange(rows, dtype=jnp.float32)[:, None], (rows, width)).reshape(-1)
    col = jnp.broadcast_to(jnp.arange(width, dtype=jnp.float32)[None, :], (rows, width)).reshape(-1)
    ar = r[:, None] * omega
    ac = col[:, None] * omega
    return jnp.concatenate([jnp.sin(ar), jnp.cos(ar), jnp.sin(ac), jnp.cos(ac)], axis=-1)

def conv_module(h, pw1_w, pw1_b, dw_w, dw_b, ln_g, ln_b, pw2_w, pw2_b):
    d = h.shape[-1]
    a, g = jnp.split(h @ pw1_w + pw1_b, 2, axis=-1)
    u = a * jax.nn.sigmoid(g)
    u = lax.conv_general_dilated(u, dw_w[:, None, :], window_strides=(1,),
                                 padding=[(CONV_PAD, CONV_PAD)],
                                 dimension_numbers=('NWC', 'WIO', 'NWC'),
                                 feature_group_count=d) + dw_b
    u = jax.nn.silu(layernorm(u, ln_g, ln_b))
    return u @ pw2_w + pw2_b

def gla_project(h, w_in, gk_up, gk_b):
    b, l, _ = h.shape
    z = h @ w_in
    idx = [GLA_KEY_DIM, 2 * GLA_KEY_DIM, 2 * GLA_KEY_DIM + GLA_VAL_DIM,
           2 * GLA_KEY_DIM + 2 * GLA_VAL_DIM, 2 * GLA_KEY_DIM + 2 * GLA_VAL_DIM + GLA_GATE_RANK]
    q, k, v, gate, lr_f, lr_b = jnp.split(z, idx, axis=-1)

    def heads(t, d):
        return t.reshape(b, l, GLA_HEADS, d).transpose(0, 2, 1, 3).astype(jnp.float32)

    log_f = jax.nn.log_sigmoid((lr_f @ gk_up[0] + gk_b[0]).astype(jnp.float32)) / GLA_GATE_NORM
    log_b = jax.nn.log_sigmoid((lr_b @ gk_up[1] + gk_b[1]).astype(jnp.float32)) / GLA_GATE_NORM
    q = heads(q, GLA_HEAD_K) * (GLA_HEAD_K ** -0.5)
    return (q, heads(k, GLA_HEAD_K), heads(v, GLA_HEAD_V), gate,
            heads(log_f, GLA_HEAD_K), heads(log_b, GLA_HEAD_K))

def gla_scan(q, k, v, logg, s0, with_out):
    b, h, l, _ = q.shape
    dv = v.shape[-1]
    n = l // GLA_CHUNK
    mask = jnp.tril(jnp.ones((GLA_CHUNK, GLA_CHUNK), dtype=bool))

    def chunks(t):
        return t.reshape(b, h, n, GLA_CHUNK, t.shape[-1]).transpose(2, 0, 1, 3, 4)

    def body(s, inp):
        qc, kc, vc, gc = inp
        cum = jnp.cumsum(gc, axis=-2)
        last = cum[..., -1:, :]
        s_new = (jnp.exp(last)[..., 0, :, None] * s
                 + jnp.einsum('bhcd,bhce->bhde', kc * jnp.exp(last - cum), vc))
        if not with_out:
            return s_new, None
        ref = cum[..., GLA_CHUNK // 2:GLA_CHUNK // 2 + 1, :]
        att = jnp.einsum('bhid,bhjd->bhij', qc * jnp.exp(cum - ref), kc * jnp.exp(ref - cum))
        att = jnp.where(mask, att, 0.0)
        o = (jnp.einsum('bhij,bhje->bhie', att, vc)
             + jnp.einsum('bhid,bhde->bhie', qc * jnp.exp(cum), s))
        return s_new, o

    s_fin, o = lax.scan(body, s0, (chunks(q), chunks(k), chunks(v), chunks(logg)))
    if not with_out:
        return s_fin, None
    return s_fin, o.transpose(1, 2, 0, 3, 4).reshape(b, h, l, dv)

def gla_bidir(q, k, v, log_f, log_b, s0_f, s0_b, with_out):
    flip = lambda t: t[:, :, ::-1]
    s_f, o_f = gla_scan(q, k, v, log_f, s0_f, with_out)
    s_b, o_b = gla_scan(flip(q), flip(k), flip(v), flip(log_b), s0_b, with_out)
    if not with_out:
        return s_f, s_b, None
    return s_f, s_b, o_f + flip(o_b)

def gla_output(o, gate, head_g, w_o):
    b, h, l, dv = o.shape
    on = o * lax.rsqrt(jnp.mean(o * o, axis=-1, keepdims=True) + EPS)
    on = on.transpose(0, 2, 1, 3).reshape(b, l, h * dv) * head_g
    return (on.astype(gate.dtype) * jax.nn.silu(gate)) @ w_o

def gla_mixer(h_ctx, h_lat, w_in, gk_up, gk_b, head_g, w_o, ctx_out):
    b = h_lat.shape[0]
    qc, kc, vc, gate_c, fc, bc = gla_project(h_ctx, w_in, gk_up, gk_b)
    zero = jnp.zeros((b, GLA_HEADS, GLA_HEAD_K, GLA_HEAD_V), jnp.float32)
    s_f, s_b, o_ctx = gla_bidir(qc, kc, vc, fc, bc, zero, zero, ctx_out)
    ql, kl, vl, gate_l, fl, bl = gla_project(h_lat, w_in, gk_up, gk_b)
    _, _, o_lat = gla_bidir(ql, kl, vl, fl, bl, s_f, s_b, True)
    y_lat = gla_output(o_lat, gate_l, head_g, w_o)
    y_ctx = gla_output(o_ctx, gate_c, head_g, w_o) if ctx_out else None
    return y_ctx, y_lat

def hier_moe(h, wg, bg, wr, br, w1, w3, w2):
    t, d = h.shape
    hf = h.astype(jnp.float32)
    g_logits = hf @ wg.astype(jnp.float32) + bg.astype(jnp.float32)
    g_prob = jax.nn.softmax(g_logits, axis=-1)
    g_idx = jnp.argmax(g_logits, axis=-1)
    g_w = jnp.take_along_axis(g_prob, g_idx[:, None], axis=-1)
    inner = (hf @ wr.astype(jnp.float32) + br.astype(jnp.float32)).reshape(t, MOE_GROUPS, MOE_PER_GROUP)
    sel = jnp.broadcast_to(g_idx[:, None, None], (t, 1, MOE_PER_GROUP))
    inner = jnp.take_along_axis(inner, sel, axis=1)[:, 0]
    top_v, top_i = lax.top_k(inner, MOE_TOP_K)
    top_w = jax.nn.softmax(top_v, axis=-1) * g_w
    expert = g_idx[:, None] * MOE_PER_GROUP + top_i

    a = t * MOE_TOP_K
    e_flat = expert.reshape(-1)
    w_flat = top_w.reshape(-1)
    tok_flat = jnp.repeat(jnp.arange(t, dtype=jnp.int32), MOE_TOP_K)
    order = jnp.argsort(e_flat)
    se, st, sw = e_flat[order], tok_flat[order], w_flat[order]
    counts = jnp.bincount(e_flat, length=MOE_EXPERTS)
    start = jnp.cumsum(counts) - counts
    padded = ((counts + MOE_BLOCK - 1) // MOE_BLOCK) * MOE_BLOCK
    pend = jnp.cumsum(padded)
    pstart = pend - padded
    dest = pstart[se] + (jnp.arange(a) - start[se])
    n_blocks = -(-a // MOE_BLOCK) + MOE_EXPERTS
    p = n_blocks * MOE_BLOCK
    tok_buf = jnp.full((p,), t, jnp.int32).at[dest].set(st)
    w_buf = jnp.zeros((p,), jnp.float32).at[dest].set(sw)
    blk_e = jnp.clip(jnp.searchsorted(pend, jnp.arange(n_blocks) * MOE_BLOCK, side='right'),
                     0, MOE_EXPERTS - 1)
    h_pad = jnp.concatenate([h, jnp.zeros((1, d), h.dtype)], axis=0)

    def block_ffn(args):
        e, idx = args
        xb = h_pad[idx]
        return (jax.nn.silu(xb @ w1[e]) * (xb @ w3[e])) @ w2[e]

    y = lax.map(block_ffn, (blk_e, tok_buf.reshape(n_blocks, MOE_BLOCK)))
    out = jnp.zeros((t + 1, d), jnp.float32).at[tok_buf].add(
        y.reshape(p, d).astype(jnp.float32) * w_buf[:, None])
    return out[:t].astype(h.dtype)

def setup_inputs(seed: int = 0) -> dict:
    key = jax.random.key(seed)
    ks = iter(jax.random.split(key, 32))
    nrm = lambda shape, scale: jax.random.normal(next(ks), shape, jnp.float32) * scale
    d, l, lc, lg = D_MODEL, DEPTH, N_CONV_LAYERS, N_GLA_LAYERS
    e, f = MOE_EXPERTS, MOE_FF
    return {
        'x': nrm((BATCH, SEQ, d), 1.0),
        'c': nrm((BATCH, d), 1.0),
        'ctx': nrm((BATCH, CTX_LEN, d), 1.0),
        'c_ctx': nrm((d,), 1.0),
        'ada_w': nrm((l, d, 6 * d), 0.5 * d ** -0.5),
        'ada_b': nrm((l, 6 * d), 0.01),
        'norm_g': 1.0 + nrm((l, 2, d), 0.01),
        'final_g': 1.0 + nrm((d,), 0.01),
        'conv_pw1_w': nrm((lc, d, 2 * d), d ** -0.5),
        'conv_pw1_b': nrm((lc, 2 * d), 0.01),
        'conv_dw_w': nrm((lc, CONV_WIDTH, d), CONV_WIDTH ** -0.5),
        'conv_dw_b': nrm((lc, d), 0.01),
        'conv_ln_g': 1.0 + nrm((lc, d), 0.01),
        'conv_ln_b': nrm((lc, d), 0.01),
        'conv_pw2_w': nrm((lc, d, d), d ** -0.5),
        'conv_pw2_b': nrm((lc, d), 0.01),
        'gla_w_in': nrm((lg, d, GLA_IN_DIM), d ** -0.5),
        'gla_gk_up': nrm((lg, 2, GLA_GATE_RANK, GLA_KEY_DIM), GLA_GATE_RANK ** -0.5),
        'gla_gk_b': nrm((lg, 2, GLA_KEY_DIM), 0.1),
        'gla_head_g': 1.0 + nrm((lg, GLA_VAL_DIM), 0.01),
        'gla_w_o': nrm((lg, GLA_VAL_DIM, d), GLA_VAL_DIM ** -0.5),
        'moe_wg': nrm((l, d, MOE_GROUPS), d ** -0.5),
        'moe_bg': nrm((l, MOE_GROUPS), 0.01),
        'moe_wr': nrm((l, d, e), d ** -0.5),
        'moe_br': nrm((l, e), 0.01),
        'moe_w1': nrm((l, e, d, f), d ** -0.5),
        'moe_w3': nrm((l, e, d, f), d ** -0.5),
        'moe_w2': nrm((l, e, f, d), f ** -0.5),
    }

def reference(x, c, ctx, c_ctx, ada_w, ada_b, norm_g, final_g,
              conv_pw1_w, conv_pw1_b, conv_dw_w, conv_dw_b, conv_ln_g, conv_ln_b,
              conv_pw2_w, conv_pw2_b, gla_w_in, gla_gk_up, gla_gk_b, gla_head_g, gla_w_o,
              moe_wg, moe_bg, moe_wr, moe_br, moe_w1, moe_w3, moe_w2):
    b, l, d = x.shape
    ROWS = l // GRID_W
    x = x + sincos_2d(ROWS, GRID_W, d).astype(x.dtype)[None]
    xc = ctx
    s_lat = jax.nn.silu(c)
    s_ctx = jax.nn.silu(c_ctx)
    for i in range(DEPTH):
        mixer, j = i % N_MIXERS, i // N_MIXERS
        ctx_live = any((m % N_MIXERS) == 1 for m in range(i + 1, DEPTH))
        mod_l = (s_lat @ ada_w[i] + ada_b[i])[:, None, :]
        mod_c = (s_ctx @ ada_w[i] + ada_b[i])[None, None, :]
        sh1, sc1, g1, sh2, sc2, g2 = jnp.split(mod_l, 6, axis=-1)
        csh1, csc1, cg1, csh2, csc2, cg2 = jnp.split(mod_c, 6, axis=-1)

        h_lat = modulate(rmsnorm(x, norm_g[i, 0]), sh1, sc1)
        if mixer == 0:
            cw = (conv_pw1_w[j], conv_pw1_b[j], conv_dw_w[j], conv_dw_b[j],
                  conv_ln_g[j], conv_ln_b[j], conv_pw2_w[j], conv_pw2_b[j])
            y_lat = conv_module(h_lat, *cw)
            if ctx_live:
                y_ctx = conv_module(modulate(rmsnorm(xc, norm_g[i, 0]), csh1, csc1), *cw)
        else:
            h_ctx = modulate(rmsnorm(xc, norm_g[i, 0]), csh1, csc1)
            y_ctx, y_lat = gla_mixer(h_ctx, h_lat, gla_w_in[j], gla_gk_up[j], gla_gk_b[j],
                                     gla_head_g[j], gla_w_o[j], ctx_live)
        x = x + g1 * y_lat
        if ctx_live:
            xc = xc + cg1 * y_ctx

        mw = (moe_wg[i], moe_bg[i], moe_wr[i], moe_br[i], moe_w1[i], moe_w3[i], moe_w2[i])
        h_lat = modulate(rmsnorm(x, norm_g[i, 1]), sh2, sc2)
        if ctx_live:
            h_ctx = modulate(rmsnorm(xc, norm_g[i, 1]), csh2, csc2)
            n_ctx = xc.shape[0] * xc.shape[1]
            out = hier_moe(jnp.concatenate([h_ctx.reshape(-1, d), h_lat.reshape(-1, d)], axis=0), *mw)
            xc = xc + cg2 * out[:n_ctx].reshape(xc.shape)
            x = x + g2 * out[n_ctx:].reshape(x.shape)
        else:
            x = x + g2 * hier_moe(h_lat.reshape(-1, d), *mw).reshape(x.shape)
    return rmsnorm(x, final_g)


_drawn_inputs = setup_inputs


def setup_inputs(seed=0):
    import zlib

    import numpy as np

    out = dict(_drawn_inputs(seed))
    spreads = {}
    factors = {'ctx': 4.592,
     'c_ctx': 6.733,
     'ada_b': 3.537,
     'norm_g': 5.117,
     'final_g': 5.743,
     'conv_pw1_b': 8.0,
     'conv_dw_b': 8.0,
     'conv_ln_g': 8.0,
     'conv_ln_b': 8.0,
     'conv_pw2_b': 8.0,
     'gla_gk_b': 5.562,
     'gla_head_g': 8.0,
     'moe_bg': 6.245,
     'moe_br': 7.661}
    for name, (base, spread) in spreads.items():
        noise = np.random.default_rng([zlib.crc32(name.encode()), seed]).standard_normal(out[name].shape)
        drawn = base * np.exp(spread * noise) if base else spread * noise
        out[name] = __import__('jax').numpy.asarray(drawn.astype(out[name].dtype))
    for name, factor in factors.items():
        out[name] = (out[name] * factor).astype(out[name].dtype)
    return out
```

```python
import concourse.bass as bass
from concourse import mybir
import numpy as np
from contextlib import ExitStack

F32 = mybir.dt.float32
F32R = mybir.dt.float32r
I32 = mybir.dt.int32
U32 = mybir.dt.uint32
ACT = mybir.ActivationFunctionType
ALU = mybir.AluOpType
AX = mybir.AxisListType
ds = bass.ds

P = 128
D = 1024
KC = D // P
SEQ, CTX_LEN, GRID_W = 1024, 256, 64
TOK = SEQ + CTX_LEN
TILES = TOK // P
CTX_TILES = CTX_LEN // P
N = 512
EPS = 1e-6
TAPS, PAD = 31, 15
HEADS, DK, DV, CHUNK, RANK = 4, 128, 256, 64, 16
GLA_IN = 2 * HEADS * DK + 2 * HEADS * DV + 2 * RANK
GROUPS, PER_GROUP, EXPERTS, FF, BLK = 4, 8, 32, 512, 128
LAT, CTX = 0, 1
SH1, SC1, G1, SH2, SC2, G2 = range(6)
STREAMS = [(CTX, 0, CTX_TILES // 2, 0), (LAT, CTX_TILES, (TILES - CTX_TILES) // 2, CTX_TILES // 2)]
LAT_STREAMS = [(LAT, CTX_TILES, 1, 0), (LAT, CTX_TILES + 2, (TILES - CTX_TILES) // 2 - 1, 1)]
GAP = PAD + CTX_LEN + PAD
CONV_GROUPS = [(0, CTX_LEN, PAD), (CTX_LEN, N, GAP), (CTX_LEN + N, N, GAP + N)]
CONV_W = GAP + SEQ + PAD
CONV_OUT = GAP + SEQ - PAD
VEC_ROWS = TAPS + 5
V_DWB, V_LNG, V_LNB, V_BA, V_BG = range(TAPS, VEC_ROWS)


class Phase:
    POOL_DMA = ("stored", "h_stored", "o_stored", "gathered")
    pool_dma = []

    def __init__(self, nc, ctx, name):
        self.pool_used = 0
        self.nc, self.ctx, self.name, self.sems = nc, ctx, name, {}

    def sb(self, name, shape, dt=F32):
        return self.ctx.enter_context(self.nc.sbuf_tensor(f"{self.name}_{name}", shape, dt))

    def ps(self, name, shape, dt=F32):
        return self.ctx.enter_context(self.nc.psum_tensor(f"{self.name}_{name}", shape, dt))

    def sem(self, name):
        if name not in self.sems and name.rstrip("01234567") in self.POOL_DMA:
            if self.pool_used == len(self.pool_dma):
                self.pool_dma.append(self.nc.alloc_semaphore(f"pool_dma{self.pool_used}"))
            self.sems[name] = self.pool_dma[self.pool_used]
            self.pool_used += 1
        if name not in self.sems:
            self.sems[name] = self.ctx.enter_context(self.nc.semaphore(f"{self.name}_{name}"))
        return self.sems[name]

    def close(self):
        numbers = sorted(sem.num for sem in self.sems.values())
        with self.nc.Block() as block:
            @block.gpsimd
            def _(pool):
                for sem in self.pool_dma[:self.pool_used]:
                    pool.dma_reset(range(sem.num, sem.num + 1))
                start = numbers[0]
                for at, num in enumerate(numbers):
                    if at + 1 == len(numbers) or numbers[at + 1] != num + 1:
                        pool.sem_clear(range(start, num + 1))
                        start = numbers[min(at + 1, len(numbers) - 1)]


def chain(ph, eng, name):
    done = [0]

    def link(ins):
        done[0] += 1
        ins.then_inc(ph.sem(name), 1)
        eng.wait_ge(ph.sem(name), done[0])
    return link


def product3(pe, out, xh, xl, wh, wl, start, stop):
    pe.matmul(out, xh, wh, start=start, stop=False)
    pe.matmul(out, xh, wl, start=False, stop=False)
    return pe.matmul(out, xl, wh, start=False, stop=stop)


class Split:

    def __init__(self, nc, ctx, name, shape, side="left"):
        self.hi = ctx.enter_context(nc.sbuf_tensor(name + "_hi", shape, F32R, side=side))
        self.lo = ctx.enter_context(nc.sbuf_tensor(name + "_lo", shape, F32R, side=side))


def modulation(nc, d):
    with ExitStack() as ctx:
        ph = Phase(nc, ctx, "ada")
        s = ph.sem
        craw = ph.sb("craw", [P, 2, KC])
        cs = ph.sb("cs", [P, KC, 2])
        w = [ph.sb(f"w{l}", [P, KC, D]) for l in range(2)]
        row = ph.sb("row", [2, 2, 6, D])
        bias = ph.sb("bias", [2, 2, 6, D])
        gain = ph.sb("gain", [2, 2, 2, D])
        acc = [ph.ps(f"acc{l}", [P, D]) for l in range(2)]
        xin = [ph.sb(f"xin{b}", [P, D]) for b in range(2)]
        pos = [ph.sb(f"pos{b}", [P, D]) for b in range(2)]
        lat_tiles = TILES - CTX_TILES

        with nc.Block() as block:
            @block.sync
            def _(sp):
                for k, src in enumerate((d.c[0, :], d.c_ctx)):
                    sp.dma_start(craw[:, k, :], src.rearrange("(p k) -> p k", k=KC)).then_inc(s("c_loaded"), 16)
                for k in range(2):
                    sp.dma_start(bias[k:k + 1, :, :, :].rearrange("o l m n -> o (l m n)"),
                                 d.ada_b.rearrange("l n -> (l n)").unsqueeze(0)).then_inc(s("b_loaded"), 16)
                    sp.dma_start(gain[k:k + 1, :, :, :].rearrange("o l m n -> o (l m n)"),
                                 d.norm_g.rearrange("l m n -> (l m n)").unsqueeze(0)).then_inc(s("b_loaded"), 16)

                def load(l, m):
                    sp.dma_start(w[l][:, :, :], d.ada_w[l, :, ds(m * D, D)].rearrange("(p k) n -> p k n", k=KC))\
                        .then_inc(s(f"w_loaded{l}"), 16)

                for l in range(2):
                    load(l, 0)
                with sp.Fori(1, 6) as m:
                    for l in range(2):
                        sp.wait_ge(s(f"acc_ready{l}"), m)
                        load(l, m)
                sp.wait_ge(s("rows_done"), 4)
                for k, stream in enumerate((LAT, CTX)):
                    sp.dma_start(d.mods[:, stream, :, :], row[k:k + 1, :, :, :]).then_inc(s("mods_stored"), 16)
                sp.wait_ge(s("mods_stored"), 32)

            @block.scalar
            def _(act):
                act.dma_start(d.xs[0:CTX_LEN, :], d.ctx[0, :, :]).then_inc(s("ctx_copied"), 16)
                act.wait_ge(s("c_loaded"), 32)
                act.activation(cs[:, :, :].rearrange("p k s -> p s k"), craw[:, :, :], ACT.Silu)\
                    .then_inc(s("c_ready"), 1)
                for t in range(lat_tiles):
                    b = t % 2
                    if t >= 2:
                        act.wait_ge(s("x_stored"), 16 * (t - 1))
                    act.dma_start(xin[b][:, :], d.x[0, t * P:(t + 1) * P, :]).then_inc(s(f"x_loaded{b}"), 16)
                    for h in range(P // GRID_W):
                        r = t * (P // GRID_W) + h
                        act.dma_start(pos[b][h * GRID_W:(h + 1) * GRID_W, 0:N],
                                      d.pos_row[r, :].partition_broadcast(GRID_W)).then_inc(s(f"x_loaded{b}"), 16)
                        act.dma_start(pos[b][h * GRID_W:(h + 1) * GRID_W, N:D], d.pos_col)\
                            .then_inc(s(f"x_loaded{b}"), 16)
                    act.wait_ge(s("x_added"), t + 1)
                    act.dma_start(d.xs[CTX_LEN + t * P:CTX_LEN + (t + 1) * P, :], xin[b][:, :])\
                        .then_inc(s("x_stored"), 16)
                act.wait_ge(s("x_stored"), 16 * lat_tiles)
                act.wait_ge(s("ctx_copied"), 16)

            @block.gpsimd
            def _(pool):
                for t in range(lat_tiles):
                    b = t % 2
                    pool.wait_ge(s(f"x_loaded{b}"), 80 * (t // 2 + 1))
                    pool.tensor_tensor(xin[b][:, :], xin[b][:, :], pos[b][:, :], ALU.add).then_inc(s("x_added"), 1)

            @block.tensor
            def _(pe):
                pe.wait_ge(s("c_ready"), 1)

                def product(l, m):
                    pe.wait_ge(s(f"w_loaded{l}"), m * 16 + 16)
                    for h in range(2):
                        for k in range(KC):
                            last = pe.matmul(acc[l][0:2, h * N:(h + 1) * N], cs[:, k, :],
                                             w[l][:, k, h * N:(h + 1) * N], start=k == 0, stop=k == KC - 1)
                    last.then_inc(s(f"acc_ready{l}"), 1)

                for l in range(2):
                    product(l, 0)
                with pe.Fori(1, 6) as m:
                    for l in range(2):
                        pe.wait_ge(s(f"row_ready{l}"), m)
                        product(l, m)

            @block.vector
            def _(dve):
                dve.wait_ge(s("b_loaded"), 64)
                with dve.Fori(0, 6) as m:
                    for l in range(2):
                        dve.wait_ge(s(f"acc_ready{l}"), m + 1)
                        dve.tensor_tensor(row[:, l, ds(m, 1), :].rearrange("p o n -> p (o n)"), acc[l][0:2, :],
                                          bias[:, l, ds(m, 1), :].rearrange("p o n -> p (o n)"), ALU.add)\
                            .then_inc(s(f"row_ready{l}"), 1)
                for l in range(2):
                    dve.wait_ge(s(f"row_ready{l}"), 6)
                for l in range(2):
                    for j, m in enumerate((SC1, SC2)):
                        dve.scalar_tensor_tensor(row[:, l, m, :], row[:, l, m, :], 1.0, gain[:, l, j, :],
                                                 ALU.add, ALU.mult).then_inc(s("rows_done"), 1)
        ph.close()


def norm_stage(ph, nc, d, layer, which, streams, ht, hd):
    s = ph.sem
    x = [ph.sb(f"x{b}", [P, D]) for b in range(2)]
    h = [ph.sb(f"h{b}", [P, D]) for b in range(2)]
    junk = ph.sb("junk", [P, D])
    stat = ph.sb("stat", [P, 2, 4])
    eps = ph.sb("eps", [P, 1])
    scale = ph.sb("scale", [P, 2, D])
    shift = ph.sb("shift", [P, 2, D])
    ident = ph.sb("ident", [P, P])
    pt = [ph.ps(f"pt{b}", [P, KC, P]) for b in range(2)]
    sh_row, sc_row = (SH1, SC1) if which == 0 else (SH2, SC2)

    def sync(sp):
        sp.dma_start(ident[:, :], d.ident).then_inc(s("tables"), 16)
        for st in (LAT, CTX):
            sp.dma_start(scale[:, st, :], d.mods[layer, st, sc_row, :].partition_broadcast(P)).then_inc(s("tables"), 16)
            sp.dma_start(shift[:, st, :], d.mods[layer, st, sh_row, :].partition_broadcast(P)).then_inc(s("tables"), 16)
        for st, t0, pairs, before in streams:
            with sp.Fori(0, pairs) as i:
                for b in range(2):
                    row = (i * 2 + (t0 + b)) * P
                    if before:
                        sp.wait_ge(s(f"scaled{b}"), i + before)
                    sp.dma_start(x[b][:, :], d.xs[ds(row, P), :]).then_inc(s(f"x_loaded{b}"), 16)

    def pool(pl):
        if hd is None:
            return
        for st, t0, pairs, before in streams:
            with pl.Fori(0, pairs) as i:
                for b in range(2):
                    row = (i * 2 + (t0 + b)) * P
                    pl.wait_ge(s(f"h_ready{b}"), i + (before + 1))
                    pl.dma_start(hd[ds(row, P), :], h[b][:, :]).then_inc(s(f"h_stored{b}"), 16)
        for b in range(2):
            pl.wait_ge(s(f"h_stored{b}"), 16 * sum(p for _, _, p, _ in streams))

    def scalar(act):
        act.preload_act_table(ACT.Sqrt)
        for st, t0, pairs, before in streams:
            with act.Fori(0, pairs) as i:
                n = i + (before + 1)
                for b in range(2):
                    act.wait_ge(s(f"x_loaded{b}"), n * 16)
                    act.activation(junk[:, :], x[b][:, :], ACT.Square, accum_out=stat[:, b, 0:1])\
                        .then_inc(s(f"squares{b}"), 1)
                    act.wait_ge(s(f"squares{b}"), n)
                    act.wait_ge(s("eps_set"), 1)
                    act.activation(stat[:, b, 1:2], stat[:, b, 0:1], ACT.Sqrt, bias=eps[:, :], scale=1.0 / D)\
                        .then_inc(s(f"root{b}"), 1)
                    act.wait_ge(s(f"t_ready{b}"), n)
                    col = (i * 2 + (t0 + b)) * P
                    act.activation(ht.hi[:, :, ds(col, P)], pt[b][:, :, :], ACT.Copy)\
                        .then_inc(s(f"ht_hi{b}"), 1)

    def vector(dve):
        dve.memset(eps[:, :], EPS).then_inc(s("eps_set"), 1)
        dve.wait_ge(s("tables"), 80)
        for st, t0, pairs, before in streams:
            with dve.Fori(0, pairs) as i:
                n = i + (before + 1)
                for b in range(2):
                    dve.wait_ge(s(f"root{b}"), n)
                    dve.reciprocal(stat[:, b, 2:3], stat[:, b, 1:2]).then_inc(s(f"rstd{b}"), 1)
                    dve.wait_ge(s(f"rstd{b}"), n)
                    if before:
                        dve.wait_ge(s(f"t_ready{b}"), n - 1)
                    if hd is not None and before:
                        dve.wait_ge(s(f"h_stored{b}"), (n - 1) * 16)
                    dve.scalar_tensor_tensor(h[b][:, :], x[b][:, :], stat[:, b, 2:3], scale[:, st, :],
                                             ALU.mult, ALU.mult).then_inc(s(f"scaled{b}"), 1)
                    dve.wait_ge(s(f"scaled{b}"), n)
                    dve.tensor_tensor(h[b][:, :], h[b][:, :], shift[:, st, :], ALU.add).then_inc(s(f"h_ready{b}"), 1)
                    dve.wait_ge(s(f"ht_hi{b}"), n)
                    col = (i * 2 + (t0 + b)) * P
                    dve.tensor_tensor(ht.lo[:, :, ds(col, P)], pt[b][:, :, :],
                                      ht.hi[:, :, ds(col, P)].bitcast(F32), ALU.subtract)\
                        .then_inc(s(f"ht_lo{b}"), 1)

    def tensor(pe):
        pe.wait_ge(s("tables"), 80)
        for st, t0, pairs, before in streams:
            with pe.Fori(0, pairs) as i:
                n = i + (before + 1)
                for b in range(2):
                    pe.wait_ge(s(f"h_ready{b}"), n)
                    if before:
                        pe.wait_ge(s(f"ht_lo{b}"), n - 1)
                    for k in range(KC):
                        last = pe.transpose(pt[b][:, k, :], h[b][:, k * P:(k + 1) * P], ident[:, :])
                    last.then_inc(s(f"t_ready{b}"), 1)

    return sync, pool, scalar, vector, tensor


def normalise(nc, d, layer, which, streams, ht, hd=None):
    with ExitStack() as ctx:
        ph = Phase(nc, ctx, f"norm{layer}{which}")
        sync, pool, scalar, vector, tensor = norm_stage(ph, nc, d, layer, which, streams, ht, hd)
        with nc.Block() as block:
            block.sync(sync)
            block.gpsimd(pool)
            block.scalar(scalar)
            block.vector(vector)
            block.tensor(tensor)
        ph.close()


def conv_taps(nc, d, ht, vt, vecs):
    with ExitStack() as ctx:
        ph = Phase(nc, ctx, "taps")
        s = ph.sem
        raw = [ph.sb(f"raw{b}", [P, KC, 2, P]) for b in range(2)]
        w = [Split(nc, ctx, f"taps_w{b}", [P, KC, 2, P]) for b in range(2)]
        rows = ph.sb("rows", [VEC_ROWS, D])
        ident = ph.sb("ident", [P, P])
        vec = [ph.sb(f"vec{b}", [P, VEC_ROWS]) for b in range(2)]
        sg = [ph.sb(f"sg{g}", [P, N]) for g in range(3)]
        u = [ph.sb(f"u{b}", [P, CONV_W]) for b in range(2)]
        acc = [ph.sb(f"acc{b}", [P, CONV_OUT]) for b in range(2)]
        za = [ph.ps(f"za{g}", [P, N]) for g in range(3)]
        zg = [ph.ps(f"zg{g}", [P, N]) for g in range(3)]
        pv = ph.ps("pv", [P, KC, VEC_ROWS])
        pairs = KC // 2

        with nc.Block() as block:
            @block.sync
            def _(sp):
                sp.dma_start(ident[:, :], d.ident).then_inc(s("rows_loaded"), 16)
                for r0, src in ((0, d.dw_w), (V_DWB, d.dw_b), (V_LNG, d.ln_g), (V_LNB, d.ln_b)):
                    n = src.shape[0]
                    sp.dma_start(rows[r0:r0 + n, :], src).then_inc(s("rows_loaded"), 16)
                sp.dma_start(rows[V_BA:V_BG + 1, :], d.pw1_b.rearrange("o (h n) -> (o h) n", h=2))\
                    .then_inc(s("rows_loaded"), 16)

                def load(b, i):
                    for h in range(2):
                        src = d.pw1_w[:, ds((i * 2 + b) * P + h * D, P)].rearrange("(k p) n -> p k n", p=P)
                        sp.dma_start(raw[b][:, :, h, :], src).then_inc(s(f"w_loaded{b}"), 16)

                for b in range(2):
                    load(b, 0)
                with sp.Fori(1, pairs) as i:
                    for b in range(2):
                        sp.wait_ge(s(f"w_lo{b}"), i)
                        load(b, i)

            @block.gpsimd
            def _(pool):
                for b in range(2):
                    pool.memset(u[b][:, :], 0.0).then_inc(s("u_zero"), 1)

                def low(b, i, first):
                    pool.wait_ge(s(f"w_hi{b}"), i + 1)
                    pool.tensor_tensor(w[b].lo[:, :, :, :], raw[b][:, :, :, :], w[b].hi[:, :, :, :].bitcast(F32),
                                       ALU.subtract).then_inc(s(f"w_lo{b}"), 1)

                for b in range(2):
                    low(b, 0, True)
                with pool.Fori(1, pairs) as i:
                    for b in range(2):
                        low(b, i, False)

            @block.tensor
            def _(pe):
                pe.wait_ge(s("rows_loaded"), 96)
                for k in range(KC):
                    last = pe.transpose(pv[:, k, :], rows[:, k * P:(k + 1) * P], ident[0:VEC_ROWS, 0:VEC_ROWS])
                last.then_inc(s("pv_ready"), 1)

                def chunk(b, i, first):
                    pe.wait_ge(s(f"w_lo{b}"), i + 1)
                    for g, (t0, n, _) in enumerate(CONV_GROUPS):
                        if not (first and b == 0):
                            pe.wait_ge(s(f"u_ready{g}{1 - b}"), i + b)
                        for h, z in ((1, zg[g]), (0, za[g])):
                            for k in range(KC):
                                last = product3(pe, z[:, 0:n], w[b].hi[:, k, h, :], w[b].lo[:, k, h, :],
                                                ht.hi[:, k, t0:t0 + n], ht.lo[:, k, t0:t0 + n], k == 0, k == KC - 1)
                        last.then_inc(s(f"z_ready{g}{b}"), 1)

                for b in range(2):
                    chunk(b, 0, True)
                with pe.Fori(1, pairs) as i:
                    for b in range(2):
                        chunk(b, i, False)

            @block.scalar
            def _(act):
                act.preload_act_table(ACT.Sigmoid)

                def high(b, i, first):
                    act.wait_ge(s(f"w_loaded{b}"), i * 32 + 32)
                    if not first:
                        act.wait_ge(s(f"z_ready2{b}"), i)
                    act.activation(w[b].hi[:, :, :, :], raw[b][:, :, :, :], ACT.Copy).then_inc(s(f"w_hi{b}"), 1)

                def chunk(b, i, first):
                    act.wait_ge(s(f"vec_ready{b}"), i + 1)
                    for g, (t0, n, _) in enumerate(CONV_GROUPS):
                        act.wait_ge(s(f"z_ready{g}{b}"), i + 1)
                        if not (first and b == 0):
                            act.wait_ge(s(f"u_ready{g}{1 - b}"), i + b)
                        act.activation(sg[g][:, 0:n], zg[g][:, 0:n], ACT.Sigmoid, bias=vec[b][:, V_BG:V_BG + 1])\
                            .then_inc(s(f"sig_ready{g}{b}"), 1)

                for b in range(2):
                    high(b, 0, True)
                for b in range(2):
                    chunk(b, 0, True)
                with act.Fori(1, pairs) as i:
                    for b in range(2):
                        high(b, i, False)
                        chunk(b, i, False)

            @block.vector
            def _(dve):
                dve.wait_ge(s("pv_ready"), 1)
                dve.tensor_copy(vecs[:, :, :], pv[:, :, :]).then_inc(s("vecs_ready"), 1)
                dve.wait_ge(s("vecs_ready"), 1)
                dve.wait_ge(s("u_zero"), 2)

                def chunk(b, i):
                    n = i + 1
                    dve.tensor_copy(vec[b][:, :], vecs[:, ds(i * 2 + b, 1), :].rearrange("p o v -> p (o v)"))\
                        .then_inc(s(f"vec_ready{b}"), 1)
                    dve.wait_ge(s(f"vec_ready{b}"), n)
                    for g, (t0, m, c0) in enumerate(CONV_GROUPS):
                        dve.wait_ge(s(f"sig_ready{g}{b}"), n)
                        dve.scalar_tensor_tensor(u[b][:, c0:c0 + m], za[g][:, 0:m], vec[b][:, V_BA:V_BA + 1],
                                                 sg[g][:, 0:m], ALU.add, ALU.mult).then_inc(s(f"u_ready{g}{b}"), 1)
                        dve.wait_ge(s(f"u_ready{g}{b}"), n)
                    dve.tensor_scalar(acc[0][:, :], u[b][:, 0:CONV_OUT], vec[b][:, 0:1], vec[b][:, V_DWB:V_DWB + 1],
                                      ALU.mult, ALU.add).then_inc(s(f"tap0{b}"), 1)
                    for k in range(1, TAPS):
                        dve.wait_ge(s(f"tap{(k - 1) % 2}{b}"), i * ((TAPS + 1 - (k - 1) % 2) // 2) + (k + 1) // 2)
                        out = acc[k % 2][:, :] if k < TAPS - 1 else \
                            vt[:, ds(i * 2 + b, 1), :].rearrange("p o n -> p (o n)")
                        dve.scalar_tensor_tensor(out, u[b][:, k:k + CONV_OUT], vec[b][:, k:k + 1],
                                                 acc[(k - 1) % 2][:, :], ALU.mult, ALU.add)\
                            .then_inc(s(f"tap{k % 2}{b}"), 1)

                for b in range(2):
                    chunk(b, 0)
                with dve.Fori(1, pairs) as i:
                    for b in range(2):
                        chunk(b, i)
                for b in range(2):
                    dve.wait_ge(s(f"tap0{b}"), pairs * 16)
        ph.close()


def conv_out(nc, d, vt, vecs):
    with ExitStack() as ctx:
        ph = Phase(nc, ctx, "pw2")
        s = ph.sem
        raw = ph.sb("raw", [P, 2, D])
        w = Split(nc, ctx, "pw2_w", [P, KC, D])
        mean_w = ph.sb("mean_w", [P, P])
        bias = ph.sb("bias", [P, D])
        gate = ph.sb("gate", [P, 2, D])
        eps = ph.sb("eps", [P, 1])
        dev = [ph.sb(f"dev{b}", [P, KC, P]) for b in range(2)]
        sq = [ph.sb(f"sq{b}", [P, KC, P]) for b in range(2)]
        root = ph.sb("root", [P, 2, P])
        rstd = ph.sb("rstd", [P, 2, P])
        act_t = [Split(nc, ctx, f"pw2_act{b}", [P, KC, P]) for b in range(2)]
        x = [ph.sb(f"x{b}", [P, D]) for b in range(2)]
        y = [ph.sb(f"y{b}", [P, D]) for b in range(2)]
        mean = [ph.ps(f"mean{b}", [P, N]) for b in range(2)]
        var = [ph.ps(f"var{b}", [P, N]) for b in range(2)]
        py = [ph.ps(f"py{b}", [P, D]) for b in range(2)]

        def vcol(i, b, st):
            return (i * 2 + b) * P + (0 if st == CTX else GAP - PAD)

        with nc.Block() as block:
            @block.sync
            def _(sp):
                sp.dma_start(mean_w[:, :], d.mean_w).then_inc(s("tables"), 16)
                sp.dma_start(bias[:, :], d.pw2_b[0, :].partition_broadcast(P)).then_inc(s("tables"), 16)
                for st in (LAT, CTX):
                    sp.dma_start(gate[:, st, :], d.mods[0, st, G1, :].partition_broadcast(P)).then_inc(s("tables"), 16)
                for k in range(KC):
                    if k >= 2:
                        sp.wait_ge(s("w_lo"), k - 1)
                    sp.dma_start(raw[:, k % 2, :], d.pw2_w[k * P:(k + 1) * P, :]).then_inc(s(f"w_loaded{k % 2}"), 16)
                for st, t0, pairs, before in STREAMS:
                    with sp.Fori(0, pairs) as i:
                        for b in range(2):
                            if before:
                                sp.wait_ge(s(f"stored{b}"), (i + before) * 16)
                            sp.dma_start(x[b][:, :], d.xs[ds((i * 2 + (t0 + b)) * P, P), :])\
                                .then_inc(s(f"x_loaded{b}"), 16)

            @block.gpsimd
            def _(pool):
                for st, t0, pairs, before in STREAMS:
                    with pool.Fori(0, pairs) as i:
                        for b in range(2):
                            pool.wait_ge(s(f"x_ready{b}"), i + (before + 1))
                            pool.dma_start(d.xs[ds((i * 2 + (t0 + b)) * P, P), :], x[b][:, :])\
                                .then_inc(s(f"stored{b}"), 16)
                for b in range(2):
                    pool.wait_ge(s(f"stored{b}"), 16 * (TILES // 2))

            @block.tensor
            def _(pe):
                pe.wait_ge(s("tables"), 64)
                pe.wait_ge(s("w_lo"), KC)
                for st, t0, pairs, before in STREAMS:
                    with pe.Fori(0, pairs) as i:
                        n = i + (before + 1)
                        for b in range(2):
                            if before:
                                pe.wait_ge(s(f"dev_ready{b}"), n - 1)
                            for k in range(KC):
                                last = pe.matmul(mean[b][:, 0:P], mean_w[:, :], vt[:, k, ds(vcol(i, b, st), P)],
                                                 start=k == 0, stop=k == KC - 1)
                            last.then_inc(s(f"mean_ready{b}"), 1)
                        for b in range(2):
                            pe.wait_ge(s(f"sq_ready{b}"), n)
                            if before:
                                pe.wait_ge(s(f"root_ready{b}"), n - 1)
                            for k in range(KC):
                                last = pe.matmul(var[b][:, 0:P], mean_w[:, :], sq[b][:, k, :],
                                                 start=k == 0, stop=k == KC - 1)
                            last.then_inc(s(f"var_ready{b}"), 1)
                        for b in range(2):
                            pe.wait_ge(s(f"act_lo{b}"), n)
                            if before:
                                pe.wait_ge(s(f"biased{b}"), n - 1)
                            for h in range(2):
                                for k in range(KC):
                                    cols = slice(h * N, (h + 1) * N)
                                    last = product3(pe, py[b][:, cols], act_t[b].hi[:, k, :], act_t[b].lo[:, k, :],
                                                    w.hi[:, k, cols], w.lo[:, k, cols], k == 0, k == KC - 1)
                            last.then_inc(s(f"y_ready{b}"), 1)

            @block.scalar
            def _(act):
                for k in range(KC):
                    act.wait_ge(s(f"w_loaded{k % 2}"), 16 * (k // 2 + 1))
                    act.activation(w.hi[:, k, :], raw[:, k % 2, :], ACT.Copy).then_inc(s("w_hi"), 1)
                act.wait_ge(s("eps_set"), 1)
                for st, t0, pairs, before in STREAMS:
                    with act.Fori(0, pairs) as i:
                        n = i + (before + 1)
                        for b in range(2):
                            act.wait_ge(s(f"dev_ready{b}"), n)
                            if before:
                                act.wait_ge(s(f"act_lo{b}"), n - 1)
                            act.activation(sq[b][:, :, :], dev[b][:, :, :], ACT.Square).then_inc(s(f"sq_ready{b}"), 1)
                        for b in range(2):
                            act.wait_ge(s(f"var_ready{b}"), n)
                            if before:
                                act.wait_ge(s(f"rstd_ready{b}"), n - 1)
                            act.activation(root[:, b, :], var[b][:, 0:P], ACT.Sqrt, bias=eps[:, :])\
                                .then_inc(s(f"root_ready{b}"), 1)
                        for b in range(2):
                            act.wait_ge(s(f"scaled{b}"), n)
                            if before:
                                act.wait_ge(s(f"y_ready{b}"), n - 1)
                                act.wait_ge(s(f"act_lo{b}"), n - 1)
                            for k in range(KC):
                                last = act.activation(sq[b][:, k, :], dev[b][:, k, :], ACT.Silu,
                                                      scale=vecs[:, k, V_LNG:V_LNG + 1],
                                                      bias=vecs[:, k, V_LNB:V_LNB + 1])
                            last.then_inc(s(f"act_ready{b}"), 1)
                        for b in range(2):
                            act.wait_ge(s(f"act_ready{b}"), n)
                            act.activation(act_t[b].hi[:, :, :], sq[b][:, :, :], ACT.Copy).then_inc(s(f"act_hi{b}"), 1)

            @block.vector
            def _(dve):
                dve.memset(eps[:, :], EPS).then_inc(s("eps_set"), 1)
                for k in range(KC):
                    dve.wait_ge(s("w_hi"), k + 1)
                    dve.tensor_tensor(w.lo[:, k, :], raw[:, k % 2, :], w.hi[:, k, :].bitcast(F32), ALU.subtract)\
                        .then_inc(s("w_lo"), 1)
                dve.wait_ge(s("tables"), 64)
                for st, t0, pairs, before in STREAMS:
                    with dve.Fori(0, pairs) as i:
                        n = i + (before + 1)
                        for b in range(2):
                            dve.wait_ge(s(f"mean_ready{b}"), n)
                            if before:
                                dve.wait_ge(s(f"act_ready{b}"), n - 1)
                            dve.tensor_tensor(dev[b][:, :, :], vt[:, :, ds(vcol(i, b, st), P)],
                                              mean[b][:, 0:P].unsqueeze(1).to_broadcast([P, KC, P]), ALU.subtract)\
                                .then_inc(s(f"dev_ready{b}"), 1)
                        for b in range(2):
                            dve.wait_ge(s(f"root_ready{b}"), n)
                            dve.reciprocal(rstd[:, b, :], root[:, b, :]).then_inc(s(f"rstd_ready{b}"), 1)
                            dve.wait_ge(s(f"rstd_ready{b}"), n)
                            dve.tensor_tensor(dev[b][:, :, :], dev[b][:, :, :],
                                              rstd[:, b:b + 1, :].to_broadcast([P, KC, P]), ALU.mult)\
                                .then_inc(s(f"scaled{b}"), 1)
                        for b in range(2):
                            dve.wait_ge(s(f"act_hi{b}"), n)
                            dve.tensor_tensor(act_t[b].lo[:, :, :], sq[b][:, :, :], act_t[b].hi[:, :, :].bitcast(F32),
                                              ALU.subtract).then_inc(s(f"act_lo{b}"), 1)
                        for b in range(2):
                            dve.wait_ge(s(f"y_ready{b}"), n)
                            dve.tensor_tensor(y[b][:, :], py[b][:, :], bias[:, :], ALU.add)\
                                .then_inc(s(f"biased{b}"), 1)
                            dve.wait_ge(s(f"biased{b}"), n)
                            dve.tensor_tensor(y[b][:, :], y[b][:, :], gate[:, st, :], ALU.mult)\
                                .then_inc(s(f"gated{b}"), 1)
                            dve.wait_ge(s(f"gated{b}"), n)
                            dve.wait_ge(s(f"x_loaded{b}"), n * 16)
                            dve.tensor_tensor(x[b][:, :], x[b][:, :], y[b][:, :], ALU.add)\
                                .then_inc(s(f"x_ready{b}"), 1)
        ph.close()


def route(nc, d, layer, streams, ht, plan):
    t0 = streams[0][1]
    nt = TILES - t0
    nb = plan.blocks
    width = GROUPS + EXPERTS
    with ExitStack() as ctx:
        ph = Phase(nc, ctx, f"route{layer}")
        s = ph.sem
        raw = ph.sb("raw", [P, KC, width])
        w = Split(nc, ctx, f"route{layer}_w", [P, KC, width])
        bias = ph.sb("bias", [width, 1])
        ident = ph.sb("ident", [P, P])
        before = ph.sb("before", [P, P])
        ones = ph.sb("ones", [P, P])
        iota = ph.sb("iota", [P, P])
        token = ph.sb("token", [P, TILES])
        lt = ph.sb("lt", [width, TOK])
        lg = ph.sb("lg", [P, nt, width])
        gm = ph.sb("gm", [P, nt])
        ga = ph.sb("ga", [P, nt, GROUPS])
        gsel = ph.sb("gsel", [P, nt, GROUPS])
        gw = ph.sb("gw", [P, nt])
        inner = [ph.sb(f"inner{j}", [P, nt, EXPERTS]) for j in range(2)]
        cand = ph.sb("cand", [P, nt, EXPERTS])
        least = ph.sb("least", [P, nt])
        top = ph.sb("top", [P, 2, nt])
        hot = ph.sb("hot", [P, 2, nt, EXPERTS])
        both = ph.sb("both", [P, nt, EXPERTS])
        sofar = ph.sb("sofar", [P, nt + 1, EXPERTS])
        rank = ph.sb("rank", [P, nt, EXPERTS])
        picked = ph.sb("picked", [P, 2, nt, EXPERTS])
        mine = ph.sb("mine", [P, 2, nt])
        first = ph.sb("first", [P, 2, nt])
        over = ph.sb("over", [P, 2, nt])
        steps = ph.sb("steps", [P, nt])
        more = ph.sb("more", [P, 2 * nt * nt + EXPERTS * nt])
        need = ph.sb("need", [P, EXPERTS])
        ends = [ph.sb(f"ends{j}", [P, EXPERTS]) for j in range(2)]
        passed = ph.sb("passed", [1, nb + 1, EXPERTS])
        blk = ph.sb("blk", [1, nb + 1])
        in_slot = ph.sb("in_slot", [P, 2 * nt, P])
        in_blk = ph.sb("in_blk", [P, 2 * nt, nb + 1])
        pl = [ph.ps(f"pl{g}", [P, N]) for g in range(3)]
        pt = ph.ps("pt", [P, nt, width])
        pr = ph.ps("pr", [P, nt * EXPERTS])
        pa = ph.ps("pa", [P, nt * EXPERTS])
        pi = ph.ps("pi", [P, nb + 1])
        groups = [(a, min(N, TOK - a)) for a in range(t0 * P, TOK, N)]

        with nc.Block() as block:
            @block.sync
            def _(sp):
                for dst, src in ((raw[:, :, 0:GROUPS], d.wg[layer].rearrange("(k p) n -> p k n", p=P)),
                                 (raw[:, :, GROUPS:width], d.wr[layer].rearrange("(k p) n -> p k n", p=P)),
                                 (bias[0:GROUPS, :], d.bg[layer, :].unsqueeze(1)),
                                 (bias[GROUPS:width, :], d.br[layer, :].unsqueeze(1)),
                                 (ident[:, :], d.ident), (before[:, :], d.before), (ones[:, :], d.ones),
                                 (iota[:, :], d.iota), (token[:, :], d.token)):
                    sp.dma_start(dst, src).then_inc(s("loaded"), 16)

            @block.tensor
            def _(pe):
                pe.wait_ge(s("loaded"), 144)
                pe.wait_ge(s("w_lo"), 1)
                for g, (a, n) in enumerate(groups):
                    for k in range(KC):
                        last = product3(pe, pl[g][0:width, 0:n], w.hi[:, k, :], w.lo[:, k, :],
                                        ht.hi[:, k, a:a + n], ht.lo[:, k, a:a + n], k == 0, k == KC - 1)
                    last.then_inc(s("logits"), 1)
                pe.wait_ge(s("biased"), len(groups))
                for t in range(nt):
                    last = pe.transpose(pt[:, t, :], lt[:, (t0 + t) * P:(t0 + t + 1) * P], ident[0:width, 0:width])
                last.then_inc(s("turned"), 1)
                pe.wait_ge(s("chosen"), 1)
                pe.matmul(pr[:, :], before[:, :], both[:, :, :].rearrange("p t e -> p (t e)"), start=True, stop=True)
                pe.matmul(pa[:, :], ones[:, :], both[:, :, :].rearrange("p t e -> p (t e)"), start=True, stop=True)\
                    .then_inc(s("counted"), 1)
                pe.wait_ge(s("hot_slots"), 4 * nt)
                for j in range(2 * nt):
                    last = pe.matmul(pi[:, :], in_slot[:, j, :], in_blk[:, j, :], start=j == 0, stop=j == 2 * nt - 1)
                last.then_inc(s("slots_done"), 1)

            @block.scalar
            def _(act):
                act.preload_act_table(ACT.Exp)
                act.wait_ge(s("loaded"), 144)
                act.activation(w.hi[:, :, :], raw[:, :, :], ACT.Copy).then_inc(s("w_hi"), 1)
                for g, (a, n) in enumerate(groups):
                    act.wait_ge(s("logits"), g + 1)
                    act.activation(lt[:, a:a + n], pl[g][0:width, 0:n], ACT.Identity, bias=bias[:, :])\
                        .then_inc(s("biased"), 1)
                act.wait_ge(s("group_shifted"), 1)
                act.activation(ga[:, :, :], ga[:, :, :], ACT.Exp).then_inc(s("group_exp"), 1)
                act.wait_ge(s("top_gap"), 1)
                act.activation(top[:, 1, :], top[:, 1, :], ACT.Exp).then_inc(s("top_exp"), 1)

            @block.vector
            def _(dve):
                link = chain(ph, dve, "step")

                def over_rows(ap, n):
                    return ap.unsqueeze(2).to_broadcast([P, nt, n])

                def along(n):
                    return iota[:, 0:n].unsqueeze(1).to_broadcast([P, nt, n])

                def first_max(values, n, biggest, hot_out):
                    link(dve.tensor_reduce(biggest, values, AX.X, ALU.max))
                    link(dve.tensor_tensor(cand[:, :, 0:n], values, over_rows(biggest, n), ALU.is_equal))
                    link(dve.scalar_tensor_tensor(cand[:, :, 0:n], cand[:, :, 0:n], -100.0, along(n), ALU.mult, ALU.add))
                    link(dve.tensor_reduce(least[:, :], cand[:, :, 0:n], AX.X, ALU.min))
                    link(dve.tensor_tensor(hot_out, cand[:, :, 0:n], over_rows(least[:, :], n), ALU.is_equal))

                dve.wait_ge(s("w_hi"), 1)
                dve.tensor_tensor(w.lo[:, :, :], raw[:, :, :], w.hi[:, :, :].bitcast(F32), ALU.subtract)\
                    .then_inc(s("w_lo"), 1)
                dve.wait_ge(s("turned"), 1)
                link(dve.tensor_copy(lg[:, :, :], pt[:, :, :]))
                first_max(lg[:, :, 0:GROUPS], GROUPS, gm[:, :], gsel[:, :, :])
                dve.tensor_tensor(ga[:, :, :], lg[:, :, 0:GROUPS], over_rows(gm[:, :], GROUPS), ALU.subtract)\
                    .then_inc(s("group_shifted"), 1)
                def by_group(ap):
                    return ap.rearrange("p t (g e) -> p t g e", g=GROUPS)
                sel = gsel[:, :, :].unsqueeze(3).to_broadcast([P, nt, GROUPS, PER_GROUP])
                link(dve.tensor_tensor(by_group(inner[0][:, :, :]), by_group(lg[:, :, GROUPS:width]), sel, ALU.mult))
                link(dve.tensor_scalar(gsel[:, :, :], gsel[:, :, :], 1.0, 1e30, ALU.subtract, ALU.mult))
                link(dve.tensor_tensor(by_group(inner[0][:, :, :]), by_group(inner[0][:, :, :]), sel, ALU.add))
                first_max(inner[0][:, :, :], EXPERTS, top[:, 0, :], hot[:, 0, :, :])
                link(dve.scalar_tensor_tensor(inner[1][:, :, :], hot[:, 0, :, :], -2e30, inner[0][:, :, :],
                                              ALU.mult, ALU.add))
                first_max(inner[1][:, :, :], EXPERTS, top[:, 1, :], hot[:, 1, :, :])
                dve.tensor_tensor(both[:, :, :], hot[:, 0, :, :], hot[:, 1, :, :], ALU.add).then_inc(s("chosen"), 1)
                dve.tensor_tensor(top[:, 1, :], top[:, 1, :], top[:, 0, :], ALU.subtract).then_inc(s("top_gap"), 1)
                dve.wait_ge(s("group_exp"), 1)
                link(dve.tensor_reduce(gw[:, :], ga[:, :, :], AX.X, ALU.add))
                link(dve.reciprocal(gw[:, :], gw[:, :]))
                dve.wait_ge(s("top_exp"), 1)
                link(dve.tensor_scalar(top[:, 0, :], top[:, 1, :], 1.0, None, ALU.add))
                link(dve.reciprocal(top[:, 0, :], top[:, 0, :]))
                link(dve.tensor_tensor(plan.weight[:, 0, :], top[:, 0, :], gw[:, :], ALU.mult))
                link(dve.tensor_tensor(plan.weight[:, 1, :], plan.weight[:, 0, :], top[:, 1, :], ALU.mult))
                dve.wait_ge(s("counted"), 1)
                link(dve.memset(sofar[:, 0, :], 0.0))
                for t in range(nt):
                    link(dve.tensor_tensor(sofar[:, t + 1, :], sofar[:, t, :], pa[:, t * EXPERTS:(t + 1) * EXPERTS],
                                           ALU.add))
                link(dve.tensor_tensor(rank[:, :, :].rearrange("p t e -> p (t e)"), pr[:, :],
                                       sofar[:, 0:nt, :].rearrange("p t e -> p (t e)"), ALU.add))
                link(dve.tensor_scalar(steps[:, :], iota[:, 0:nt], float(BLK), None, ALU.mult))
                taken = more[:, 2 * nt * nt:].rearrange("p (e t) -> p e t", t=nt)
                link(dve.tensor_tensor(taken, sofar[:, nt, :].unsqueeze(2).to_broadcast([P, EXPERTS, nt]),
                                       steps[:, :].unsqueeze(1).to_broadcast([P, EXPERTS, nt]), ALU.is_gt))
                link(dve.tensor_reduce(need[:, :], taken, AX.X, ALU.add))
                link(dve.tensor_copy(ends[0][:, :], need[:, :]))
                for j in range(5):
                    a, b, step = ends[j % 2], ends[(j + 1) % 2], 1 << j
                    link(dve.tensor_copy(b[:, 0:step], a[:, 0:step]))
                    link(dve.tensor_tensor(b[:, step:], a[:, step:], a[:, 0:EXPERTS - step], ALU.add))
                end = ends[1]
                link(dve.tensor_tensor(need[:, :], end[:, :], need[:, :], ALU.subtract))
                for j in range(2):
                    link(dve.tensor_tensor(picked[:, j, :, :], hot[:, j, :, :], rank[:, :, :], ALU.mult))
                link(dve.tensor_reduce(mine[:, :, :], picked[:, :, :, :], AX.X, ALU.add))
                for j in range(2):
                    link(dve.tensor_tensor(picked[:, j, :, :], hot[:, j, :, :],
                                           need[:, :].unsqueeze(1).to_broadcast([P, nt, EXPERTS]), ALU.mult))
                link(dve.tensor_reduce(first[:, :, :], picked[:, :, :, :], AX.X, ALU.add))
                for j in range(2):
                    full = more[:, j * nt * nt:j * nt * nt + nt * (nt - 1)].rearrange("p (t k) -> p t k", k=nt - 1)
                    link(dve.tensor_tensor(full, over_rows(mine[:, j, :], nt - 1),
                                           steps[:, 1:nt].unsqueeze(1).to_broadcast([P, nt, nt - 1]), ALU.is_ge))
                    link(dve.tensor_reduce(over[:, j, :], full, AX.X, ALU.add))
                link(dve.tensor_tensor(first[:, :, :], first[:, :, :], over[:, :, :], ALU.add))
                link(dve.scalar_tensor_tensor(mine[:, :, :], over[:, :, :], -float(BLK), mine[:, :, :],
                                              ALU.mult, ALU.add))
                link(dve.scalar_tensor_tensor(plan.slot[:, :, :], first[:, :, :], float(BLK), mine[:, :, :],
                                              ALU.mult, ALU.add))
                for j in range(2):
                    for t in range(nt):
                        q = j * nt + t
                        dve.tensor_scalar(in_slot[:, q, :], iota[:, :], mine[:, j, t:t + 1], None, ALU.is_equal)\
                            .then_inc(s("hot_slots"), 1)
                        dve.tensor_scalar(in_blk[:, q, :], iota[:, 0:nb + 1], first[:, j, t:t + 1],
                                          token[:, t0 + t:t0 + t + 1], ALU.is_equal, ALU.mult)\
                            .then_inc(s("hot_slots"), 1)
                link(dve.tensor_tensor(passed[:, :, :], iota[0:1, 0:nb + 1].unsqueeze(2).to_broadcast([1, nb + 1, EXPERTS]),
                                       end[0:1, :].unsqueeze(1).to_broadcast([1, nb + 1, EXPERTS]), ALU.is_ge))
                link(dve.tensor_reduce(blk[:, :], passed[:, :, :], AX.X, ALU.add))
                link(dve.tensor_scalar(blk[:, :], blk[:, :], float(EXPERTS - 1), None, ALU.min))
                link(dve.tensor_copy(blk[:, nb:nb + 1], end[0:1, EXPERTS - 1:EXPERTS]))
                link(dve.tensor_copy(plan.block[:, :], blk[:, :]))
                dve.wait_ge(s("slots_done"), 1)
                link(dve.tensor_copy(plan.token[:, :], pi[:, :]))
        ph.close()


class Plan:
    def __init__(self, nc, ctx, layer, tiles):
        self.blocks = 2 * tiles + EXPERTS
        def sb(name, shape, dt):
            return ctx.enter_context(nc.sbuf_tensor(f"plan{layer}_{name}", shape, dt))
        self.slot = sb("slot", [P, 2, tiles], I32)
        self.weight = sb("weight", [P, 2, tiles], F32)
        self.token = sb("token", [P, self.blocks + 1], I32)
        self.block = sb("block", [1, self.blocks + 1], I32)


def experts(nc, d, layer, plan):
    FC = FF // P
    nb = plan.blocks
    with ExitStack() as ctx:
        ph = Phase(nc, ctx, f"moe{layer}")
        s = ph.sem
        shapes = {"w1": [P, KC, FF], "w3": [P, KC, FF], "w2": [P, FC, D]}
        raw = {m: ph.sb(f"{m}_raw", sh) for m, sh in shapes.items()}
        hi = {m: ph.sb(f"{m}_hi", sh, F32R) for m, sh in shapes.items()}
        lo = {m: ph.sb(f"{m}_lo", sh, F32R) for m, sh in shapes.items()}
        half = {m: sh[1] // 2 for m, sh in shapes.items()}
        dram = {"w1": d.w1, "w3": d.w3, "w2": d.w2}
        ident = ph.sb("ident", [P, P])
        idx = ph.sb("idx", [P, 1], I32)
        xg = ph.sb("xg", [P, D])
        xt_hi = ph.sb("xt_hi", [P, KC, P], F32R)
        xt_lo = ph.sb("xt_lo", [P, KC, P], F32R)
        sil = ph.sb("sil", [P, FF])
        a = ph.sb("a", [P, FF])
        at_hi = ph.sb("at_hi", [P, FC, P], F32R)
        at_lo = ph.sb("at_lo", [P, FC, P], F32R)
        y = ph.sb("y", [P, D])
        zero = ph.sb("zero", [P, D])
        pxt = ph.ps("pxt", [P, KC, P])
        pg = ph.ps("pg", [P, FF])
        pu = ph.ps("pu", [P, FF])
        pat = ph.ps("pat", [P, FC, P])
        py = ph.ps("py", [P, D])

        def blocks(eng, body, last=None, otherwise=None):
            count = eng.value_load(plan.block[0:1, nb:nb + 1], min_val=1, max_val=nb)
            body(0, True)
            with eng.Fori(1, nb) as k:
                with eng.If(k < count):
                    body(k, False)
                if otherwise:
                    with eng.If(k >= count):
                        otherwise(k)
            if last:
                last(count)

        with nc.Block() as block:
            @block.sync
            def _(sp):
                sp.dma_start(ident[:, :], d.ident).then_inc(s("ident"), 16)

                def load(k, first):
                    e = sp.value_load(plan.block[0:1, ds(k, 1)], min_val=0, max_val=EXPERTS - 1)
                    for m in ("w1", "w3", "w2"):
                        for h in range(2):
                            cut = slice(h * half[m], (h + 1) * half[m])
                            if not first:
                                sp.wait_ge(s(f"{m}_lo{h}"), k)
                            sp.dma_start(raw[m][:, cut, :],
                                         dram[m][layer, ds(e, 1), h * half[m] * P:(h + 1) * half[m] * P, :]
                                         .rearrange("o (k p) n -> p (o k) n", p=P)).then_inc(s(f"{m}_raw{h}"), 16)

                def unused(k):
                    sp.dma_start(d.yd[ds(k * BLK, BLK), :], zero[:, :]).then_inc(s("covered"), 16)

                sp.wait_ge(s("zero_set"), 1)
                blocks(sp, load, None, unused)

            @block.gpsimd
            def _(pool):
                def gather(k, n):
                    pool.tensor_copy(idx[:, :], plan.token[:, ds(k, 1)]).then_inc(s("idx_ready"), 1)
                    pool.wait_ge(s("idx_ready"), n + 1)
                    pool.sem_inc(s("gathers"), 1)
                    pool.indirect_dma_start(xg[:, :], None, d.hd[:, :], bass.IndirectOffsetOnAxis(idx[:, :], 0))\
                        .then_inc(s("gathered"), 16)

                def ahead(k, first):
                    pool.wait_ge(s("xt_turned"), k + 1)
                    gather(k + 1, k + 1)

                def finish(count):
                    pool.wait_ge(s("gathered"), count * 16 + 16)
                    pool.wait_ge(s("y_stored"), count * 16 + 16)
                    pool.wait_ge(s("covered"), nb * 16)

                pool.memset(zero[:, :], 0.0).then_inc(s("zero_set"), 1)
                gather(0, 0)
                blocks(pool, ahead, finish)

            @block.tensor
            def _(pe):
                def turn_x(n):
                    pe.wait_ge(s("gathered"), n * 16)
                    for k in range(KC):
                        last = pe.transpose(pxt[:, k, :], xg[:, k * P:(k + 1) * P], ident[:, :])
                    last.then_inc(s("xt_turned"), 1)

                def body(b, first):
                    n = b + 1
                    pe.wait_ge(s("xt_hi"), n)
                    pe.wait_ge(s("xt_lo"), n)
                    for w, out, used in (("w1", pg, "sil_ready"), ("w3", pu, "a_ready")):
                        if not first:
                            pe.wait_ge(s(used), b)
                        for h in range(2):
                            pe.wait_ge(s(f"{w}_lo{h}"), n)
                            for k in range(h * half[w], (h + 1) * half[w]):
                                last = product3(pe, out[:, :], xt_hi[:, k, :], xt_lo[:, k, :], hi[w][:, k, :],
                                                lo[w][:, k, :], k == 0, k == KC - 1)
                        last.then_inc(s(f"{w}_done"), 1)
                    turn_x(n + 1)
                    pe.wait_ge(s("a_ready"), n)
                    if not first:
                        pe.wait_ge(s("at_lo"), b)
                    for k in range(FC):
                        last = pe.transpose(pat[:, k, :], a[:, k * P:(k + 1) * P], ident[:, :])
                    last.then_inc(s("at_turned"), 1)
                    pe.wait_ge(s("at_lo"), n)
                    if not first:
                        pe.wait_ge(s("y_out"), b)
                    for h in range(2):
                        pe.wait_ge(s(f"w2_lo{h}"), n)
                        for c in range(2):
                            for k in range(h * half["w2"], (h + 1) * half["w2"]):
                                cols = slice(c * N, (c + 1) * N)
                                last = product3(pe, py[:, cols], at_hi[:, k, :], at_lo[:, k, :],
                                                hi["w2"][:, k, cols], lo["w2"][:, k, cols], k == 0, k == FC - 1)
                    last.then_inc(s("w2_done"), 1)

                pe.wait_ge(s("ident"), 16)
                turn_x(1)
                blocks(pe, body)

            @block.scalar
            def _(act):
                act.preload_act_table(ACT.Silu)

                def high(m, b, first):
                    for h in range(2):
                        cut = slice(h * half[m], (h + 1) * half[m])
                        act.wait_ge(s(f"{m}_raw{h}"), (b + 1) * 16)
                        if h == 0 and not first:
                            act.wait_ge(s(f"{m}_done"), b)
                        act.activation(hi[m][:, cut, :], raw[m][:, cut, :], ACT.Copy).then_inc(s(f"{m}_hi{h}"), 1)

                def put_out(n):
                    act.wait_ge(s("w2_done"), n)
                    act.wait_ge(s("y_stored"), n * 16)
                    act.activation(y[:, :], py[:, :], ACT.Copy).then_inc(s("y_out"), 1)
                    act.wait_ge(s("y_out"), n)
                    act.dma_start(d.yd[ds((n - 1) * BLK, BLK), :], y[:, :]).then_inc(s("y_stored"), 16)

                def x_high(n):
                    act.wait_ge(s("xt_turned"), n)
                    act.activation(xt_hi[:, :, :], pxt[:, :, :], ACT.Copy).then_inc(s("xt_hi"), 1)

                def body(b, first):
                    n = b + 1
                    high("w1", b, first)
                    high("w3", b, first)
                    if not first:
                        put_out(b)
                    high("w2", b, first)
                    act.wait_ge(s("w1_done"), n)
                    if not first:
                        act.wait_ge(s("a_ready"), b)
                    act.activation(sil[:, :], pg[:, :], ACT.Silu).then_inc(s("sil_ready"), 1)
                    act.wait_ge(s("w3_done"), n)
                    x_high(n + 1)
                    act.wait_ge(s("at_turned"), n)
                    if not first:
                        act.wait_ge(s("w2_done"), b)
                    act.activation(at_hi[:, :, :], pat[:, :, :], ACT.Copy).then_inc(s("at_hi"), 1)

                x_high(1)

                blocks(act, body, put_out)

            @block.vector
            def _(dve):
                def low(m, b, first):
                    for h in range(2):
                        cut = slice(h * half[m], (h + 1) * half[m])
                        dve.wait_ge(s(f"{m}_hi{h}"), b + 1)
                        dve.tensor_tensor(lo[m][:, cut, :], raw[m][:, cut, :], hi[m][:, cut, :].bitcast(F32),
                                          ALU.subtract).then_inc(s(f"{m}_lo{h}"), 1)

                def x_low(n):
                    dve.wait_ge(s("xt_hi"), n)
                    dve.tensor_tensor(xt_lo[:, :, :], pxt[:, :, :], xt_hi[:, :, :].bitcast(F32), ALU.subtract)\
                        .then_inc(s("xt_lo"), 1)

                def body(b, first):
                    n = b + 1
                    dve.sem_inc(s("covered"), 16)
                    low("w1", b, first)
                    low("w3", b, first)
                    low("w2", b, first)
                    dve.wait_ge(s("sil_ready"), n)
                    dve.wait_ge(s("w3_done"), n)
                    if not first:
                        dve.wait_ge(s("at_turned"), b)
                    dve.tensor_tensor(a[:, :], sil[:, :], pu[:, :], ALU.mult).then_inc(s("a_ready"), 1)
                    x_low(n + 1)
                    dve.wait_ge(s("at_hi"), n)
                    dve.tensor_tensor(at_lo[:, :, :], pat[:, :, :], at_hi[:, :, :].bitcast(F32), ALU.subtract)\
                        .then_inc(s("at_lo"), 1)

                dve.sem_inc(s("y_stored"), 16)
                x_low(1)
                blocks(dve, body)
        ph.close()


def combine(nc, d, layer, streams, plan, final):
    t0 = streams[0][1]
    with ExitStack() as ctx:
        ph = Phase(nc, ctx, f"comb{layer}")
        s = ph.sem
        x = [ph.sb(f"x{b}", [P, D]) for b in range(2)]
        y = [[ph.sb(f"y{j}{b}", [P, D]) for b in range(2)] for j in range(2)]
        idx = [[ph.sb(f"idx{j}{b}", [P, 1], I32) for b in range(2)] for j in range(2)]
        wt = [ph.sb(f"wt{b}", [P, 2]) for b in range(2)]
        gate = ph.sb("gate", [P, 2, D])
        fin_g = ph.sb("fin_g", [P, D])
        junk = ph.sb("junk", [P, D])
        stat = ph.sb("stat", [P, 2, 4])
        eps = ph.sb("eps", [P, 1])
        total = sum(p for _, _, p, _ in streams)
        dst = d.out if final else d.xs

        with nc.Block() as block:
            @block.sync
            def _(sp):
                for st in (LAT, CTX):
                    sp.dma_start(gate[:, st, :], d.mods[layer, st, G2, :].partition_broadcast(P))\
                        .then_inc(s("tables"), 16)
                sp.dma_start(fin_g[:, :], d.final_g.partition_broadcast(P)).then_inc(s("tables"), 16)
                for st, ta, pairs, before in streams:
                    with sp.Fori(0, pairs) as i:
                        for b in range(2):
                            if before:
                                sp.wait_ge(s(f"x_stored{b}"), (i + before) * 16)
                            sp.dma_start(x[b][:, :], d.xs[ds((i * 2 + (ta + b)) * P, P), :])\
                                .then_inc(s(f"x_loaded{b}"), 16)

            @block.gpsimd
            def _(pool):
                for st, ta, pairs, before in streams:
                    with pool.Fori(0, pairs) as i:
                        n = i + (before + 1)
                        for b in range(2):
                            for j in range(2):
                                if before:
                                    pool.wait_ge(s(f"gathered{j}{b}"), (n - 1) * 16)
                                pool.tensor_copy(idx[j][b][:, :], plan.slot[:, j, ds(i * 2 + (ta - t0 + b), 1)])\
                                    .then_inc(s(f"idx_ready{j}{b}"), 1)
                                pool.wait_ge(s(f"idx_ready{j}{b}"), n)
                                if before:
                                    pool.wait_ge(s(f"x_ready{b}"), n - 1)
                                pool.sem_inc(s("gathers"), 1)
                                pool.indirect_dma_start(y[j][b][:, :], None, d.yd[:, :],
                                                        bass.IndirectOffsetOnAxis(idx[j][b][:, :], 0))\
                                    .then_inc(s(f"gathered{j}{b}"), 16)

            @block.scalar
            def _(act):
                act.preload_act_table(ACT.Sqrt)
                for st, ta, pairs, before in streams:
                    with act.Fori(0, pairs) as i:
                        n = i + (before + 1)
                        for b in range(2):
                            act.wait_ge(s(f"x_ready{b}"), n)
                            if final:
                                act.activation(junk[:, :], x[b][:, :], ACT.Square, accum_out=stat[:, b, 0:1])\
                                    .then_inc(s(f"squares{b}"), 1)
                                act.wait_ge(s(f"squares{b}"), n)
                                act.wait_ge(s("eps_set"), 1)
                                act.activation(stat[:, b, 1:2], stat[:, b, 0:1], ACT.Sqrt, bias=eps[:, :],
                                               scale=1.0 / D).then_inc(s(f"root{b}"), 1)
                                act.wait_ge(s(f"normed{b}"), n)
                            row = (i * 2 + (ta + b - (CTX_TILES if final else 0))) * P
                            act.dma_start(dst[ds(row, P), :], x[b][:, :]).then_inc(s(f"x_stored{b}"), 16)
                for b in range(2):
                    act.wait_ge(s(f"x_stored{b}"), 16 * total)

            @block.vector
            def _(dve):
                dve.memset(eps[:, :], EPS).then_inc(s("eps_set"), 1)
                dve.wait_ge(s("tables"), 48)
                for st, ta, pairs, before in streams:
                    with dve.Fori(0, pairs) as i:
                        n = i + (before + 1)
                        for b in range(2):
                            dve.tensor_copy(wt[b][:, :].unsqueeze(2), plan.weight[:, :, ds(i * 2 + (ta - t0 + b), 1)])\
                                .then_inc(s(f"wt_ready{b}"), 1)
                            dve.wait_ge(s(f"wt_ready{b}"), n)
                            dve.wait_ge(s(f"gathered0{b}"), n * 16)
                            dve.tensor_scalar(y[0][b][:, :], y[0][b][:, :], wt[b][:, 0:1], None, ALU.mult)\
                                .then_inc(s(f"first{b}"), 1)
                            dve.wait_ge(s(f"first{b}"), n)
                            dve.wait_ge(s(f"gathered1{b}"), n * 16)
                            dve.scalar_tensor_tensor(y[1][b][:, :], y[1][b][:, :], wt[b][:, 1:2], y[0][b][:, :],
                                                     ALU.mult, ALU.add).then_inc(s(f"second{b}"), 1)
                            dve.wait_ge(s(f"second{b}"), n)
                            dve.tensor_tensor(y[1][b][:, :], y[1][b][:, :], gate[:, st, :], ALU.mult)\
                                .then_inc(s(f"gated{b}"), 1)
                            dve.wait_ge(s(f"gated{b}"), n)
                            dve.wait_ge(s(f"x_loaded{b}"), n * 16)
                            dve.tensor_tensor(x[b][:, :], x[b][:, :], y[1][b][:, :], ALU.add)\
                                .then_inc(s(f"x_ready{b}"), 1)
                            if final:
                                dve.wait_ge(s(f"root{b}"), n)
                                dve.reciprocal(stat[:, b, 2:3], stat[:, b, 1:2]).then_inc(s(f"rstd{b}"), 1)
                                dve.wait_ge(s(f"rstd{b}"), n)
                                dve.scalar_tensor_tensor(x[b][:, :], x[b][:, :], stat[:, b, 2:3], fin_g[:, :],
                                                         ALU.mult, ALU.mult).then_inc(s(f"normed{b}"), 1)
        ph.close()


QK, VG = 2 * HEADS * DK, 2 * HEADS * DV
LAT_TILES = TILES - CTX_TILES
TOKEN_GROUPS = [(0, CTX_LEN), (CTX_LEN, N), (CTX_LEN + N, N)]
SCAN = [(CTX, 0, CTX_TILES - 1, 1, 0), (LAT, CTX_TILES, TILES - 1, 1, 1),
        (LAT, CTX_TILES + 2, TILES - 3, LAT_TILES // 2 - 1, 2)]
LAST = {0: CHUNK - 1, 1: 0}
REF = {0: CHUNK // 2, 1: CHUNK // 2 - 1}


def gla_values(nc, d, ht):
    with ExitStack() as ctx:
        ph = Phase(nc, ctx, "glav")
        s = ph.sem
        raw = ph.sb("raw", [P, KC, N])
        w = [Split(nc, ctx, f"glav_w{b}", [P, KC, N]) for b in range(2)]
        out = [ph.sb(f"out{b}", [P, N]) for b in range(4)]
        acc = [ph.ps(f"acc{b}", [P, N]) for b in range(4)]
        jobs = [("v", 0, 0), ("v", 1, 0), ("gate", 0, CTX_TILES), ("gate", 1, CTX_TILES)]
        steps = [(g, t) for g, job in enumerate(jobs) for t in range(job[2], TILES)]

        with nc.Block() as block:
            @block.sync
            def _(sp):
                def load(g):
                    c0 = QK + g * N
                    if g:
                        sp.wait_ge(s("w_lo"), g)
                    sp.dma_start(raw[:, :, :], d.w_in[:, c0:c0 + N].rearrange("(k p) n -> p k n", p=P))\
                        .then_inc(s("w_loaded"), 16)
                for g in range(len(jobs)):
                    load(g)

            @block.gpsimd
            def _(pool):
                for n, (g, t) in enumerate(steps):
                    kind, half, t0 = jobs[g]
                    dst, row = (d.vd, t * P) if kind == "v" else (d.gd, (t - CTX_TILES) * P)
                    pool.wait_ge(s("out_ready"), n + 1)
                    pool.dma_start(dst[row:row + P, half * N:(half + 1) * N], out[n % 4][:, :])\
                        .then_inc(s(f"stored{n % 4}"), 16)
                for b in range(4):
                    pool.wait_ge(s(f"stored{b}"), 16 * len(range(b, len(steps), 4)))

            @block.tensor
            def _(pe):
                for n, (g, t) in enumerate(steps):
                    if t == jobs[g][2]:
                        pe.wait_ge(s("w_lo"), g + 1)
                    if n >= 4:
                        pe.wait_ge(s("out_ready"), n - 3)
                    cols = slice(t * P, (t + 1) * P)
                    for k in range(KC):
                        last = product3(pe, acc[n % 4][:, :], ht.hi[:, k, cols], ht.lo[:, k, cols],
                                        w[g % 2].hi[:, k, :], w[g % 2].lo[:, k, :], k == 0, k == KC - 1)
                    last.then_inc(s("acc_ready"), 1)

            @block.scalar
            def _(act):
                act.preload_act_table(ACT.Silu)
                starts = [min(n for n, (g, _) in enumerate(steps) if g == q) for q in range(len(jobs))]

                def high(g):
                    act.wait_ge(s("w_loaded"), 16 * (g + 1))
                    if g >= 2:
                        act.wait_ge(s("acc_ready"), starts[g - 1])
                    act.activation(w[g % 2].hi[:, :, :], raw[:, :, :], ACT.Copy).then_inc(s("w_hi"), 1)

                high(0)
                for n, (g, t) in enumerate(steps):
                    if n == starts[g] and g + 1 < len(jobs):
                        high(g + 1)
                    act.wait_ge(s("acc_ready"), n + 1)
                    if n >= 4:
                        act.wait_ge(s(f"stored{n % 4}"), 16 * (n // 4))
                    act.activation(out[n % 4][:, :], acc[n % 4][:, :], ACT.Copy if jobs[g][0] == "v" else ACT.Silu)\
                        .then_inc(s("out_ready"), 1)

            @block.vector
            def _(dve):
                for g in range(len(jobs)):
                    dve.wait_ge(s("w_hi"), g + 1)
                    dve.tensor_tensor(w[g % 2].lo[:, :, :], raw[:, :, :], w[g % 2].hi[:, :, :].bitcast(F32),
                                      ALU.subtract).then_inc(s("w_lo"), 1)
        ph.close()


def gla_keys(nc, d, ht, qk, cum):
    with ExitStack() as ctx:
        ph = Phase(nc, ctx, "glak")
        s = ph.sem
        raw = ph.sb("raw", [P, KC, P])
        w = [Split(nc, ctx, f"glak_w{b}", [P, KC, P]) for b in range(2)]
        lr_raw = ph.sb("lr_raw", [P, KC, 2, RANK])
        lr_w = Split(nc, ctx, "glak_lrw", [P, KC, 2, RANK])
        low = [ph.sb(f"low{r}", [RANK + 1, TOK]) for r in range(2)]
        up = [ph.sb(f"up{r}", [RANK + 1, HEADS * DK]) for r in range(2)]
        cums = ph.sb("cums", [P, 2, P])
        e = [ph.sb(f"e{b}", [P, HEADS * DK]) for b in range(2)]
        logs = [ph.sb(f"logs{b}", [P, HEADS * DK]) for b in range(2)]
        acc = [ph.ps(f"acc{g}", [P, N]) for g in range(3)]
        pz = [ph.ps(f"pz{b}", [P, N]) for b in range(2)]
        pc = [ph.ps(f"pc{b}", [P, N]) for b in range(2)]
        chunks = QK // P
        pairs = chunks // 2
        units = [(t, r) for t in range(TILES) for r in range(2)]

        with nc.Block() as block:
            @block.sync
            def _(sp):
                sp.dma_start(lr_raw[:, :, :, :].rearrange("p k r n -> p k (r n)"),
                             d.w_in[:, QK + VG:GLA_IN].rearrange("(k p) n -> p k n", p=P)).then_inc(s("lr_loaded"), 16)
                for r in range(2):
                    sp.dma_start(up[r][0:RANK, :], d.gk_up[r]).then_inc(s("up_loaded"), 16)
                    sp.dma_start(up[r][RANK:RANK + 1, :], d.gk_b[r:r + 1, :]).then_inc(s("up_loaded"), 16)
                sp.dma_start(cums[:, :, :], d.cums).then_inc(s("up_loaded"), 16)

                def load(b, i):
                    sp.dma_start(raw[:, :, :], d.w_in[:, ds((i * 2 + b) * P, P)].rearrange("(k p) n -> p k n", p=P))\
                        .then_inc(s(f"w_loaded{b}"), 16)

                load(0, 0)
                sp.wait_ge(s("w_lo0"), 1)
                load(1, 0)
                with sp.Fori(1, pairs) as i:
                    for b in range(2):
                        sp.wait_ge(s(f"w_lo{1 - b}"), i + b)
                        load(b, i)

            @block.gpsimd
            def _(pool):
                for r in range(2):
                    pool.memset(low[r][:, :], 1.0).then_inc(s("ones_set"), 1)

            @block.tensor
            def _(pe):
                pe.wait_ge(s("lr_lo"), 1)
                for r in range(2):
                    for g, (a, n) in enumerate(TOKEN_GROUPS):
                        if r:
                            pe.wait_ge(s("low_ready"), g + 1)
                        for k in range(KC):
                            last = product3(pe, acc[g][0:RANK, 0:n], lr_w.hi[:, k, r, :], lr_w.lo[:, k, r, :],
                                            ht.hi[:, k, a:a + n], ht.lo[:, k, a:a + n], k == 0, k == KC - 1)
                        last.then_inc(s("low_summed"), 1)

                def chunk(b, i, first):
                    pe.wait_ge(s(f"w_lo{b}"), i + 1)
                    for g, (a, n) in enumerate(TOKEN_GROUPS):
                        if first and b == 0:
                            pe.wait_ge(s("low_ready"), len(TOKEN_GROUPS) + g + 1)
                        else:
                            pe.wait_ge(s(f"qk_ready{g}{1 - b}"), i + b)
                        for k in range(KC):
                            last = product3(pe, acc[g][:, 0:n], w[b].hi[:, k, :], w[b].lo[:, k, :],
                                            ht.hi[:, k, a:a + n], ht.lo[:, k, a:a + n], k == 0, k == KC - 1)
                        last.then_inc(s(f"qk_summed{g}{b}"), 1)

                for b in range(2):
                    chunk(b, 0, True)
                with pe.Fori(1, pairs) as i:
                    for b in range(2):
                        chunk(b, i, False)

                pe.wait_ge(s("up_loaded"), 80)

                def sums(n):
                    t, r = units[n]
                    pe.wait_ge(s("logs_ready"), n + 1)
                    if n >= 2:
                        pe.wait_ge(s("cum_ready"), n - 1)
                    for h in range(HEADS):
                        last = pe.matmul(pc[n % 2][:, h * P:(h + 1) * P], logs[n % 2][:, h * DK:(h + 1) * DK],
                                         cums[:, r, :], start=True, stop=True)
                    last.then_inc(s("cum_summed"), 1)

                for n, (t, r) in enumerate(units):
                    if n >= 2:
                        pe.wait_ge(s("e_ready"), n - 1)
                        pe.wait_ge(s("z_ready"), n - 1)
                    pe.matmul(pz[n % 2][:, :], low[r][:, t * P:(t + 1) * P], up[r][:, :], start=True, stop=True)\
                        .then_inc(s("z_summed"), 1)
                    if n:
                        sums(n - 1)
                sums(len(units) - 1)

            @block.scalar
            def _(act):
                act.preload_act_table_set("natural_log_exp_and_others")
                act.wait_ge(s("lr_loaded"), 16)
                act.activation(lr_w.hi[:, :, :, :], lr_raw[:, :, :, :], ACT.Copy).then_inc(s("lr_hi"), 1)
                act.wait_ge(s("ones_set"), 2)
                for r in range(2):
                    for g, (a, n) in enumerate(TOKEN_GROUPS):
                        act.wait_ge(s("low_summed"), r * 3 + g + 1)
                        act.activation(low[r][0:RANK, a:a + n], acc[g][0:RANK, 0:n], ACT.Copy)\
                            .then_inc(s("low_ready"), 1)

                def high(b, i, first):
                    act.wait_ge(s(f"w_loaded{b}"), i * 16 + 16)
                    if not first:
                        act.wait_ge(s(f"qk_summed2{b}"), i)
                    act.activation(w[b].hi[:, :, :], raw[:, :, :], ACT.Copy).then_inc(s(f"w_hi{b}"), 1)

                def chunk(b, i):
                    for g, (a, n) in enumerate(TOKEN_GROUPS):
                        act.wait_ge(s(f"qk_summed{g}{b}"), i + 1)
                        act.activation(qk[:, ds(i * 2 + b, 1), a:a + n].rearrange("p o n -> p (o n)"),
                                       acc[g][:, 0:n], ACT.Copy).then_inc(s(f"qk_ready{g}{b}"), 1)

                for b in range(2):
                    high(b, 0, True)
                for b in range(2):
                    chunk(b, 0)
                with act.Fori(1, pairs) as i:
                    for b in range(2):
                        high(b, i, False)
                    for b in range(2):
                        chunk(b, i)

                for n, (t, r) in enumerate(units):
                    b = n % 2
                    act.wait_ge(s("z_summed"), n + 1)
                    if n >= 2:
                        act.wait_ge(s("logs_ready"), n - 1)
                    act.activation(e[b][:, :], pz[b][:, :], ACT.Abs).then_inc(s("e_ready"), 1)
                    act.wait_ge(s("e_ready"), n + 1)
                    act.activation(e[b][:, :], e[b][:, :], ACT.Exp, scale=-1.0).then_inc(s("e_exp"), 1)
                    act.wait_ge(s("e_exp"), n + 1)
                    act.activation(e[b][:, :], e[b][:, :], ACT.Ln, bias=1.0).then_inc(s("e_log"), 1)

            @block.vector
            def _(dve):
                dve.wait_ge(s("lr_hi"), 1)
                dve.tensor_tensor(lr_w.lo[:, :, :, :], lr_raw[:, :, :, :], lr_w.hi[:, :, :, :].bitcast(F32),
                                  ALU.subtract).then_inc(s("lr_lo"), 1)

                def lows(b, i):
                    dve.wait_ge(s(f"w_hi{b}"), i + 1)
                    dve.tensor_tensor(w[b].lo[:, :, :], raw[:, :, :], w[b].hi[:, :, :].bitcast(F32),
                                      ALU.subtract).then_inc(s(f"w_lo{b}"), 1)

                for b in range(2):
                    lows(b, 0)
                with dve.Fori(1, pairs) as i:
                    for b in range(2):
                        lows(b, i)

                def take(n):
                    t, r = units[n]
                    dve.wait_ge(s("cum_summed"), n + 1)
                    dve.tensor_copy(cum[:, r, :, t * P:(t + 1) * P],
                                    pc[n % 2][:, :].rearrange("p (h n) -> p h n", h=HEADS)).then_inc(s("cum_ready"), 1)

                for n, (t, r) in enumerate(units):
                    b = n % 2
                    dve.wait_ge(s("e_ready"), n + 1)
                    if n >= 2:
                        dve.wait_ge(s("cum_summed"), n - 1)
                    dve.tensor_scalar(logs[b][:, :], pz[b][:, :], 0.0, None, ALU.min).then_inc(s("z_ready"), 1)
                    dve.wait_ge(s("z_ready"), n + 1)
                    dve.wait_ge(s("e_log"), n + 1)
                    dve.tensor_tensor(logs[b][:, :], logs[b][:, :], e[b][:, :], ALU.subtract).then_inc(s("logs_ready"), 1)
                    if n:
                        take(n - 1)
                take(len(units) - 1)
        ph.close()


def gla_scan(nc, d, qk, cum):
    with ExitStack() as ctx:
        ph = Phase(nc, ctx, "scan")
        s = ph.sem
        W = HEADS * P
        v = [[ph.sb(f"v{r}{b}", [P, HEADS * DV]) for b in range(2)] for r in range(2)]
        names = ("cr", "cl", "eq", "ek", "es", "el", "qi", "ki", "qs", "ks")
        t_ = {m: [ph.sb(f"{m}{r}", [P, HEADS, P]) for r in range(2)] for m in names}
        att = [ph.sb(f"att{r}", [P, HEADS, P]) for r in range(2)]
        kst = [ph.sb(f"kst{r}", [P, HEADS, P]) for r in range(2)]
        state = [ph.sb(f"state{r}", [P, HEADS, DV]) for r in range(2)]
        o = [ph.sb(f"o{r}", [P, HEADS * DV]) for r in range(2)]
        seen = ph.sb("seen", [P, 2, CHUNK], I32)
        ident = ph.sb("ident", [P, P])
        patt = ph.ps("patt", [P, 2, HEADS, CHUNK])
        pkst = ph.ps("pkst", [P, HEADS, P])
        po = [ph.ps(f"po{r}", [P, HEADS, DV]) for r in range(2)]
        pds = ph.ps("pds", [P, HEADS, DV])

        def tile(i, b, r, ta, tb):
            return i * 2 + (ta + b) if r == 0 else i * -2 + (tb - b)

        def after(eng, what, r, b, n, first, per=1):
            if b == 1:
                eng.wait_ge(s(f"{what}{r}0"), n * per)
            elif not first:
                eng.wait_ge(s(f"{what}{r}1"), (n - 1) * per)

        def order(r):
            return (0, 1) if r == 0 else (1, 0)

        with nc.Block() as block:
            @block.sync
            def _(sp):
                sp.dma_start(seen[:, :, :], d.seen).then_inc(s("tables"), 16)
                sp.dma_start(ident[:, :], d.ident).then_inc(s("tables"), 16)
                for st, ta, tb, pairs, before in SCAN:
                    with sp.Fori(0, pairs) as i:
                        n, first = i + (before + 1), before == 0
                        m, first_lat = i + before, before == 1
                        for b in range(2):
                            for r in range(2):
                                if before:
                                    sp.wait_ge(s(f"pds1{r}{b}"), (n - 1) * 2)
                                sp.dma_start(v[r][b][:, :], d.vd[ds(tile(i, b, r, ta, tb) * P, P), :])\
                                    .then_inc(s(f"v_loaded{r}{b}"), 16)

            @block.gpsimd
            def _(pool):
                for r in range(2):
                    pool.memset(att[r][:, :, :], 0.0).then_inc(s("zeroed"), 1)
                    pool.memset(state[r][:, :, :], 0.0).then_inc(s("zeroed"), 1)
                for st, ta, tb, pairs, before in SCAN:
                    if st == CTX:
                        continue
                    with pool.Fori(0, pairs) as i:
                        for b in range(2):
                            for r in range(2):
                                row = (tile(i, b, r, ta, tb) - CTX_TILES) * P
                                pool.wait_ge(s(f"o_ready{r}{b}"), i + before)
                                pool.dma_start(d.od[r, ds(row, P), :], o[r][:, :]).then_inc(s(f"o_stored{r}{b}"), 16)
                for b in range(2):
                    for r in range(2):
                        pool.wait_ge(s(f"o_stored{r}{b}"), 16 * (LAT_TILES // 2))

            @block.tensor
            def _(pe):
                pe.wait_ge(s("tables"), 32)
                for st, ta, tb, pairs, before in SCAN:
                    with pe.Fori(0, pairs) as i:
                        n, first = i + (before + 1), before == 0
                        m, first_lat = i + before, before == 1
                        for b in range(2):
                            if st == LAT:
                                for r in range(2):
                                    pe.wait_ge(s(f"qi{r}{b}"), m)
                                    pe.wait_ge(s(f"ki{r}{b}"), m)
                                    after(pe, "masked", 1, b, m, first_lat, 2)
                                    for h in range(HEADS):
                                        for c in range(2):
                                            at = slice(c * CHUNK, (c + 1) * CHUNK)
                                            last = pe.matmul(patt[at, r, h, :], t_["ki"][r][:, h, at],
                                                             t_["qi"][r][:, h, at], start=True, stop=True)
                                    last.then_inc(s(f"scored{r}{b}"), 1)
                            for r in range(2):
                                pe.wait_ge(s(f"ks{r}{b}"), n)
                                if r == 1:
                                    pe.wait_ge(s(f"kst0{b}"), n)
                                else:
                                    after(pe, "kst", 1, b, n, first)
                                for h in range(HEADS):
                                    last = pe.transpose(pkst[:, h, :], t_["ks"][r][:, h, :], ident[:, :])
                                last.then_inc(s(f"turned{r}{b}"), 1)
                            for j in range(2):
                                for r in range(2):
                                    c = order(r)[j]
                                    at = slice(c * CHUNK, (c + 1) * CHUNK)
                                    if j == 0:
                                        pe.wait_ge(s(f"v_loaded{r}{b}"), n * 16)
                                    if st == LAT:
                                        if j == 0:
                                            pe.wait_ge(s(f"masked{r}{b}"), m * 2)
                                            after(pe, "o_ready", r, b, m, first_lat)
                                            for h in range(HEADS):
                                                pe.matmul(po[r][:, h, :], att[r][:, h, :],
                                                          v[r][b][:, h * DV:(h + 1) * DV], start=h % 2 == 0, stop=False)
                                        for half in range(2):
                                            if j == 1:
                                                pe.wait_ge(s(f"state{half}{r}{b}"), n * 2 - 1)
                                            else:
                                                after(pe, f"state{half}", r, b, n, first, 2)
                                                pe.wait_ge(s(f"qs{r}{b}"), m)
                                        for h in range(HEADS):
                                            last = pe.matmul(po[r][at, h, :], t_["qs"][r][:, h, at],
                                                             state[r][:, h, :], start=False, stop=h % 2 == 1)
                                        if j == 1:
                                            last.then_inc(s(f"o_summed{r}{b}"), 1)
                                    if j == 0:
                                        pe.wait_ge(s(f"kst{r}{b}"), n)
                                    for half in range(2):
                                        if r == 1:
                                            pe.wait_ge(s(f"state{half}0{b}"), n * 2 - (1 - j))
                                        elif j == 1:
                                            pe.wait_ge(s(f"state{half}1{b}"), n * 2 - 1)
                                        else:
                                            after(pe, f"state{half}", 1, b, n, first, 2)
                                        for h in range(half * 2, half * 2 + 2):
                                            last = pe.matmul(pds[:, h, :], kst[r][at, h, :],
                                                             v[r][b][at, h * DV:(h + 1) * DV], start=True, stop=True)
                                        last.then_inc(s(f"pds{half}{r}{b}"), 1)

            @block.scalar
            def _(act):
                act.preload_act_table(ACT.Exp)
                for st, ta, tb, pairs, before in SCAN:
                    with act.Fori(0, pairs) as i:
                        n, first = i + (before + 1), before == 0
                        m, first_lat = i + before, before == 1
                        for b in range(2):
                            for r in range(2):
                                act.wait_ge(s(f"cl{r}{b}"), n)
                                after(act, "ks", r, b, n, first)
                                act.activation(t_["el"][r][:, :, :], t_["cl"][r][:, :, :], ACT.Exp)\
                                    .then_inc(s(f"el{r}{b}"), 1)
                                t = tile(i, b, r, ta, tb)
                                after(act, "state1", r, b, n, first, 2)
                                act.activation(t_["es"][r][:, :, :], cum[:, r, :, ds(t * P, P)], ACT.Exp)\
                                    .then_inc(s(f"es{r}{b}"), 1)
                                if st == LAT:
                                    act.wait_ge(s(f"cr{r}{b}"), m)
                                    act.activation(t_["eq"][r][:, :, :], t_["cr"][r][:, :, :], ACT.Exp)\
                                        .then_inc(s(f"eq{r}{b}"), 1)
                                    act.activation(t_["ek"][r][:, :, :], t_["cr"][r][:, :, :], ACT.Exp, scale=-1.0)\
                                        .then_inc(s(f"ek{r}{b}"), 1)
                            for r in range(2):
                                act.wait_ge(s(f"turned{r}{b}"), n)
                                after(act, "pds1", r, b, n, first, 2)
                                act.activation(kst[r][:, :, :], pkst[:, :, :], ACT.Copy).then_inc(s(f"kst{r}{b}"), 1)
                            if st == LAT:
                                for r in range(2):
                                    act.wait_ge(s(f"o_summed{r}{b}"), m)
                                    after(act, "o_stored", r, b, m, first_lat, 16)
                                    act.activation(o[r][:, :], po[r][:, :, :].rearrange("p h n -> p (h n)"), ACT.Copy)\
                                        .then_inc(s(f"o_ready{r}{b}"), 1)

            @block.vector
            def _(dve):
                dve.wait_ge(s("tables"), 32)
                dve.wait_ge(s("zeroed"), 4)

                def chunks(ap):
                    return ap.rearrange("p h (c n) -> p h c n", c=2)

                for st, ta, tb, pairs, before in SCAN:
                    with dve.Fori(0, pairs) as i:
                        n, first = i + (before + 1), before == 0
                        m, first_lat = i + before, before == 1
                        for b in range(2):
                            for r in range(2):
                                t = tile(i, b, r, ta, tb)
                                cv = chunks(cum[:, r, :, ds(t * P, P)])
                                shape = [P, HEADS, 2, CHUNK]
                                after(dve, "el", r, b, n, first)
                                dve.tensor_tensor(chunks(t_["cl"][r][:, :, :]),
                                                  cv[:, :, :, LAST[r]:LAST[r] + 1].to_broadcast(shape), cv,
                                                  ALU.subtract).then_inc(s(f"cl{r}{b}"), 1)
                                if st == LAT:
                                    after(dve, "ek", r, b, m, first_lat)
                                    dve.tensor_tensor(chunks(t_["cr"][r][:, :, :]), cv,
                                                      cv[:, :, :, REF[r]:REF[r] + 1].to_broadcast(shape),
                                                      ALU.subtract).then_inc(s(f"cr{r}{b}"), 1)
                            for r in range(2):
                                t = tile(i, b, r, ta, tb)
                                q = qk[:, 0:HEADS, ds(t * P, P)]
                                k = qk[:, HEADS:2 * HEADS, ds(t * P, P)]
                                dve.wait_ge(s(f"el{r}{b}"), n)
                                after(dve, "turned", r, b, n, first)
                                dve.tensor_tensor(t_["ks"][r][:, :, :], k, t_["el"][r][:, :, :], ALU.mult)\
                                    .then_inc(s(f"ks{r}{b}"), 1)
                                if st == LAT:
                                    dve.wait_ge(s(f"eq{r}{b}"), m)
                                    dve.scalar_tensor_tensor(t_["qi"][r][:, :, :], q, DK ** -0.5,
                                                             t_["eq"][r][:, :, :], ALU.mult, ALU.mult)\
                                        .then_inc(s(f"qi{r}{b}"), 1)
                                    dve.wait_ge(s(f"ek{r}{b}"), m)
                                    dve.tensor_tensor(t_["ki"][r][:, :, :], k, t_["ek"][r][:, :, :], ALU.mult)\
                                        .then_inc(s(f"ki{r}{b}"), 1)
                                dve.wait_ge(s(f"es{r}{b}"), n)
                                if st == LAT:
                                    after(dve, "o_summed", r, b, m, first_lat)
                                    dve.scalar_tensor_tensor(t_["qs"][r][:, :, :], q, DK ** -0.5,
                                                             t_["es"][r][:, :, :], ALU.mult, ALU.mult)\
                                        .then_inc(s(f"qs{r}{b}"), 1)
                            if st == LAT:
                                for r in range(2):
                                    dve.wait_ge(s(f"scored1{b}"), m)
                                    dve.sem_inc(s("score_tiles"), 1)
                                    for c in range(2):
                                        at = slice(c * CHUNK, (c + 1) * CHUNK)
                                        dve.copy_predicated(att[r][at, :, at],
                                                            seen[at, r:r + 1, :].to_broadcast([CHUNK, HEADS, CHUNK]),
                                                            patt[at, r, :, :]).then_inc(s(f"masked{r}{b}"), 1)
                            for j in range(2):
                                for r in range(2):
                                    c = order(r)[j]
                                    end = c * CHUNK + LAST[r]
                                    for half in range(2):
                                        dve.wait_ge(s(f"pds{half}{r}{b}"), n * 2 - (1 - j))
                                        if j == 1:
                                            dve.wait_ge(s(f"state{half}{r}{b}"), n * 2 - 1)
                                        else:
                                            after(dve, f"state{half}", r, b, n, first, 2)
                                        for h in range(half * 2, half * 2 + 2):
                                            last = dve.scalar_tensor_tensor(
                                                state[r][:, h, :], state[r][:, h, :], t_["es"][r][:, h, end:end + 1],
                                                pds[:, h, :], ALU.mult, ALU.add)
                                        last.then_inc(s(f"state{half}{r}{b}"), 1)
        ph.close()


def gla_output(nc, d):
    with ExitStack() as ctx:
        ph = Phase(nc, ctx, "wo")
        s = ph.sem
        raw = ph.sb("raw", [P, 2, D])
        w = Split(nc, ctx, "wo_w", [P, KC, D])
        ident = ph.sb("ident", [P, P])
        head_g = ph.sb("head_g", [P, D])
        res_gate = ph.sb("res_gate", [P, D])
        eps = ph.sb("eps", [P, 1])
        o = [[ph.sb(f"o{r}{b}", [P, HEADS, DV]) for b in range(2)] for r in range(2)]
        gate = [ph.sb(f"gate{b}", [P, HEADS, DV]) for b in range(2)]
        x = [ph.sb(f"x{b}", [P, D]) for b in range(2)]
        junk = ph.sb("junk", [P, HEADS, DV])
        stat = ph.sb("stat", [P, 2, 3, HEADS])
        ot = [Split(nc, ctx, f"wo_ot{b}", [P, KC, P]) for b in range(2)]
        y = [ph.sb(f"y{b}", [P, D]) for b in range(2)]
        pt = [ph.ps(f"pt{b}", [P, KC, P]) for b in range(2)]
        py = [ph.ps(f"py{b}", [P, D]) for b in range(2)]
        total = LAT_TILES // 2

        with nc.Block() as block:
            @block.sync
            def _(sp):
                sp.dma_start(ident[:, :], d.ident).then_inc(s("tables"), 16)
                sp.dma_start(head_g[:, :], d.head_g[0, :].partition_broadcast(P)).then_inc(s("tables"), 16)
                sp.dma_start(res_gate[:, :], d.mods[1, LAT, G1, :].partition_broadcast(P)).then_inc(s("tables"), 16)
                for k in range(KC):
                    if k >= 2:
                        sp.wait_ge(s("w_lo"), k - 1)
                    sp.dma_start(raw[:, k % 2, :], d.w_o[k * P:(k + 1) * P, :]).then_inc(s(f"w_loaded{k % 2}"), 16)
                for st, t0, pairs, before in LAT_STREAMS:
                    with sp.Fori(0, pairs) as i:
                        n = i + (before + 1)
                        for b in range(2):
                            row = (i * 2 + (t0 + b - CTX_TILES)) * P
                            if before:
                                sp.wait_ge(s(f"turned{b}"), n - 1)
                            for r in range(2):
                                sp.dma_start(o[r][b][:, :, :].rearrange("p h n -> p (h n)"), d.od[r, ds(row, P), :])\
                                    .then_inc(s(f"o_loaded{b}"), 16)
                            sp.dma_start(gate[b][:, :, :].rearrange("p h n -> p (h n)"), d.gd[ds(row, P), :])\
                                .then_inc(s(f"o_loaded{b}"), 16)
                            if before:
                                sp.wait_ge(s(f"stored{b}"), (n - 1) * 16)
                            sp.dma_start(x[b][:, :], d.xs[ds(row + CTX_LEN, P), :]).then_inc(s(f"x_loaded{b}"), 16)

            @block.gpsimd
            def _(pool):
                for st, t0, pairs, before in LAT_STREAMS:
                    with pool.Fori(0, pairs) as i:
                        for b in range(2):
                            pool.wait_ge(s(f"x_ready{b}"), i + (before + 1))
                            pool.dma_start(d.xs[ds((i * 2 + (t0 + b)) * P, P), :], x[b][:, :])\
                                .then_inc(s(f"stored{b}"), 16)
                for b in range(2):
                    pool.wait_ge(s(f"stored{b}"), 16 * total)

            @block.tensor
            def _(pe):
                pe.wait_ge(s("tables"), 48)
                pe.wait_ge(s("w_lo"), KC)
                for st, t0, pairs, before in LAT_STREAMS:
                    with pe.Fori(0, pairs) as i:
                        n = i + (before + 1)
                        for b in range(2):
                            pe.wait_ge(s(f"gated{b}"), n)
                            if before:
                                pe.wait_ge(s(f"ot_lo{b}"), n - 1)
                            for k in range(KC):
                                h, c = divmod(k * P, DV)
                                last = pe.transpose(pt[b][:, k, :], o[0][b][:, h, c:c + P], ident[:, :])
                            last.then_inc(s(f"turned{b}"), 1)
                        for b in range(2):
                            pe.wait_ge(s(f"ot_lo{b}"), n)
                            if before:
                                pe.wait_ge(s(f"y_gated{b}"), n - 1)
                            for h in range(2):
                                cols = slice(h * N, (h + 1) * N)
                                for k in range(KC):
                                    last = product3(pe, py[b][:, cols], ot[b].hi[:, k, :], ot[b].lo[:, k, :],
                                                    w.hi[:, k, cols], w.lo[:, k, cols], k == 0, k == KC - 1)
                            last.then_inc(s(f"y_ready{b}"), 1)

            @block.scalar
            def _(act):
                act.preload_act_table(ACT.Sqrt)
                for k in range(KC):
                    act.wait_ge(s(f"w_loaded{k % 2}"), 16 * (k // 2 + 1))
                    act.activation(w.hi[:, k, :], raw[:, k % 2, :], ACT.Copy).then_inc(s("w_hi"), 1)
                act.wait_ge(s("eps_set"), 1)
                for st, t0, pairs, before in LAT_STREAMS:
                    with act.Fori(0, pairs) as i:
                        n = i + (before + 1)
                        for b in range(2):
                            act.wait_ge(s(f"o_added{b}"), n)
                            for h in range(HEADS):
                                last = act.activation(junk[:, h, :], o[0][b][:, h, :], ACT.Square,
                                                      accum_out=stat[:, b, 0, h:h + 1])
                            last.then_inc(s(f"squares{b}"), 1)
                            act.wait_ge(s(f"squares{b}"), n)
                            if before:
                                act.wait_ge(s(f"rstd{b}"), n - 1)
                            act.activation(stat[:, b, 1, :], stat[:, b, 0, :], ACT.Sqrt, bias=eps[:, :],
                                           scale=1.0 / DV).then_inc(s(f"root{b}"), 1)
                        for b in range(2):
                            act.wait_ge(s(f"turned{b}"), n)
                            if before:
                                act.wait_ge(s(f"y_ready{b}"), n - 1)
                            act.activation(ot[b].hi[:, :, :], pt[b][:, :, :], ACT.Copy).then_inc(s(f"ot_hi{b}"), 1)

            @block.vector
            def _(dve):
                dve.memset(eps[:, :], EPS).then_inc(s("eps_set"), 1)
                for k in range(KC):
                    dve.wait_ge(s("w_hi"), k + 1)
                    dve.tensor_tensor(w.lo[:, k, :], raw[:, k % 2, :], w.hi[:, k, :].bitcast(F32), ALU.subtract)\
                        .then_inc(s("w_lo"), 1)
                dve.wait_ge(s("tables"), 48)
                for st, t0, pairs, before in LAT_STREAMS:
                    with dve.Fori(0, pairs) as i:
                        n = i + (before + 1)
                        for b in range(2):
                            dve.wait_ge(s(f"o_loaded{b}"), n * 48)
                            dve.tensor_tensor(o[0][b][:, :, :], o[0][b][:, :, :], o[1][b][:, :, :], ALU.add)\
                                .then_inc(s(f"o_added{b}"), 1)
                            dve.tensor_tensor(gate[b][:, :, :].rearrange("p h n -> p (h n)"),
                                              gate[b][:, :, :].rearrange("p h n -> p (h n)"), head_g[:, :], ALU.mult)\
                                .then_inc(s(f"gain{b}"), 1)
                        for b in range(2):
                            dve.wait_ge(s(f"root{b}"), n)
                            dve.reciprocal(stat[:, b, 2, :], stat[:, b, 1, :]).then_inc(s(f"rstd{b}"), 1)
                            dve.wait_ge(s(f"rstd{b}"), n)
                            dve.wait_ge(s(f"gain{b}"), n)
                            for h in range(HEADS):
                                last = dve.scalar_tensor_tensor(o[0][b][:, h, :], o[0][b][:, h, :],
                                                                stat[:, b, 2, h:h + 1], gate[b][:, h, :],
                                                                ALU.mult, ALU.mult)
                            last.then_inc(s(f"gated{b}"), 1)
                        for b in range(2):
                            dve.wait_ge(s(f"ot_hi{b}"), n)
                            dve.tensor_tensor(ot[b].lo[:, :, :], pt[b][:, :, :], ot[b].hi[:, :, :].bitcast(F32),
                                              ALU.subtract).then_inc(s(f"ot_lo{b}"), 1)
                        for b in range(2):
                            dve.wait_ge(s(f"y_ready{b}"), n)
                            dve.tensor_tensor(y[b][:, :], py[b][:, :], res_gate[:, :], ALU.mult)\
                                .then_inc(s(f"y_gated{b}"), 1)
                            dve.wait_ge(s(f"y_gated{b}"), n)
                            dve.wait_ge(s(f"x_loaded{b}"), n * 16)
                            dve.tensor_tensor(x[b][:, :], x[b][:, :], y[b][:, :], ALU.add)\
                                .then_inc(s(f"x_ready{b}"), 1)
        ph.close()

MAX_BLOCKS = 2 * TILES + EXPERTS
OUT_SHAPE = (1, SEQ, D)


def moe(nc, d, layer, streams, final):
    with ExitStack() as ctx:
        plan = Plan(nc, ctx, layer, TILES - streams[0][1])
        with ExitStack() as inner:
            ht = Split(nc, inner, f"ht_moe{layer}", [P, KC, TOK])
            normalise(nc, d, layer, 1, streams, ht, d.hd)
            route(nc, d, layer, streams, ht, plan)
        experts(nc, d, layer, plan)
        combine(nc, d, layer, streams, plan, final)


def conv_layer(nc, d):
    with ExitStack() as ctx:
        vt = ctx.enter_context(nc.sbuf_tensor("taps_out", [P, KC, CONV_OUT], F32))
        vecs = ctx.enter_context(nc.sbuf_tensor("channel_vectors", [P, KC, VEC_ROWS], F32))
        with ExitStack() as inner:
            ht = Split(nc, inner, "ht_conv", [P, KC, TOK])
            normalise(nc, d, 0, 0, STREAMS, ht)
            conv_taps(nc, d, ht, vt, vecs)
        conv_out(nc, d, vt, vecs)


def gla_layer(nc, d):
    with ExitStack() as ctx, ExitStack() as rows:
        ht = Split(nc, rows, "ht_gla", [P, KC, TOK], side="right")
        normalise(nc, d, 1, 0, STREAMS, ht)
        gla_values(nc, d, ht)
        qk = ctx.enter_context(nc.sbuf_tensor("qk", [P, 2 * HEADS, TOK], F32))
        cum = ctx.enter_context(nc.sbuf_tensor("cum", [P, 2, HEADS, TOK], F32))
        gla_keys(nc, d, ht, qk, cum)
        rows.close()
        gla_scan(nc, d, qk, cum)
    gla_output(nc, d)


def program(nc, d):
    Phase.pool_dma = []
    modulation(nc, d)
    conv_layer(nc, d)
    moe(nc, d, 0, STREAMS, False)
    gla_layer(nc, d)
    moe(nc, d, 1, LAT_STREAMS, True)


class Dram:

    def __init__(self, nc, a, out):
        def scratch(name, shape, dt=F32):
            return nc.dram_tensor("scratch_" + name, shape, dt, kind="Internal").ap()

        self.x, self.c, self.ctx, self.c_ctx = a["in_x"], a["in_c"], a["in_ctx"], a["in_c_ctx"]
        self.ada_w, self.ada_b, self.norm_g, self.final_g = a["in_ada_w"], a["in_ada_b"], a["in_norm_g"], a["in_final_g"]
        self.pw1_w, self.pw1_b = a["in_conv_pw1_w"][0], a["in_conv_pw1_b"]
        self.dw_w, self.dw_b = a["in_conv_dw_w"][0], a["in_conv_dw_b"]
        self.ln_g, self.ln_b = a["in_conv_ln_g"], a["in_conv_ln_b"]
        self.pw2_w, self.pw2_b = a["in_conv_pw2_w"][0], a["in_conv_pw2_b"]
        self.w_in, self.gk_up, self.gk_b = a["in_gla_w_in"][0], a["in_gla_gk_up"][0], a["in_gla_gk_b"][0]
        self.head_g, self.w_o = a["in_gla_head_g"], a["in_gla_w_o"][0]
        self.wg, self.bg, self.wr, self.br = a["in_moe_wg"], a["in_moe_bg"], a["in_moe_wr"], a["in_moe_br"]
        self.w1, self.w3, self.w2 = a["in_moe_w1"], a["in_moe_w3"], a["in_moe_w2"]
        self.pos_row, self.pos_col, self.ident = a["const_pos_row"], a["const_pos_col"], a["const_ident"]
        self.mean_w, self.ones, self.before = a["const_mean_w"], a["const_ones"], a["const_before"]
        self.iota, self.token = a["const_iota"], a["const_token"]
        self.cums, self.seen = a["const_cums"], a["const_seen"]
        self.out = out if len(out.shape) == 2 else out[0]
        self.xs = scratch("residual", (TOK, D))
        self.mods = scratch("modulation", (2, 2, 6, D))
        self.hd = scratch("experts_in", (TOK, D))
        self.vd = scratch("gla_values", (TOK, D))
        self.gd = scratch("gla_gates", (SEQ, D))
        self.od = scratch("gla_out", (2, SEQ, D))
        self.yd = scratch("experts_out", (MAX_BLOCKS * BLK, D))


_INS = ['x', 'c', 'ctx', 'c_ctx', 'ada_w', 'ada_b', 'norm_g', 'final_g', 'conv_pw1_w', 'conv_pw1_b', 'conv_dw_w',
        'conv_dw_b', 'conv_ln_g', 'conv_ln_b', 'conv_pw2_w', 'conv_pw2_b', 'gla_w_in', 'gla_gk_up', 'gla_gk_b',
        'gla_head_g', 'gla_w_o', 'moe_wg', 'moe_bg', 'moe_wr', 'moe_br', 'moe_w1', 'moe_w3', 'moe_w2']


def shape_tables():
    quarter = D // 4
    omega = (1.0 / (10000.0 ** (np.arange(quarter, dtype=np.float32) / np.float32(quarter)))).astype(np.float32)
    ar = np.arange(SEQ // GRID_W, dtype=np.float32)[:, None] * omega
    ac = np.arange(GRID_W, dtype=np.float32)[:, None] * omega
    k = np.arange(P)
    same = (k[:, None] // CHUNK) == (k[None, :] // CHUNK)
    return {
        'pos_row': np.concatenate([np.sin(ar), np.cos(ar)], axis=1).astype(np.float32),
        'pos_col': np.concatenate([np.sin(ac), np.cos(ac)], axis=1).astype(np.float32),
        'ident': np.eye(P, dtype=np.float32),
        'mean_w': np.full((P, P), 1.0 / D, np.float32),
        'ones': np.ones((P, P), np.float32),
        'before': (k[:, None] < k[None, :]).astype(np.float32),
        'iota': np.broadcast_to(np.arange(P, dtype=np.float32), (P, P)).copy(),
        'token': (np.arange(TILES, dtype=np.float32)[None, :] * P + k[:, None].astype(np.float32)).astype(np.float32),
        'cums': np.stack([(same & (k[:, None] <= k[None, :])).astype(np.float32) / 16.0,
                          (same & (k[:, None] >= k[None, :])).astype(np.float32) / 16.0], axis=1),
        'seen': np.stack([np.tile((k[:CHUNK, None] <= k[None, :CHUNK]), (2, 1)),
                          np.tile((k[:CHUNK, None] >= k[None, :CHUNK]), (2, 1))], axis=1).astype(np.int32),
    }


def kernel(**inputs):
    import concourse.bacc as _bacc
    from concourse.bass_utils import run_bass_kernel_spmd as _run

    nc = _bacc.Bacc("TRN2", target_bir_lowering=False, num_devices=1)
    arrays, args = {}, {}
    for name in _INS:
        arrays["in_" + name] = np.ascontiguousarray(inputs[name])
    for name, table in shape_tables().items():
        arrays["const_" + name] = np.ascontiguousarray(table)
    for name, a in arrays.items():
        args[name] = nc.dram_tensor(name, a.shape, mybir.dt.from_np(a.dtype), kind="ExternalInput").ap()
    out = nc.dram_tensor("out", OUT_SHAPE, F32, kind="ExternalOutput").ap()
    program(nc, Dram(nc, args, out))
    r = _run(nc, [arrays], core_ids=[0])
    return r.results[0]["out"]
```

```python
import concourse.bass as bass
from concourse import mybir
import numpy as np
from contextlib import ExitStack

F32 = mybir.dt.float32
F32R = mybir.dt.float32r
I32 = mybir.dt.int32
U32 = mybir.dt.uint32
ACT = mybir.ActivationFunctionType
ALU = mybir.AluOpType
AX = mybir.AxisListType
ds = bass.ds

P = 128
D = 1024
KC = D // P
SEQ, CTX_LEN, GRID_W = 1024, 256, 64
TOK = SEQ + CTX_LEN
TILES = TOK // P
CTX_TILES = CTX_LEN // P
N = 512
EPS = 1e-6
TAPS, PAD = 31, 15
HEADS, DK, DV, CHUNK, RANK = 4, 128, 256, 64, 16
GLA_IN = 2 * HEADS * DK + 2 * HEADS * DV + 2 * RANK
GROUPS, PER_GROUP, EXPERTS, FF, BLK = 4, 8, 32, 512, 128
LAT, CTX = 0, 1
SH1, SC1, G1, SH2, SC2, G2 = range(6)
STREAMS = [(CTX, 0, CTX_TILES // 2, 0), (LAT, CTX_TILES, (TILES - CTX_TILES) // 2, CTX_TILES // 2)]
LAT_STREAMS = [(LAT, CTX_TILES, 1, 0), (LAT, CTX_TILES + 2, (TILES - CTX_TILES) // 2 - 1, 1)]
GAP = PAD + CTX_LEN + PAD
CONV_GROUPS = [(0, CTX_LEN, PAD), (CTX_LEN, N, GAP), (CTX_LEN + N, N, GAP + N)]
CONV_W = GAP + SEQ + PAD
CONV_OUT = GAP + SEQ - PAD
VEC_ROWS = TAPS + 5
V_DWB, V_LNG, V_LNB, V_BA, V_BG = range(TAPS, VEC_ROWS)


class Phase:
    POOL_DMA = ("stored", "h_stored", "o_stored", "gathered")
    pool_dma = []

    def __init__(self, nc, ctx, name):
        self.pool_used = 0
        self.nc, self.ctx, self.name, self.sems = nc, ctx, name, {}

    def sb(self, name, shape, dt=F32):
        return self.ctx.enter_context(self.nc.sbuf_tensor(f"{self.name}_{name}", shape, dt))

    def ps(self, name, shape, dt=F32):
        return self.ctx.enter_context(self.nc.psum_tensor(f"{self.name}_{name}", shape, dt))

    def sem(self, name):
        if name not in self.sems and name.rstrip("01234567") in self.POOL_DMA:
            if self.pool_used == len(self.pool_dma):
                self.pool_dma.append(self.nc.alloc_semaphore(f"pool_dma{self.pool_used}"))
            self.sems[name] = self.pool_dma[self.pool_used]
            self.pool_used += 1
        if name not in self.sems:
            self.sems[name] = self.ctx.enter_context(self.nc.semaphore(f"{self.name}_{name}"))
        return self.sems[name]

    def close(self):
        numbers = sorted(sem.num for sem in self.sems.values())
        with self.nc.Block() as block:
            @block.gpsimd
            def _(pool):
                for sem in self.pool_dma[:self.pool_used]:
                    pool.dma_reset(range(sem.num, sem.num + 1))
                start = numbers[0]
                for at, num in enumerate(numbers):
                    if at + 1 == len(numbers) or numbers[at + 1] != num + 1:
                        pool.sem_clear(range(start, num + 1))
                        start = numbers[min(at + 1, len(numbers) - 1)]


def chain(ph, eng, name):
    done = [0]

    def link(ins):
        done[0] += 1
        ins.then_inc(ph.sem(name), 1)
        eng.wait_ge(ph.sem(name), done[0])
    return link


def product3(pe, out, xh, xl, wh, wl, start, stop):
    pe.matmul(out, xh, wh, start=start, stop=False)
    pe.matmul(out, xh, wl, start=False, stop=False)
    return pe.matmul(out, xl, wh, start=False, stop=stop)


class Split:

    def __init__(self, nc, ctx, name, shape, side="left"):
        self.hi = ctx.enter_context(nc.sbuf_tensor(name + "_hi", shape, F32R, side=side))
        self.lo = ctx.enter_context(nc.sbuf_tensor(name + "_lo", shape, F32R, side=side))


def modulation(nc, d, cs):
    with ExitStack() as ctx:
        ph = Phase(nc, ctx, "ada")
        s = ph.sem
        rows = (SH1, SC1)
        craw = ph.sb("craw", [P, 2, KC])
        w = [ph.sb(f"w{m}", [P, KC, D]) for m in rows]
        row = ph.sb("row", [2, len(rows), D])
        bias = ph.sb("bias", [2, len(rows), D])
        acc = [ph.ps(f"acc{m}", [P, D]) for m in rows]
        xin = [ph.sb(f"xin{b}", [P, D]) for b in range(4)]
        pos_row = [ph.sb(f"pos_row{b}", [P, N]) for b in range(4)]
        pos_col = ph.sb("pos_col", [P, N])
        lat_tiles = TILES - CTX_TILES

        with nc.Block() as block:
            @block.sync
            def _(sp):
                for k, src in enumerate((d.c[0, :], d.c_ctx)):
                    sp.dma_start(craw[:, k, :], src.rearrange("(p k) -> p k", k=KC)).then_inc(s("c_loaded"), 16)
                for m in rows:
                    for h in range(2):
                        cols = slice(h * N, (h + 1) * N)
                        sp.dma_start(w[m][:, :, cols], d.ada_w[0, :, m * D + h * N:m * D + (h + 1) * N]
                                     .rearrange("(p k) n -> p k n", k=KC)).then_inc(s(f"w_loaded{m}{h}"), 16)
                sp.dma_start(bias[:, :, :].rearrange("o m n -> o (m n)"),
                             d.ada_b[0, 0:len(rows) * D].partition_broadcast(2)).then_inc(s("b_loaded"), 16)
                for t in range(lat_tiles):
                    sp.wait_ge(s("x_added"), 2 * (t + 1))
                    sp.dma_start(d.xs[CTX_LEN + t * P:CTX_LEN + (t + 1) * P, :], xin[t % 4][:, :])\
                        .then_inc(s(f"x_stored{t % 4}"), 16)
                sp.wait_ge(s("rows_done"), len(rows))
                for k, stream in enumerate((LAT, CTX)):
                    sp.dma_start(d.mods[0, stream, 0:len(rows), :], row[k:k + 1, :, :]).then_inc(s("mods_stored"), 16)
                sp.wait_ge(s("mods_stored"), 32)
                for b in range(4):
                    sp.wait_ge(s(f"x_stored{b}"), 16 * (lat_tiles // 4))

            @block.scalar
            def _(act):
                act.wait_ge(s("c_loaded"), 32)
                act.activation(cs[:, :, :].rearrange("p k s -> p s k"), craw[:, :, :], ACT.Silu)\
                    .then_inc(s("c_ready"), 1)
                act.dma_start(d.xs[0:CTX_LEN, :], d.ctx[0, :, :]).then_inc(s("ctx_copied"), 16)
                for h in range(P // GRID_W):
                    act.dma_start(pos_col[h * GRID_W:(h + 1) * GRID_W, :], d.pos_col).then_inc(s("col_loaded"), 16)
                for t in range(lat_tiles):
                    b = t % 4
                    if t >= 4:
                        act.wait_ge(s(f"x_stored{b}"), 16 * (t // 4))
                    act.dma_start(xin[b][:, :], d.x[0, t * P:(t + 1) * P, :]).then_inc(s(f"x_loaded{b}"), 16)
                    for h in range(P // GRID_W):
                        r = t * (P // GRID_W) + h
                        act.dma_start(pos_row[b][h * GRID_W:(h + 1) * GRID_W, :],
                                      d.pos_row[r, :].partition_broadcast(GRID_W)).then_inc(s(f"x_loaded{b}"), 16)
                act.wait_ge(s("ctx_copied"), 16)

            @block.tensor
            def _(pe):
                pe.wait_ge(s("c_ready"), 1)
                for m in rows:
                    for h in range(2):
                        pe.wait_ge(s(f"w_loaded{m}{h}"), 16)
                        for k in range(KC):
                            last = pe.matmul(acc[m][0:2, h * N:(h + 1) * N], cs[:, k, :],
                                             w[m][:, k, h * N:(h + 1) * N], start=k == 0, stop=k == KC - 1)
                    last.then_inc(s("acc_ready"), 1)

            @block.vector
            def _(dve):
                dve.wait_ge(s("col_loaded"), 32)
                for t in range(lat_tiles):
                    b = t % 4
                    dve.wait_ge(s(f"x_loaded{b}"), 48 * (t // 4 + 1))
                    for half, table in ((0, pos_row[b]), (1, pos_col)):
                        cols = slice(half * N, (half + 1) * N)
                        dve.tensor_tensor(xin[b][:, cols], xin[b][:, cols], table[:, :], ALU.add)\
                            .then_inc(s("x_added"), 1)
                dve.wait_ge(s("b_loaded"), 16)
                for m in rows:
                    dve.wait_ge(s("acc_ready"), m + 1)
                    dve.tensor_tensor(row[:, m, :], acc[m][0:2, :], bias[:, m, :], ALU.add).then_inc(s("rows_done"), 1)
        ph.close()


def norm_stage(ph, nc, d, layer, which, streams, ht, hd):
    s = ph.sem
    x = [ph.sb(f"x{b}", [P, D]) for b in range(2)]
    h = [ph.sb(f"h{b}", [P, D]) for b in range(2)]
    junk = ph.sb("junk", [P, D])
    stat = ph.sb("stat", [P, 2, 4])
    eps = ph.sb("eps", [P, 1])
    scale = ph.sb("scale", [P, 2, D])
    shift = ph.sb("shift", [P, 2, D])
    gain = ph.sb("gain", [P, D])
    ident = ph.sb("ident", [P, P])
    pt = [ph.ps(f"pt{b}", [P, KC, P]) for b in range(2)]
    sh_row, sc_row = (SH1, SC1) if which == 0 else (SH2, SC2)
    total = sum(pairs for _, _, pairs, _ in streams)

    def sync(sp):
        for st, t0, pairs, before in streams:
            with sp.Fori(0, pairs) as i:
                for b in range(2):
                    row = (i * 2 + (t0 + b)) * P
                    if before:
                        sp.wait_ge(s(f"scaled{b}"), i + before)
                    sp.dma_start(x[b][:, :], d.xs[ds(row, P), :]).then_inc(s(f"x_loaded{b}"), 16)

    def pool(pl):
        if hd is None:
            return
        for st, t0, pairs, before in streams:
            with pl.Fori(0, pairs) as i:
                for b in range(2):
                    row = (i * 2 + (t0 + b)) * P
                    pl.wait_ge(s(f"h_ready{b}"), i + (before + 1))
                    pl.dma_start(hd[ds(row, P), :], h[b][:, :]).then_inc(s(f"h_stored{b}"), 16)
        for b in range(2):
            pl.wait_ge(s(f"h_stored{b}"), 16 * sum(p for _, _, p, _ in streams))

    def scalar(act):
        for st in (LAT, CTX):
            act.dma_start(scale[:, st, :], d.mods[layer, st, sc_row, :].partition_broadcast(P)).then_inc(s("tables"), 16)
            act.dma_start(shift[:, st, :], d.mods[layer, st, sh_row, :].partition_broadcast(P)).then_inc(s("tables"), 16)
        act.dma_start(gain[:, :], d.norm_g[layer, which, :].partition_broadcast(P)).then_inc(s("tables"), 16)
        act.dma_start(ident[:, :], d.ident).then_inc(s("tables"), 16)
        act.preload_act_table(ACT.Sqrt)
        act.wait_ge(s("eps_set"), 1)

        def root(b, n):
            act.wait_ge(s(f"x_loaded{b}"), n * 16)
            act.activation(junk[:, :], x[b][:, :], ACT.Square, accum_out=stat[:, b, 0:1])\
                .then_inc(s(f"squares{b}"), 1)
            act.wait_ge(s(f"squares{b}"), n)
            act.activation(stat[:, b, 1:2], stat[:, b, 0:1], ACT.Sqrt, bias=eps[:, :], scale=1.0 / D)\
                .then_inc(s(f"root{b}"), 1)

        def high(b, n, tile):
            act.wait_ge(s(f"t_ready{b}"), n)
            act.activation(ht.hi[:, :, ds(tile * P, P)], pt[b][:, :, :], ACT.Copy).then_inc(s(f"ht_hi{b}"), 1)

        for st, t0, pairs, before in streams:
            with act.Fori(0, pairs) as i:
                n, tile = i + (before + 1), i * 2 + t0
                root(0, n)
                if before:
                    high(1, n - 1, tile - 1)
                root(1, n)
                high(0, n, tile)
        high(1, total, TILES - 1)

    def vector(dve):
        dve.memset(eps[:, :], EPS).then_inc(s("eps_set"), 1)
        dve.wait_ge(s("tables"), 96)
        for st in (LAT, CTX):
            dve.scalar_tensor_tensor(scale[:, st, :], scale[:, st, :], 1.0, gain[:, :], ALU.add, ALU.mult)\
                .then_inc(s("scale_ready"), 1)
        dve.wait_ge(s("scale_ready"), 2)

        def norm(b, n, st, before):
            dve.wait_ge(s(f"root{b}"), n)
            dve.reciprocal(stat[:, b, 2:3], stat[:, b, 1:2]).then_inc(s(f"rstd{b}"), 1)
            dve.wait_ge(s(f"rstd{b}"), n)
            if before:
                dve.wait_ge(s(f"t_ready{b}"), n - 1)
                if hd is not None:
                    dve.wait_ge(s(f"h_stored{b}"), (n - 1) * 16)
            dve.scalar_tensor_tensor(h[b][:, :], x[b][:, :], stat[:, b, 2:3], scale[:, st, :],
                                     ALU.mult, ALU.mult).then_inc(s(f"scaled{b}"), 1)
            dve.wait_ge(s(f"scaled{b}"), n)
            dve.tensor_tensor(h[b][:, :], h[b][:, :], shift[:, st, :], ALU.add).then_inc(s(f"h_ready{b}"), 1)

        def low(b, n, tile):
            dve.wait_ge(s(f"ht_hi{b}"), n)
            dve.tensor_tensor(ht.lo[:, :, ds(tile * P, P)], pt[b][:, :, :],
                              ht.hi[:, :, ds(tile * P, P)].bitcast(F32), ALU.subtract).then_inc(s(f"ht_lo{b}"), 1)

        for st, t0, pairs, before in streams:
            with dve.Fori(0, pairs) as i:
                n, tile = i + (before + 1), i * 2 + t0
                norm(0, n, st, before)
                if before:
                    low(1, n - 1, tile - 1)
                norm(1, n, st, before)
                low(0, n, tile)
        low(1, total, TILES - 1)

    def tensor(pe):
        pe.wait_ge(s("tables"), 96)
        for st, t0, pairs, before in streams:
            with pe.Fori(0, pairs) as i:
                n = i + (before + 1)
                for b in range(2):
                    pe.wait_ge(s(f"h_ready{b}"), n)
                    if before:
                        pe.wait_ge(s(f"ht_lo{b}"), n - 1)
                    for k in range(KC):
                        last = pe.transpose(pt[b][:, k, :], h[b][:, k * P:(k + 1) * P], ident[:, :])
                    last.then_inc(s(f"t_ready{b}"), 1)

    return sync, pool, scalar, vector, tensor


def normalise(nc, d, layer, which, streams, ht, hd=None):
    with ExitStack() as ctx:
        ph = Phase(nc, ctx, f"norm{layer}{which}")
        sync, pool, scalar, vector, tensor = norm_stage(ph, nc, d, layer, which, streams, ht, hd)
        with nc.Block() as block:
            block.sync(sync)
            block.gpsimd(pool)
            block.scalar(scalar)
            block.vector(vector)
            block.tensor(tensor)
        ph.close()


ADA_UNITS = [(0, 0, 2, 0, 2 * D), (0, 0, 2, 1, 2 * D), (0, 1, 3, 0, 0), (1, 1, 3, 1, 0), (1, 1, 3, 2, 0)]


def conv_taps(nc, d, ht, vt, vecs, cs):
    with ExitStack() as ctx:
        ph = Phase(nc, ctx, "taps")
        s = ph.sem
        raw = [ph.sb(f"raw{b}", [P, KC, 2, P]) for b in range(2)]
        w = Split(nc, ctx, "taps_w", [P, KC, 2, P])
        ada_w = [ph.sb(f"ada_w{h}", [P, KC // 2, N]) for h in range(2)]
        ada_b = ph.sb("ada_b", [2, N])
        ada_sum = ph.sb("ada_sum", [2, N])
        ada_row = ph.sb("ada_row", [2, N])
        ada_acc = ph.ps("ada_acc", [P, N])
        rows = ph.sb("rows", [VEC_ROWS, D])
        ident = ph.sb("ident", [P, P])
        vec = [ph.sb(f"vec{b}", [P, VEC_ROWS]) for b in range(2)]
        sg = [ph.sb(f"sg{g}", [P, N]) for g in range(3)]
        u = [ph.sb(f"u{b}", [P, CONV_W]) for b in range(2)]
        acc = [ph.sb(f"acc{b}", [P, CONV_OUT]) for b in range(2)]
        za = [ph.ps(f"za{g}", [P, N]) for g in range(3)]
        zg = [ph.ps(f"zg{g}", [P, N]) for g in range(3)]
        pv = ph.ps("pv", [P, KC, VEC_ROWS])
        pairs = KC // 2

        with nc.Block() as block:
            @block.sync
            def _(sp):
                sp.dma_start(ident[:, :], d.ident).then_inc(s("rows_loaded"), 16)
                for r0, src in ((0, d.dw_w), (V_DWB, d.dw_b), (V_LNG, d.ln_g), (V_LNB, d.ln_b)):
                    n = src.shape[0]
                    sp.dma_start(rows[r0:r0 + n, :], src).then_inc(s("rows_loaded"), 16)
                sp.dma_start(rows[V_BA:V_BG + 1, :], d.pw1_b.rearrange("o (h n) -> (o h) n", h=2))\
                    .then_inc(s("rows_loaded"), 16)

                def load(b, i):
                    for h in range(2):
                        src = d.pw1_w[:, ds((i * 2 + b) * P + h * D, P)].rearrange("(k p) n -> p k n", p=P)
                        sp.dma_start(raw[b][:, :, h, :], src).then_inc(s(f"w_loaded{b}"), 16)

                def load_unit(j, i, first):
                    _, l, per, at, c0 = ADA_UNITS[j]
                    u = i * len(ADA_UNITS) + j
                    col = (i * per + at) * N + c0
                    for h in range(2):
                        if not (first and j == 0):
                            sp.wait_ge(s(f"ada_used{h}"), u)
                        half = slice(h * (KC // 2), (h + 1) * (KC // 2))
                        sp.dma_start(ada_w[h][:, :, :], d.ada_w[l, :, ds(col, N)]
                                     .rearrange("(p k) n -> p k n", k=KC)[:, half, :]).then_inc(s(f"ada_loaded{h}"), 16)
                    if not (first and j == 0):
                        sp.wait_ge(s("ada_out"), u)
                    sp.dma_start(ada_b[:, :], d.ada_b[l, ds(col, N)].partition_broadcast(2))\
                        .then_inc(s("ada_b_loaded"), 16)

                def pair(i, first, last):
                    for b in range(2):
                        for j, unit in enumerate(ADA_UNITS):
                            if unit[0] == b:
                                load_unit(j, i, first)
                        if not last:
                            sp.wait_ge(s(f"w_lo{b}"), i + 1)
                            load(b, i + 1)

                for b in range(2):
                    load(b, 0)
                pair(0, True, False)
                with sp.Fori(1, pairs - 1) as i:
                    pair(i, False, False)
                pair(pairs - 1, False, True)

            @block.gpsimd
            def _(pool):
                for b in range(2):
                    pool.memset(u[b][:, :], 0.0).then_inc(s("u_zero"), 1)

                def low(b, i):
                    pool.wait_ge(s(f"w_hi{b}"), i + 1)
                    pool.tensor_tensor(w.lo[:, :, :, :], raw[b][:, :, :, :], w.hi[:, :, :, :].bitcast(F32),
                                       ALU.subtract).then_inc(s(f"w_lo{b}"), 1)

                def units_out(b, i, first):
                    for j, (when, l, per, at, c0) in enumerate(ADA_UNITS):
                        if when != b:
                            continue
                        u = i * len(ADA_UNITS) + j
                        pool.wait_ge(s("ada_b_loaded"), (u + 1) * 16)
                        pool.wait_ge(s("ada_taken"), u + 1)
                        if not (first and j == 0):
                            pool.wait_ge(s("stored"), u * 16)
                        pool.tensor_tensor(ada_row[:, :], ada_sum[:, :], ada_b[:, :], ALU.add)\
                            .then_inc(s("ada_out"), 1)
                        pool.wait_ge(s("ada_out"), u + 1)
                        pool.dma_start(d.mods[l].rearrange("s m n -> s (m n)")[:, ds((i * per + at) * N + c0, N)],
                                       ada_row[:, :]).then_inc(s("stored"), 16)

                low(0, 0)
                low(1, 0)
                units_out(0, 0, True)
                with pool.Fori(1, pairs) as i:
                    low(0, i)
                    units_out(1, i - 1, False)
                    low(1, i)
                    units_out(0, i, False)
                units_out(1, pairs - 1, False)
                pool.wait_ge(s("stored"), 16 * pairs * len(ADA_UNITS))

            @block.tensor
            def _(pe):
                pe.wait_ge(s("rows_loaded"), 96)
                for k in range(KC):
                    last = pe.transpose(pv[:, k, :], rows[:, k * P:(k + 1) * P], ident[0:VEC_ROWS, 0:VEC_ROWS])
                last.then_inc(s("pv_ready"), 1)

                def chunk(b, i, first):
                    pe.wait_ge(s(f"w_lo{b}"), i + 1)
                    for g, (t0, n, _) in enumerate(CONV_GROUPS):
                        if not (first and b == 0):
                            pe.wait_ge(s(f"u_ready{g}{1 - b}"), i + b)
                        for h, z in ((1, zg[g]), (0, za[g])):
                            for k in range(KC):
                                last = product3(pe, z[:, 0:n], w.hi[:, k, h, :], w.lo[:, k, h, :],
                                                ht.hi[:, k, t0:t0 + n], ht.lo[:, k, t0:t0 + n], k == 0, k == KC - 1)
                        last.then_inc(s(f"z_ready{g}{b}"), 1)

                def units(b, i, first):
                    for j, unit in enumerate(ADA_UNITS):
                        if unit[0] != b:
                            continue
                        u = i * len(ADA_UNITS) + j
                        if not (first and j == 0):
                            pe.wait_ge(s("ada_taken"), u)
                        for h in range(2):
                            pe.wait_ge(s(f"ada_loaded{h}"), (u + 1) * 16)
                            for k in range(KC // 2):
                                last = pe.matmul(ada_acc[0:2, :], cs[:, h * (KC // 2) + k, :], ada_w[h][:, k, :],
                                                 start=h == 0 and k == 0, stop=h == 1 and k == KC // 2 - 1)
                            last.then_inc(s(f"ada_used{h}"), 1)

                for b in range(2):
                    chunk(b, 0, True)
                    units(b, 0, True)
                with pe.Fori(1, pairs) as i:
                    for b in range(2):
                        chunk(b, i, False)
                        units(b, i, False)

            @block.scalar
            def _(act):
                act.preload_act_table(ACT.Sigmoid)

                def high(b, i, first):
                    act.wait_ge(s(f"w_loaded{b}"), i * 32 + 32)
                    if not (first and b == 0):
                        act.wait_ge(s(f"z_ready2{1 - b}"), i + b)
                    act.activation(w.hi[:, :, :, :], raw[b][:, :, :, :], ACT.Copy).then_inc(s(f"w_hi{b}"), 1)

                def take_units(b, i, first):
                    for j, unit in enumerate(ADA_UNITS):
                        if unit[0] != b:
                            continue
                        u = i * len(ADA_UNITS) + j
                        act.wait_ge(s("ada_used1"), u + 1)
                        if not (first and j == 0):
                            act.wait_ge(s("ada_out"), u)
                        act.activation(ada_sum[:, :], ada_acc[0:2, :], ACT.Copy).then_inc(s("ada_taken"), 1)

                def chunk(b, i, first):
                    act.wait_ge(s(f"vec_ready{b}"), i + 1)
                    for g, (t0, n, _) in enumerate(CONV_GROUPS):
                        act.wait_ge(s(f"z_ready{g}{b}"), i + 1)
                        if not (first and b == 0):
                            act.wait_ge(s(f"u_ready{g}{1 - b}"), i + b)
                        act.activation(sg[g][:, 0:n], zg[g][:, 0:n], ACT.Sigmoid, bias=vec[b][:, V_BG:V_BG + 1])\
                            .then_inc(s(f"sig_ready{g}{b}"), 1)

                high(0, 0, True)
                chunk(0, 0, True)
                high(1, 0, True)
                take_units(0, 0, True)
                chunk(1, 0, True)
                with act.Fori(1, pairs) as i:
                    high(0, i, False)
                    take_units(1, i - 1, False)
                    chunk(0, i, False)
                    high(1, i, False)
                    take_units(0, i, False)
                    chunk(1, i, False)
                take_units(1, pairs - 1, False)

            @block.vector
            def _(dve):
                dve.wait_ge(s("pv_ready"), 1)
                dve.tensor_copy(vecs[:, :, :], pv[:, :, :]).then_inc(s("vecs_ready"), 1)
                dve.wait_ge(s("vecs_ready"), 1)
                dve.wait_ge(s("u_zero"), 2)

                def chunk(b, i):
                    n = i + 1
                    dve.tensor_copy(vec[b][:, :], vecs[:, ds(i * 2 + b, 1), :].rearrange("p o v -> p (o v)"))\
                        .then_inc(s(f"vec_ready{b}"), 1)
                    dve.wait_ge(s(f"vec_ready{b}"), n)
                    for g, (t0, m, c0) in enumerate(CONV_GROUPS):
                        dve.wait_ge(s(f"sig_ready{g}{b}"), n)
                        dve.scalar_tensor_tensor(u[b][:, c0:c0 + m], za[g][:, 0:m], vec[b][:, V_BA:V_BA + 1],
                                                 sg[g][:, 0:m], ALU.add, ALU.mult).then_inc(s(f"u_ready{g}{b}"), 1)
                        dve.wait_ge(s(f"u_ready{g}{b}"), n)
                    dve.tensor_scalar(acc[0][:, :], u[b][:, 0:CONV_OUT], vec[b][:, 0:1], vec[b][:, V_DWB:V_DWB + 1],
                                      ALU.mult, ALU.add).then_inc(s(f"tap0{b}"), 1)
                    dve.tensor_scalar(acc[1][:, :], u[b][:, 1:1 + CONV_OUT], vec[b][:, 1:2], None, ALU.mult)\
                        .then_inc(s(f"tap1{b}"), 1)
                    for k in range(2, TAPS):
                        q = k % 2
                        dve.wait_ge(s(f"tap{q}{b}"), i * len(range(q, TAPS, 2)) + k // 2)
                        dve.scalar_tensor_tensor(acc[q][:, :], u[b][:, k:k + CONV_OUT], vec[b][:, k:k + 1],
                                                 acc[q][:, :], ALU.mult, ALU.add).then_inc(s(f"tap{q}{b}"), 1)
                    for q in range(2):
                        dve.wait_ge(s(f"tap{q}{b}"), n * len(range(q, TAPS, 2)))
                    dve.tensor_tensor(vt[:, ds(i * 2 + b, 1), :].rearrange("p o n -> p (o n)"), acc[0][:, :],
                                      acc[1][:, :], ALU.add).then_inc(s("taps_summed"), 1)

                for b in range(2):
                    chunk(b, 0)
                with dve.Fori(1, pairs) as i:
                    for b in range(2):
                        chunk(b, i)
                dve.wait_ge(s("taps_summed"), KC)
        ph.close()


AHEAD = [(CTX, 0, 1, 0, None), (LAT, CTX_TILES, 1, 1, CTX), (LAT, CTX_TILES + 2, TILES // 2 - 2, 2, LAT)]


def conv_out(nc, d, vt, vecs):
    with ExitStack() as ctx:
        ph = Phase(nc, ctx, "pw2")
        s = ph.sem
        raw = ph.sb("raw", [P, 2, D])
        w = Split(nc, ctx, "pw2_w", [P, KC, D])
        mean_w = ph.sb("mean_w", [P, P])
        bias = ph.sb("bias", [P, D])
        gate = ph.sb("gate", [P, 2, D])
        eps = ph.sb("eps", [P, 1])
        dev = [ph.sb(f"dev{b}", [P, KC, P]) for b in range(2)]
        sq = [ph.sb(f"sq{b}", [P, KC, P]) for b in range(2)]
        root = ph.sb("root", [P, 2, P])
        rstd = ph.sb("rstd", [P, 2, P])
        act_t = [Split(nc, ctx, f"pw2_act{b}", [P, KC, P]) for b in range(2)]
        x = [ph.sb(f"x{b}", [P, D]) for b in range(2)]
        y = [ph.sb(f"y{b}", [P, D]) for b in range(2)]
        mean = [ph.ps(f"mean{b}", [P, N]) for b in range(2)]
        var = [ph.ps(f"var{b}", [P, N]) for b in range(2)]
        py = [ph.ps(f"py{b}", [P, D]) for b in range(2)]

        def vcol(i, b, t0):
            return (i * 2 + (t0 + b)) * P + (0 if t0 < CTX_TILES else GAP - PAD - CTX_LEN)

        with nc.Block() as block:
            @block.sync
            def _(sp):
                sp.dma_start(mean_w[:, :], d.mean_w).then_inc(s("tables"), 16)
                sp.dma_start(bias[:, :], d.pw2_b[0, :].partition_broadcast(P)).then_inc(s("tables"), 16)
                for st in (LAT, CTX):
                    sp.dma_start(gate[:, st, :], d.mods[0, st, G1, :].partition_broadcast(P)).then_inc(s("tables"), 16)
                for k in range(KC):
                    if k >= 2:
                        sp.wait_ge(s("w_lo"), k - 1)
                    sp.dma_start(raw[:, k % 2, :], d.pw2_w[k * P:(k + 1) * P, :]).then_inc(s(f"w_loaded{k % 2}"), 16)
                for st, t0, pairs, before in STREAMS:
                    with sp.Fori(0, pairs) as i:
                        for b in range(2):
                            if before:
                                sp.wait_ge(s(f"stored{b}"), (i + before) * 16)
                            sp.dma_start(x[b][:, :], d.xs[ds((i * 2 + (t0 + b)) * P, P), :])\
                                .then_inc(s(f"x_loaded{b}"), 16)

            @block.gpsimd
            def _(pool):
                for k in range(KC):
                    pool.wait_ge(s("w_hi"), k + 1)
                    pool.tensor_tensor(w.lo[:, k, :], raw[:, k % 2, :], w.hi[:, k, :].bitcast(F32), ALU.subtract)\
                        .then_inc(s("w_lo"), 1)
                for st, t0, pairs, before in STREAMS:
                    with pool.Fori(0, pairs) as i:
                        for b in range(2):
                            pool.wait_ge(s(f"x_ready{b}"), i + (before + 1))
                            pool.dma_start(d.xs[ds((i * 2 + (t0 + b)) * P, P), :], x[b][:, :])\
                                .then_inc(s(f"stored{b}"), 16)
                for b in range(2):
                    pool.wait_ge(s(f"stored{b}"), 16 * (TILES // 2))

            @block.tensor
            def _(pe):
                def average(what, b, i, t0):
                    for k in range(KC):
                        if what == "mean":
                            out, src = mean[b], vt[:, k, ds(vcol(i, b, t0), P)]
                        else:
                            out, src = var[b], sq[b][:, k, :]
                        last = pe.matmul(out[:, 0:P], mean_w[:, :], src, start=k == 0, stop=k == KC - 1)
                    last.then_inc(s(f"{what}_ready{b}"), 1)

                def product(b, n, before):
                    pe.wait_ge(s(f"act_lo{b}"), n)
                    if before:
                        pe.wait_ge(s(f"biased{b}"), n - 1)
                    for h in range(2):
                        for k in range(KC):
                            cols = slice(h * N, (h + 1) * N)
                            last = product3(pe, py[b][:, cols], act_t[b].hi[:, k, :], act_t[b].lo[:, k, :],
                                            w.hi[:, k, cols], w.lo[:, k, cols], k == 0, k == KC - 1)
                    last.then_inc(s(f"y_ready{b}"), 1)

                pe.wait_ge(s("tables"), 64)
                for st, t0, pairs, before, prev in AHEAD:
                    with pe.Fori(0, pairs) as i:
                        n = i + (before + 1)
                        for b in range(2):
                            if before:
                                pe.wait_ge(s(f"dev_ready{b}"), n - 1)
                            average("mean", b, i, t0)
                        if before == 1:
                            pe.wait_ge(s("w_lo"), KC)
                        if before:
                            product(0, n - 1, before - 1)
                        for b in range(2):
                            pe.wait_ge(s(f"sq_ready{b}"), n)
                            if before:
                                pe.wait_ge(s(f"root_ready{b}"), n - 1)
                            average("var", b, i, t0)
                        if before:
                            product(1, n - 1, before - 1)
                for b in range(2):
                    product(b, TILES // 2, 1)

            @block.scalar
            def _(act):
                for k in range(KC):
                    act.wait_ge(s(f"w_loaded{k % 2}"), 16 * (k // 2 + 1))
                    act.activation(w.hi[:, k, :], raw[:, k % 2, :], ACT.Copy).then_inc(s("w_hi"), 1)
                act.wait_ge(s("eps_set"), 1)
                for st, t0, pairs, before, prev in AHEAD:
                    with act.Fori(0, pairs) as i:
                        n = i + (before + 1)
                        for b in range(2):
                            act.wait_ge(s(f"dev_ready{b}"), n)
                            if before:
                                act.wait_ge(s(f"act_lo{b}"), n - 1)
                            act.activation(sq[b][:, :, :], dev[b][:, :, :], ACT.Square).then_inc(s(f"sq_ready{b}"), 1)
                        for b in range(2):
                            act.wait_ge(s(f"var_ready{b}"), n)
                            if before:
                                act.wait_ge(s(f"rstd_ready{b}"), n - 1)
                            act.activation(root[:, b, :], var[b][:, 0:P], ACT.Sqrt, bias=eps[:, :])\
                                .then_inc(s(f"root_ready{b}"), 1)
                        for b in range(2):
                            act.wait_ge(s(f"scaled{b}"), n)
                            for k in range(KC):
                                last = act.activation(sq[b][:, k, :], dev[b][:, k, :], ACT.Silu,
                                                      scale=vecs[:, k, V_LNG:V_LNG + 1],
                                                      bias=vecs[:, k, V_LNB:V_LNB + 1])
                            last.then_inc(s(f"act_ready{b}"), 1)
                        for b in range(2):
                            act.wait_ge(s(f"act_ready{b}"), n)
                            if before:
                                act.wait_ge(s(f"y_ready{b}"), n - 1)
                            act.activation(act_t[b].hi[:, :, :], sq[b][:, :, :], ACT.Copy).then_inc(s(f"act_hi{b}"), 1)

            @block.vector
            def _(dve):
                def low(b, n):
                    dve.wait_ge(s(f"act_hi{b}"), n)
                    dve.tensor_tensor(act_t[b].lo[:, :, :], sq[b][:, :, :], act_t[b].hi[:, :, :].bitcast(F32),
                                      ALU.subtract).then_inc(s(f"act_lo{b}"), 1)

                def add(b, n, st):
                    dve.wait_ge(s(f"y_ready{b}"), n)
                    dve.tensor_tensor(y[b][:, :], py[b][:, :], bias[:, :], ALU.add).then_inc(s(f"biased{b}"), 1)
                    dve.wait_ge(s(f"biased{b}"), n)
                    dve.tensor_tensor(y[b][:, :], y[b][:, :], gate[:, st, :], ALU.mult).then_inc(s(f"gated{b}"), 1)
                    dve.wait_ge(s(f"gated{b}"), n)
                    dve.wait_ge(s(f"x_loaded{b}"), n * 16)
                    dve.tensor_tensor(x[b][:, :], x[b][:, :], y[b][:, :], ALU.add).then_inc(s(f"x_ready{b}"), 1)

                dve.memset(eps[:, :], EPS).then_inc(s("eps_set"), 1)
                dve.wait_ge(s("tables"), 64)
                for st, t0, pairs, before, prev in AHEAD:
                    with dve.Fori(0, pairs) as i:
                        n = i + (before + 1)
                        for b in range(2):
                            dve.wait_ge(s(f"mean_ready{b}"), n)
                            if before:
                                dve.wait_ge(s(f"act_ready{b}"), n - 1)
                            dve.tensor_tensor(dev[b][:, :, :], vt[:, :, ds(vcol(i, b, t0), P)],
                                              mean[b][:, 0:P].unsqueeze(1).to_broadcast([P, KC, P]), ALU.subtract)\
                                .then_inc(s(f"dev_ready{b}"), 1)
                        if before:
                            add(0, n - 1, prev)
                        for b in range(2):
                            dve.wait_ge(s(f"root_ready{b}"), n)
                            dve.reciprocal(rstd[:, b, :], root[:, b, :]).then_inc(s(f"rstd_ready{b}"), 1)
                            dve.wait_ge(s(f"rstd_ready{b}"), n)
                            dve.tensor_tensor(dev[b][:, :, :], dev[b][:, :, :],
                                              rstd[:, b:b + 1, :].to_broadcast([P, KC, P]), ALU.mult)\
                                .then_inc(s(f"scaled{b}"), 1)
                        low(0, n)
                        if before:
                            add(1, n - 1, prev)
                        low(1, n)
                for b in range(2):
                    add(b, TILES // 2, LAT)
        ph.close()


def route(nc, d, layer, streams, ht, plan):
    t0 = streams[0][1]
    nt = TILES - t0
    nb = plan.blocks
    width = GROUPS + EXPERTS
    with ExitStack() as ctx:
        ph = Phase(nc, ctx, f"route{layer}")
        s = ph.sem
        raw = ph.sb("raw", [P, KC, width])
        w = Split(nc, ctx, f"route{layer}_w", [P, KC, width])
        bias = ph.sb("bias", [width, 1])
        ident = ph.sb("ident", [P, P])
        before = ph.sb("before", [P, P])
        ones = ph.sb("ones", [P, P])
        iota = ph.sb("iota", [P, P])
        token = ph.sb("token", [P, TILES])
        lt = ph.sb("lt", [width, TOK])
        lg = ph.sb("lg", [P, nt, width])
        gm = ph.sb("gm", [P, nt])
        ga = ph.sb("ga", [P, nt, GROUPS])
        gsel = ph.sb("gsel", [P, nt, GROUPS])
        gw = ph.sb("gw", [P, nt])
        inner = [ph.sb(f"inner{j}", [P, nt, EXPERTS]) for j in range(2)]
        cand = ph.sb("cand", [P, nt, EXPERTS])
        least = ph.sb("least", [P, nt])
        top = ph.sb("top", [P, 2, nt])
        hot = ph.sb("hot", [P, 2, nt, EXPERTS])
        both = ph.sb("both", [P, nt, EXPERTS])
        sofar = ph.sb("sofar", [P, nt + 1, EXPERTS])
        rank = ph.sb("rank", [P, nt, EXPERTS])
        picked = ph.sb("picked", [P, 2, nt, EXPERTS])
        mine = ph.sb("mine", [P, 2, nt])
        first = ph.sb("first", [P, 2, nt])
        over = ph.sb("over", [P, 2, nt])
        steps = ph.sb("steps", [P, nt])
        more = ph.sb("more", [P, 2 * nt * nt + EXPERTS * nt])
        need = ph.sb("need", [P, EXPERTS])
        ends = [ph.sb(f"ends{j}", [P, EXPERTS]) for j in range(2)]
        passed = ph.sb("passed", [1, nb, EXPERTS])
        blk = ph.sb("blk", [1, nb + 2])
        fresh = ph.sb("fresh", [1, nb])
        in_slot = ph.sb("in_slot", [P, 2 * nt, P])
        in_blk = ph.sb("in_blk", [P, 2 * nt, nb + 1])
        pl = [ph.ps(f"pl{g}", [P, N]) for g in range(3)]
        pt = ph.ps("pt", [P, nt, width])
        pr = ph.ps("pr", [P, nt * EXPERTS])
        pa = ph.ps("pa", [P, nt * EXPERTS])
        pi = ph.ps("pi", [P, nb + 1])
        groups = [(a, min(N, TOK - a)) for a in range(t0 * P, TOK, N)]

        with nc.Block() as block:
            @block.sync
            def _(sp):
                for dst, src in ((raw[:, :, 0:GROUPS], d.wg[layer].rearrange("(k p) n -> p k n", p=P)),
                                 (raw[:, :, GROUPS:width], d.wr[layer].rearrange("(k p) n -> p k n", p=P)),
                                 (bias[0:GROUPS, :], d.bg[layer, :].unsqueeze(1)),
                                 (bias[GROUPS:width, :], d.br[layer, :].unsqueeze(1)),
                                 (ident[:, :], d.ident), (before[:, :], d.before), (ones[:, :], d.ones),
                                 (iota[:, :], d.iota), (token[:, :], d.token)):
                    sp.dma_start(dst, src).then_inc(s("loaded"), 16)

            @block.tensor
            def _(pe):
                pe.wait_ge(s("loaded"), 144)
                pe.wait_ge(s("w_lo"), 1)
                for g, (a, n) in enumerate(groups):
                    for k in range(KC):
                        last = product3(pe, pl[g][0:width, 0:n], w.hi[:, k, :], w.lo[:, k, :],
                                        ht.hi[:, k, a:a + n], ht.lo[:, k, a:a + n], k == 0, k == KC - 1)
                    last.then_inc(s("logits"), 1)
                pe.wait_ge(s("biased"), len(groups))
                for t in range(nt):
                    last = pe.transpose(pt[:, t, :], lt[:, (t0 + t) * P:(t0 + t + 1) * P], ident[0:width, 0:width])
                last.then_inc(s("turned"), 1)
                pe.wait_ge(s("chosen"), 1)
                pe.matmul(pr[:, :], before[:, :], both[:, :, :].rearrange("p t e -> p (t e)"), start=True, stop=True)
                pe.matmul(pa[:, :], ones[:, :], both[:, :, :].rearrange("p t e -> p (t e)"), start=True, stop=True)\
                    .then_inc(s("counted"), 1)
                pe.wait_ge(s("hot_slots"), 4 * nt)
                for j in range(2 * nt):
                    last = pe.matmul(pi[:, :], in_slot[:, j, :], in_blk[:, j, :], start=j == 0, stop=j == 2 * nt - 1)
                last.then_inc(s("slots_done"), 1)

            @block.scalar
            def _(act):
                act.preload_act_table(ACT.Exp)
                act.wait_ge(s("loaded"), 144)
                act.activation(w.hi[:, :, :], raw[:, :, :], ACT.Copy).then_inc(s("w_hi"), 1)
                for g, (a, n) in enumerate(groups):
                    act.wait_ge(s("logits"), g + 1)
                    act.activation(lt[:, a:a + n], pl[g][0:width, 0:n], ACT.Identity, bias=bias[:, :])\
                        .then_inc(s("biased"), 1)
                act.wait_ge(s("group_shifted"), 1)
                act.activation(ga[:, :, :], ga[:, :, :], ACT.Exp).then_inc(s("group_exp"), 1)
                act.wait_ge(s("top_gap"), 1)
                act.activation(top[:, 1, :], top[:, 1, :], ACT.Exp).then_inc(s("top_exp"), 1)

            @block.vector
            def _(dve):
                link = chain(ph, dve, "step")

                def over_rows(ap, n):
                    return ap.unsqueeze(2).to_broadcast([P, nt, n])

                def along(n):
                    return iota[:, 0:n].unsqueeze(1).to_broadcast([P, nt, n])

                def first_max(values, n, biggest, hot_out):
                    link(dve.tensor_reduce(biggest, values, AX.X, ALU.max))
                    link(dve.tensor_tensor(cand[:, :, 0:n], values, over_rows(biggest, n), ALU.is_equal))
                    link(dve.scalar_tensor_tensor(cand[:, :, 0:n], cand[:, :, 0:n], -100.0, along(n), ALU.mult, ALU.add))
                    link(dve.tensor_reduce(least[:, :], cand[:, :, 0:n], AX.X, ALU.min))
                    link(dve.tensor_tensor(hot_out, cand[:, :, 0:n], over_rows(least[:, :], n), ALU.is_equal))

                dve.wait_ge(s("w_hi"), 1)
                dve.tensor_tensor(w.lo[:, :, :], raw[:, :, :], w.hi[:, :, :].bitcast(F32), ALU.subtract)\
                    .then_inc(s("w_lo"), 1)
                dve.wait_ge(s("turned"), 1)
                link(dve.tensor_copy(lg[:, :, :], pt[:, :, :]))
                first_max(lg[:, :, 0:GROUPS], GROUPS, gm[:, :], gsel[:, :, :])
                dve.tensor_tensor(ga[:, :, :], lg[:, :, 0:GROUPS], over_rows(gm[:, :], GROUPS), ALU.subtract)\
                    .then_inc(s("group_shifted"), 1)
                def by_group(ap):
                    return ap.rearrange("p t (g e) -> p t g e", g=GROUPS)
                sel = gsel[:, :, :].unsqueeze(3).to_broadcast([P, nt, GROUPS, PER_GROUP])
                link(dve.tensor_tensor(by_group(inner[0][:, :, :]), by_group(lg[:, :, GROUPS:width]), sel, ALU.mult))
                link(dve.tensor_scalar(gsel[:, :, :], gsel[:, :, :], 1.0, 1e30, ALU.subtract, ALU.mult))
                link(dve.tensor_tensor(by_group(inner[0][:, :, :]), by_group(inner[0][:, :, :]), sel, ALU.add))
                first_max(inner[0][:, :, :], EXPERTS, top[:, 0, :], hot[:, 0, :, :])
                link(dve.scalar_tensor_tensor(inner[1][:, :, :], hot[:, 0, :, :], -2e30, inner[0][:, :, :],
                                              ALU.mult, ALU.add))
                first_max(inner[1][:, :, :], EXPERTS, top[:, 1, :], hot[:, 1, :, :])
                dve.tensor_tensor(both[:, :, :], hot[:, 0, :, :], hot[:, 1, :, :], ALU.add).then_inc(s("chosen"), 1)
                dve.tensor_tensor(top[:, 1, :], top[:, 1, :], top[:, 0, :], ALU.subtract).then_inc(s("top_gap"), 1)
                dve.wait_ge(s("group_exp"), 1)
                link(dve.tensor_reduce(gw[:, :], ga[:, :, :], AX.X, ALU.add))
                link(dve.reciprocal(gw[:, :], gw[:, :]))
                dve.wait_ge(s("top_exp"), 1)
                link(dve.tensor_scalar(top[:, 0, :], top[:, 1, :], 1.0, None, ALU.add))
                link(dve.reciprocal(top[:, 0, :], top[:, 0, :]))
                link(dve.tensor_tensor(plan.weight[:, 0, :], top[:, 0, :], gw[:, :], ALU.mult))
                link(dve.tensor_tensor(plan.weight[:, 1, :], plan.weight[:, 0, :], top[:, 1, :], ALU.mult))
                dve.wait_ge(s("counted"), 1)
                link(dve.memset(sofar[:, 0, :], 0.0))
                for t in range(nt):
                    link(dve.tensor_tensor(sofar[:, t + 1, :], sofar[:, t, :], pa[:, t * EXPERTS:(t + 1) * EXPERTS],
                                           ALU.add))
                link(dve.tensor_tensor(rank[:, :, :].rearrange("p t e -> p (t e)"), pr[:, :],
                                       sofar[:, 0:nt, :].rearrange("p t e -> p (t e)"), ALU.add))
                link(dve.tensor_scalar(steps[:, :], iota[:, 0:nt], float(BLK), None, ALU.mult))
                taken = more[:, 2 * nt * nt:].rearrange("p (e t) -> p e t", t=nt)
                link(dve.tensor_tensor(taken, sofar[:, nt, :].unsqueeze(2).to_broadcast([P, EXPERTS, nt]),
                                       steps[:, :].unsqueeze(1).to_broadcast([P, EXPERTS, nt]), ALU.is_gt))
                link(dve.tensor_reduce(need[:, :], taken, AX.X, ALU.add))
                link(dve.tensor_copy(ends[0][:, :], need[:, :]))
                for j in range(5):
                    a, b, step = ends[j % 2], ends[(j + 1) % 2], 1 << j
                    link(dve.tensor_copy(b[:, 0:step], a[:, 0:step]))
                    link(dve.tensor_tensor(b[:, step:], a[:, step:], a[:, 0:EXPERTS - step], ALU.add))
                end = ends[1]
                link(dve.tensor_tensor(need[:, :], end[:, :], need[:, :], ALU.subtract))
                for j in range(2):
                    link(dve.tensor_tensor(picked[:, j, :, :], hot[:, j, :, :], rank[:, :, :], ALU.mult))
                link(dve.tensor_reduce(mine[:, :, :], picked[:, :, :, :], AX.X, ALU.add))
                for j in range(2):
                    link(dve.tensor_tensor(picked[:, j, :, :], hot[:, j, :, :],
                                           need[:, :].unsqueeze(1).to_broadcast([P, nt, EXPERTS]), ALU.mult))
                link(dve.tensor_reduce(first[:, :, :], picked[:, :, :, :], AX.X, ALU.add))
                for j in range(2):
                    full = more[:, j * nt * nt:j * nt * nt + nt * (nt - 1)].rearrange("p (t k) -> p t k", k=nt - 1)
                    link(dve.tensor_tensor(full, over_rows(mine[:, j, :], nt - 1),
                                           steps[:, 1:nt].unsqueeze(1).to_broadcast([P, nt, nt - 1]), ALU.is_ge))
                    link(dve.tensor_reduce(over[:, j, :], full, AX.X, ALU.add))
                link(dve.tensor_tensor(first[:, :, :], first[:, :, :], over[:, :, :], ALU.add))
                link(dve.scalar_tensor_tensor(mine[:, :, :], over[:, :, :], -float(BLK), mine[:, :, :],
                                              ALU.mult, ALU.add))
                link(dve.scalar_tensor_tensor(plan.slot[:, :, :], first[:, :, :], float(BLK), mine[:, :, :],
                                              ALU.mult, ALU.add))
                for j in range(2):
                    for t in range(nt):
                        q = j * nt + t
                        dve.tensor_scalar(in_slot[:, q, :], iota[:, :], mine[:, j, t:t + 1], None, ALU.is_equal)\
                            .then_inc(s("hot_slots"), 1)
                        dve.tensor_scalar(in_blk[:, q, :], iota[:, 0:nb + 1], first[:, j, t:t + 1],
                                          token[:, t0 + t:t0 + t + 1], ALU.is_equal, ALU.mult)\
                            .then_inc(s("hot_slots"), 1)
                link(dve.tensor_tensor(passed[:, :, :], iota[0:1, 0:nb].unsqueeze(2).to_broadcast([1, nb, EXPERTS]),
                                       end[0:1, :].unsqueeze(1).to_broadcast([1, nb, EXPERTS]), ALU.is_ge))
                link(dve.tensor_reduce(blk[:, 0:nb], passed[:, :, :], AX.X, ALU.add))
                link(dve.tensor_scalar(blk[:, 0:nb], blk[:, 0:nb], float(EXPERTS - 1), None, ALU.min))
                link(dve.memset(fresh[:, :], 1.0))
                link(dve.tensor_tensor(fresh[:, 1:nb], blk[:, 1:nb], blk[:, 0:nb - 1], ALU.not_equal))
                link(dve.tensor_copy(plan.fresh[:, :], fresh[:, :]))
                link(dve.tensor_copy(blk[:, nb:nb + 1], end[0:1, EXPERTS - 1:EXPERTS]))
                link(dve.tensor_scalar(blk[:, nb + 1:nb + 2], end[0:1, EXPERTS - 1:EXPERTS], 1.0, None, ALU.subtract))
                link(dve.tensor_copy(plan.block[:, :], blk[:, :]))
                dve.wait_ge(s("slots_done"), 1)
                link(dve.tensor_copy(plan.token[:, :], pi[:, :]))
        ph.close()


class Plan:
    def __init__(self, nc, ctx, layer, tiles):
        self.blocks = 2 * tiles + EXPERTS
        self.fewest = 2 * tiles
        def sb(name, shape, dt):
            return ctx.enter_context(nc.sbuf_tensor(f"plan{layer}_{name}", shape, dt))
        self.slot = sb("slot", [P, 2, tiles], I32)
        self.weight = sb("weight", [P, 2, tiles], F32)
        self.token = sb("token", [P, self.blocks + 1], I32)
        self.block = sb("block", [1, self.blocks + 2], I32)
        self.fresh = sb("fresh", [1, self.blocks], I32)


def experts(nc, d, layer, plan):
    FC = FF // P
    nb = plan.blocks
    with ExitStack() as ctx:
        ph = Phase(nc, ctx, f"moe{layer}")
        s = ph.sem
        shapes = {"w1": [P, KC, FF], "w3": [P, KC, FF], "w2": [P, FC, D]}
        raw = {m: ph.sb(f"{m}_raw", sh) for m, sh in shapes.items()}
        hi = {m: ph.sb(f"{m}_hi", sh, F32R) for m, sh in shapes.items()}
        lo = {m: ph.sb(f"{m}_lo", sh, F32R) for m, sh in shapes.items()}
        half = {m: sh[1] // 2 for m, sh in shapes.items()}
        dram = {"w1": d.w1, "w3": d.w3, "w2": d.w2}
        ident = ph.sb("ident", [P, P])
        idx = ph.sb("idx", [P, 1], I32)
        xg = ph.sb("xg", [P, D])
        xt_hi = ph.sb("xt_hi", [P, KC, P], F32R)
        xt_lo = ph.sb("xt_lo", [P, KC, P], F32R)
        sil = ph.sb("sil", [P, FF])
        a = ph.sb("a", [P, FF])
        at_hi = ph.sb("at_hi", [P, FC, P], F32R)
        at_lo = ph.sb("at_lo", [P, FC, P], F32R)
        y = ph.sb("y", [P, D])
        zero = ph.sb("zero", [P, D])
        pxt = ph.ps("pxt", [P, KC, P])
        pg = ph.ps("pg", [P, FF])
        pu = ph.ps("pu", [P, FF])
        pat = ph.ps("pat", [P, FC, P])
        py = ph.ps("py", [P, D])

        MATS = ("w1", "w3", "w2")

        def blocks(eng, body, tail=None, otherwise=None):
            count = eng.value_load(plan.block[0:1, nb:nb + 1], min_val=plan.fewest, max_val=nb)
            for k in range(2):
                body(k, k)
            with eng.Fori(2, nb) as k:
                with eng.If(k < count):
                    body(k, 2)
                if otherwise:
                    with eng.If(k >= count):
                        otherwise(k)
            if tail:
                tail(count, eng.value_load(plan.block[0:1, nb + 1:nb + 2], min_val=plan.fewest - 1, max_val=nb - 1))

        def by_expert(eng, k, least, fresh, kept):
            if least == 0:
                fresh()
                return
            new = eng.value_load(plan.fresh[0:1, ds(k, 1)], min_val=0, max_val=1)
            with eng.If(new > 0):
                fresh()
            with eng.If(new < 1):
                kept()

        with nc.Block() as block:
            @block.sync
            def _(sp):
                sp.dma_start(ident[:, :], d.ident).then_inc(s("ident"), 16)

                def bring(mats, k, least):
                    def fresh():
                        e = sp.value_load(plan.block[0:1, ds(k, 1)], min_val=0, max_val=EXPERTS - 1)
                        for m in mats:
                            for h in range(2):
                                cut = slice(h * half[m], (h + 1) * half[m])
                                if least:
                                    sp.wait_ge(s(f"{m}_lo{h}"), k)
                                sp.dma_start(raw[m][:, cut, :],
                                             dram[m][layer, ds(e, 1), h * half[m] * P:(h + 1) * half[m] * P, :]
                                             .rearrange("o (k p) n -> p (o k) n", p=P)).then_inc(s(f"{m}_raw{h}"), 16)

                    def kept():
                        for m in mats:
                            for h in range(2):
                                sp.wait_ge(s(f"{m}_lo{h}"), k)
                                sp.sem_inc(s(f"{m}_raw{h}"), 16)

                    by_expert(sp, k, least, fresh, kept)

                def body(b, least):
                    bring(("w1", "w3"), b, least)
                    if least:
                        bring(("w2",), b - 1, least - 1)

                def unused(k):
                    sp.dma_start(d.yd[ds(k * BLK, BLK), :], zero[:, :]).then_inc(s("covered"), 16)

                sp.wait_ge(s("zero_set"), 1)
                blocks(sp, body, lambda count, last: bring(("w2",), last, 1), None if layer else unused)

            @block.gpsimd
            def _(pool):
                def gather(k, n):
                    pool.tensor_copy(idx[:, :], plan.token[:, ds(k, 1)]).then_inc(s("idx_ready"), 1)
                    pool.wait_ge(s("idx_ready"), n + 1)
                    pool.sem_inc(s("gathers"), 1)
                    pool.indirect_dma_start(xg[:, :], None, d.hd[:, :], bass.IndirectOffsetOnAxis(idx[:, :], 0))\
                        .then_inc(s("gathered"), 16)

                def ahead(k, least):
                    pool.wait_ge(s("xt_turned"), k + 1)
                    gather(k + 1, k + 1)

                def finish(count, last):
                    pool.wait_ge(s("gathered"), count * 16 + 16)
                    pool.wait_ge(s("y_stored"), count * 16 + 16)
                    if layer == 0:
                        pool.wait_ge(s("covered"), nb * 16)

                pool.memset(zero[:, :], 0.0).then_inc(s("zero_set"), 1)
                gather(0, 0)
                blocks(pool, ahead, finish)

            @block.tensor
            def _(pe):
                def turn_x(n):
                    pe.wait_ge(s("gathered"), n * 16)
                    for k in range(KC):
                        last = pe.transpose(pxt[:, k, :], xg[:, k * P:(k + 1) * P], ident[:, :])
                    last.then_inc(s("xt_turned"), 1)

                def out_product(n, before, least):
                    pe.wait_ge(s("at_lo"), n)
                    if least:
                        pe.wait_ge(s("y_out"), before)
                    for h in range(2):
                        pe.wait_ge(s(f"w2_lo{h}"), n)
                        for c in range(2):
                            for k in range(h * half["w2"], (h + 1) * half["w2"]):
                                cols = slice(c * N, (c + 1) * N)
                                last = product3(pe, py[:, cols], at_hi[:, k, :], at_lo[:, k, :],
                                                hi["w2"][:, k, cols], lo["w2"][:, k, cols], k == 0, k == FC - 1)
                    last.then_inc(s("w2_done"), 1)

                def body(b, least):
                    n = b + 1
                    pe.wait_ge(s("xt_hi"), n)
                    pe.wait_ge(s("xt_lo"), n)
                    for w, out, used in (("w1", pg, "sil_ready"), ("w3", pu, "a_ready")):
                        if least:
                            pe.wait_ge(s(used), b)
                        for h in range(2):
                            pe.wait_ge(s(f"{w}_lo{h}"), n)
                            for k in range(h * half[w], (h + 1) * half[w]):
                                last = product3(pe, out[:, :], xt_hi[:, k, :], xt_lo[:, k, :], hi[w][:, k, :],
                                                lo[w][:, k, :], k == 0, k == KC - 1)
                        last.then_inc(s(f"{w}_done"), 1)
                    turn_x(n + 1)
                    if least:
                        out_product(b, b - 1, least - 1)
                    pe.wait_ge(s("a_ready"), n)
                    for k in range(FC):
                        last = pe.transpose(pat[:, k, :], a[:, k * P:(k + 1) * P], ident[:, :])
                    last.then_inc(s("at_turned"), 1)

                pe.wait_ge(s("ident"), 16)
                turn_x(1)
                blocks(pe, body, lambda count, last: out_product(count, last, 1))

            @block.scalar
            def _(act):
                act.preload_act_table(ACT.Silu)

                def high(m, n, before, least):
                    for h in range(2):
                        cut = slice(h * half[m], (h + 1) * half[m])
                        act.wait_ge(s(f"{m}_raw{h}"), n * 16)
                        if h == 0 and least:
                            act.wait_ge(s(f"{m}_done"), before)
                        act.activation(hi[m][:, cut, :], raw[m][:, cut, :], ACT.Copy).then_inc(s(f"{m}_hi{h}"), 1)

                def skip(m):
                    for h in range(2):
                        act.sem_inc(s(f"{m}_hi{h}"), 1)

                def put_out(n, k):
                    act.wait_ge(s("w2_done"), n)
                    act.wait_ge(s("y_stored"), n * 16)
                    act.activation(y[:, :], py[:, :], ACT.Copy).then_inc(s("y_out"), 1)
                    act.wait_ge(s("y_out"), n)
                    act.dma_start(d.yd[ds(k * BLK, BLK), :], y[:, :]).then_inc(s("y_stored"), 16)

                def x_high(n):
                    act.wait_ge(s("xt_turned"), n)
                    act.activation(xt_hi[:, :, :], pxt[:, :, :], ACT.Copy).then_inc(s("xt_hi"), 1)

                def before_out(n, k, least):
                    act.wait_ge(s("at_turned"), n)
                    act.activation(at_hi[:, :, :], pat[:, :, :], ACT.Copy).then_inc(s("at_hi"), 1)
                    by_expert(act, k, least, lambda: high("w2", n, k, least), lambda: skip("w2"))

                def body(b, least):
                    n = b + 1

                    def fresh():
                        high("w1", n, b, least)
                        x_high(n)
                        high("w3", n, b, least)

                    def kept():
                        skip("w1")
                        x_high(n)
                        skip("w3")

                    by_expert(act, b, least, fresh, kept)
                    if least > 1:
                        put_out(b - 1, b - 2)
                    if least:
                        before_out(b, b - 1, least - 1)
                    act.wait_ge(s("w1_done"), n)
                    if least:
                        act.wait_ge(s("a_ready"), b)
                    act.activation(sil[:, :], pg[:, :], ACT.Silu).then_inc(s("sil_ready"), 1)

                def tail(count, last):
                    put_out(last, last - 1)
                    before_out(count, last, 1)
                    put_out(count, last)

                blocks(act, body, tail)

            @block.vector
            def _(dve):
                def low(m, n):
                    for h in range(2):
                        cut = slice(h * half[m], (h + 1) * half[m])
                        dve.wait_ge(s(f"{m}_hi{h}"), n)
                        dve.tensor_tensor(lo[m][:, cut, :], raw[m][:, cut, :], hi[m][:, cut, :].bitcast(F32),
                                          ALU.subtract).then_inc(s(f"{m}_lo{h}"), 1)

                def skip(m, n):
                    for h in range(2):
                        dve.wait_ge(s(f"{m}_hi{h}"), n)
                        dve.sem_inc(s(f"{m}_lo{h}"), 1)

                def x_low(n):
                    dve.wait_ge(s("xt_hi"), n)
                    dve.tensor_tensor(xt_lo[:, :, :], pxt[:, :, :], xt_hi[:, :, :].bitcast(F32), ALU.subtract)\
                        .then_inc(s("xt_lo"), 1)

                def before_out(n, k, least):
                    dve.wait_ge(s("at_hi"), n)
                    dve.tensor_tensor(at_lo[:, :, :], pat[:, :, :], at_hi[:, :, :].bitcast(F32), ALU.subtract)\
                        .then_inc(s("at_lo"), 1)
                    by_expert(dve, k, least, lambda: low("w2", n), lambda: skip("w2", n))

                def body(b, least):
                    n = b + 1
                    if layer == 0:
                        dve.sem_inc(s("covered"), 16)

                    def fresh():
                        low("w1", n)
                        x_low(n)
                        low("w3", n)

                    def kept():
                        skip("w1", n)
                        x_low(n)
                        skip("w3", n)

                    by_expert(dve, b, least, fresh, kept)
                    if least:
                        before_out(b, b - 1, least - 1)
                    dve.wait_ge(s("sil_ready"), n)
                    dve.wait_ge(s("w3_done"), n)
                    if least:
                        dve.wait_ge(s("at_turned"), b)
                    dve.tensor_tensor(a[:, :], sil[:, :], pu[:, :], ALU.mult).then_inc(s("a_ready"), 1)

                dve.sem_inc(s("y_stored"), 16)
                blocks(dve, body, lambda count, last: before_out(count, last, 1))
        ph.close()


def combine(nc, d, layer, streams, plan, final):
    t0 = streams[0][1]
    with ExitStack() as ctx:
        ph = Phase(nc, ctx, f"comb{layer}")
        s = ph.sem
        x = [ph.sb(f"x{b}", [P, D]) for b in range(2)]
        y = [[ph.sb(f"y{j}{b}", [P, D]) for b in range(2)] for j in range(2)]
        idx = [[ph.sb(f"idx{j}{b}", [P, 1], I32) for b in range(2)] for j in range(2)]
        wt = [ph.sb(f"wt{b}", [P, 2]) for b in range(2)]
        gate = ph.sb("gate", [P, 2, D])
        fin_g = ph.sb("fin_g", [P, D])
        junk = ph.sb("junk", [P, D])
        stat = ph.sb("stat", [P, 2, 4])
        eps = ph.sb("eps", [P, 1])
        total = sum(p for _, _, p, _ in streams)
        dst = d.out if final else d.xs

        with nc.Block() as block:
            @block.sync
            def _(sp):
                for st in (LAT, CTX):
                    sp.dma_start(gate[:, st, :], d.mods[layer, st, G2, :].partition_broadcast(P))\
                        .then_inc(s("tables"), 16)
                sp.dma_start(fin_g[:, :], d.final_g.partition_broadcast(P)).then_inc(s("tables"), 16)
                for st, ta, pairs, before in streams:
                    with sp.Fori(0, pairs) as i:
                        for b in range(2):
                            if before:
                                sp.wait_ge(s(f"x_stored{b}"), (i + before) * 16)
                            sp.dma_start(x[b][:, :], d.xs[ds((i * 2 + (ta + b)) * P, P), :])\
                                .then_inc(s(f"x_loaded{b}"), 16)

            @block.gpsimd
            def _(pool):
                for st, ta, pairs, before in streams:
                    with pool.Fori(0, pairs) as i:
                        n = i + (before + 1)
                        for b in range(2):
                            for j in range(2):
                                if before:
                                    pool.wait_ge(s(f"gathered{j}{b}"), (n - 1) * 16)
                                pool.tensor_copy(idx[j][b][:, :], plan.slot[:, j, ds(i * 2 + (ta - t0 + b), 1)])\
                                    .then_inc(s(f"idx_ready{j}{b}"), 1)
                                pool.wait_ge(s(f"idx_ready{j}{b}"), n)
                                if before:
                                    pool.wait_ge(s(f"x_ready{b}"), n - 1)
                                pool.sem_inc(s("gathers"), 1)
                                pool.indirect_dma_start(y[j][b][:, :], None, d.yd[:, :],
                                                        bass.IndirectOffsetOnAxis(idx[j][b][:, :], 0))\
                                    .then_inc(s(f"gathered{j}{b}"), 16)

            @block.scalar
            def _(act):
                act.preload_act_table(ACT.Sqrt)
                for st, ta, pairs, before in streams:
                    with act.Fori(0, pairs) as i:
                        n = i + (before + 1)
                        for b in range(2):
                            act.wait_ge(s(f"x_ready{b}"), n)
                            if final:
                                act.activation(junk[:, :], x[b][:, :], ACT.Square, accum_out=stat[:, b, 0:1])\
                                    .then_inc(s(f"squares{b}"), 1)
                                act.wait_ge(s(f"squares{b}"), n)
                                act.wait_ge(s("eps_set"), 1)
                                act.activation(stat[:, b, 1:2], stat[:, b, 0:1], ACT.Sqrt, bias=eps[:, :],
                                               scale=1.0 / D).then_inc(s(f"root{b}"), 1)
                                act.wait_ge(s(f"normed{b}"), n)
                            row = (i * 2 + (ta + b - (CTX_TILES if final else 0))) * P
                            act.dma_start(dst[ds(row, P), :], x[b][:, :]).then_inc(s(f"x_stored{b}"), 16)
                for b in range(2):
                    act.wait_ge(s(f"x_stored{b}"), 16 * total)

            @block.vector
            def _(dve):
                dve.memset(eps[:, :], EPS).then_inc(s("eps_set"), 1)
                dve.wait_ge(s("tables"), 48)
                for st, ta, pairs, before in streams:
                    with dve.Fori(0, pairs) as i:
                        n = i + (before + 1)
                        for b in range(2):
                            dve.tensor_copy(wt[b][:, :].unsqueeze(2), plan.weight[:, :, ds(i * 2 + (ta - t0 + b), 1)])\
                                .then_inc(s(f"wt_ready{b}"), 1)
                            dve.wait_ge(s(f"wt_ready{b}"), n)
                            dve.wait_ge(s(f"gathered0{b}"), n * 16)
                            dve.tensor_scalar(y[0][b][:, :], y[0][b][:, :], wt[b][:, 0:1], None, ALU.mult)\
                                .then_inc(s(f"first{b}"), 1)
                            dve.wait_ge(s(f"first{b}"), n)
                            dve.wait_ge(s(f"gathered1{b}"), n * 16)
                            dve.scalar_tensor_tensor(y[1][b][:, :], y[1][b][:, :], wt[b][:, 1:2], y[0][b][:, :],
                                                     ALU.mult, ALU.add).then_inc(s(f"second{b}"), 1)
                            dve.wait_ge(s(f"second{b}"), n)
                            dve.tensor_tensor(y[1][b][:, :], y[1][b][:, :], gate[:, st, :], ALU.mult)\
                                .then_inc(s(f"gated{b}"), 1)
                            dve.wait_ge(s(f"gated{b}"), n)
                            dve.wait_ge(s(f"x_loaded{b}"), n * 16)
                            dve.tensor_tensor(x[b][:, :], x[b][:, :], y[1][b][:, :], ALU.add)\
                                .then_inc(s(f"x_ready{b}"), 1)
                            if final:
                                dve.wait_ge(s(f"root{b}"), n)
                                dve.reciprocal(stat[:, b, 2:3], stat[:, b, 1:2]).then_inc(s(f"rstd{b}"), 1)
                                dve.wait_ge(s(f"rstd{b}"), n)
                                dve.scalar_tensor_tensor(x[b][:, :], x[b][:, :], stat[:, b, 2:3], fin_g[:, :],
                                                         ALU.mult, ALU.mult).then_inc(s(f"normed{b}"), 1)
        ph.close()


QK, VG = 2 * HEADS * DK, 2 * HEADS * DV
LAT_TILES = TILES - CTX_TILES
TOKEN_GROUPS = [(0, CTX_LEN), (CTX_LEN, N), (CTX_LEN + N, N)]
SCAN = [(CTX, 0, CTX_TILES - 1, 1, 0), (LAT, CTX_TILES, TILES - 1, 1, 1),
        (LAT, CTX_TILES + 2, TILES - 3, LAT_TILES // 2 - 1, 2)]
LAST = {0: CHUNK - 1, 1: 0}
REF = {0: CHUNK // 2, 1: CHUNK // 2 - 1}


def gla_values(nc, d, ht):
    with ExitStack() as ctx:
        ph = Phase(nc, ctx, "glav")
        s = ph.sem
        raw = ph.sb("raw", [P, KC, N])
        w = [Split(nc, ctx, f"glav_w{b}", [P, KC, N]) for b in range(2)]
        out = [ph.sb(f"out{b}", [P, N]) for b in range(4)]
        acc = [ph.ps(f"acc{b}", [P, N]) for b in range(4)]
        jobs = [("v", 0, 0), ("v", 1, 0), ("gate", 0, CTX_TILES), ("gate", 1, CTX_TILES)]
        steps = [(g, t) for g, job in enumerate(jobs) for t in range(job[2], TILES)]

        with nc.Block() as block:
            @block.sync
            def _(sp):
                def load(g):
                    c0 = QK + g * N
                    if g:
                        sp.wait_ge(s("w_lo"), g)
                    sp.dma_start(raw[:, :, :], d.w_in[:, c0:c0 + N].rearrange("(k p) n -> p k n", p=P))\
                        .then_inc(s("w_loaded"), 16)
                for g in range(len(jobs)):
                    load(g)

            @block.gpsimd
            def _(pool):
                for n, (g, t) in enumerate(steps):
                    kind, half, t0 = jobs[g]
                    dst, row = (d.vd, t * P) if kind == "v" else (d.gd, (t - CTX_TILES) * P)
                    pool.wait_ge(s("out_ready"), n + 1)
                    pool.dma_start(dst[row:row + P, half * N:(half + 1) * N], out[n % 4][:, :])\
                        .then_inc(s(f"stored{n % 4}"), 16)
                for b in range(4):
                    pool.wait_ge(s(f"stored{b}"), 16 * len(range(b, len(steps), 4)))

            @block.tensor
            def _(pe):
                for n, (g, t) in enumerate(steps):
                    if t == jobs[g][2]:
                        pe.wait_ge(s("w_lo"), g + 1)
                    if n >= 4:
                        pe.wait_ge(s("out_ready"), n - 3)
                    cols = slice(t * P, (t + 1) * P)
                    for k in range(KC):
                        last = product3(pe, acc[n % 4][:, :], ht.hi[:, k, cols], ht.lo[:, k, cols],
                                        w[g % 2].hi[:, k, :], w[g % 2].lo[:, k, :], k == 0, k == KC - 1)
                    last.then_inc(s("acc_ready"), 1)

            @block.scalar
            def _(act):
                act.preload_act_table(ACT.Silu)
                starts = [min(n for n, (g, _) in enumerate(steps) if g == q) for q in range(len(jobs))]

                def high(g):
                    act.wait_ge(s("w_loaded"), 16 * (g + 1))
                    if g >= 2:
                        act.wait_ge(s("acc_ready"), starts[g - 1])
                    act.activation(w[g % 2].hi[:, :, :], raw[:, :, :], ACT.Copy).then_inc(s("w_hi"), 1)

                high(0)
                for n, (g, t) in enumerate(steps):
                    if n == starts[g] and g + 1 < len(jobs):
                        high(g + 1)
                    act.wait_ge(s("acc_ready"), n + 1)
                    if n >= 4:
                        act.wait_ge(s(f"stored{n % 4}"), 16 * (n // 4))
                    act.activation(out[n % 4][:, :], acc[n % 4][:, :], ACT.Copy if jobs[g][0] == "v" else ACT.Silu)\
                        .then_inc(s("out_ready"), 1)

            @block.vector
            def _(dve):
                for g in range(len(jobs)):
                    dve.wait_ge(s("w_hi"), g + 1)
                    dve.tensor_tensor(w[g % 2].lo[:, :, :], raw[:, :, :], w[g % 2].hi[:, :, :].bitcast(F32),
                                      ALU.subtract).then_inc(s("w_lo"), 1)
        ph.close()


def gla_keys(nc, d, ht, qk, cum):
    with ExitStack() as ctx:
        ph = Phase(nc, ctx, "glak")
        s = ph.sem
        raw = ph.sb("raw", [P, KC, P])
        w = [Split(nc, ctx, f"glak_w{b}", [P, KC, P]) for b in range(2)]
        lr_raw = ph.sb("lr_raw", [P, KC, 2, RANK])
        lr_w = Split(nc, ctx, "glak_lrw", [P, KC, 2, RANK])
        low = [ph.sb(f"low{r}", [RANK + 1, TOK]) for r in range(2)]
        up = [ph.sb(f"up{r}", [RANK + 1, HEADS * DK]) for r in range(2)]
        cums = ph.sb("cums", [P, 2, P])
        e = [ph.sb(f"e{b}", [P, HEADS * DK]) for b in range(2)]
        logs = [ph.sb(f"logs{b}", [P, HEADS * DK]) for b in range(2)]
        acc = [ph.ps(f"acc{g}", [P, N]) for g in range(3)]
        pz = [ph.ps(f"pz{b}", [P, N]) for b in range(2)]
        pc = [ph.ps(f"pc{b}", [P, N]) for b in range(2)]
        chunks = QK // P
        pairs = chunks // 2
        units = [(t, r) for t in range(TILES) for r in range(2)]

        with nc.Block() as block:
            @block.sync
            def _(sp):
                sp.dma_start(lr_raw[:, :, :, :].rearrange("p k r n -> p k (r n)"),
                             d.w_in[:, QK + VG:GLA_IN].rearrange("(k p) n -> p k n", p=P)).then_inc(s("lr_loaded"), 16)
                for r in range(2):
                    sp.dma_start(up[r][0:RANK, :], d.gk_up[r]).then_inc(s("up_loaded"), 16)
                    sp.dma_start(up[r][RANK:RANK + 1, :], d.gk_b[r:r + 1, :]).then_inc(s("up_loaded"), 16)
                sp.dma_start(cums[:, :, :], d.cums).then_inc(s("up_loaded"), 16)

                def load(b, i):
                    sp.dma_start(raw[:, :, :], d.w_in[:, ds((i * 2 + b) * P, P)].rearrange("(k p) n -> p k n", p=P))\
                        .then_inc(s(f"w_loaded{b}"), 16)

                load(0, 0)
                sp.wait_ge(s("w_lo0"), 1)
                load(1, 0)
                with sp.Fori(1, pairs) as i:
                    for b in range(2):
                        sp.wait_ge(s(f"w_lo{1 - b}"), i + b)
                        load(b, i)

            @block.gpsimd
            def _(pool):
                for r in range(2):
                    pool.memset(low[r][:, :], 1.0).then_inc(s("ones_set"), 1)

            @block.tensor
            def _(pe):
                pe.wait_ge(s("lr_lo"), 1)
                for r in range(2):
                    for g, (a, n) in enumerate(TOKEN_GROUPS):
                        if r:
                            pe.wait_ge(s("low_ready"), g + 1)
                        for k in range(KC):
                            last = product3(pe, acc[g][0:RANK, 0:n], lr_w.hi[:, k, r, :], lr_w.lo[:, k, r, :],
                                            ht.hi[:, k, a:a + n], ht.lo[:, k, a:a + n], k == 0, k == KC - 1)
                        last.then_inc(s("low_summed"), 1)

                def chunk(b, i, first):
                    pe.wait_ge(s(f"w_lo{b}"), i + 1)
                    for g, (a, n) in enumerate(TOKEN_GROUPS):
                        if first and b == 0:
                            pe.wait_ge(s("low_ready"), len(TOKEN_GROUPS) + g + 1)
                        else:
                            pe.wait_ge(s(f"qk_ready{g}{1 - b}"), i + b)
                        for k in range(KC):
                            last = product3(pe, acc[g][:, 0:n], w[b].hi[:, k, :], w[b].lo[:, k, :],
                                            ht.hi[:, k, a:a + n], ht.lo[:, k, a:a + n], k == 0, k == KC - 1)
                        last.then_inc(s(f"qk_summed{g}{b}"), 1)

                for b in range(2):
                    chunk(b, 0, True)
                with pe.Fori(1, pairs) as i:
                    for b in range(2):
                        chunk(b, i, False)

                pe.wait_ge(s("up_loaded"), 80)

                def sums(n):
                    t, r = units[n]
                    pe.wait_ge(s("logs_ready"), n + 1)
                    if n >= 2:
                        pe.wait_ge(s("cum_ready"), n - 1)
                    for h in range(HEADS):
                        last = pe.matmul(pc[n % 2][:, h * P:(h + 1) * P], logs[n % 2][:, h * DK:(h + 1) * DK],
                                         cums[:, r, :], start=True, stop=True)
                    last.then_inc(s("cum_summed"), 1)

                for n, (t, r) in enumerate(units):
                    if n >= 2:
                        pe.wait_ge(s("e_ready"), n - 1)
                        pe.wait_ge(s("z_ready"), n - 1)
                    pe.matmul(pz[n % 2][:, :], low[r][:, t * P:(t + 1) * P], up[r][:, :], start=True, stop=True)\
                        .then_inc(s("z_summed"), 1)
                    if n:
                        sums(n - 1)
                sums(len(units) - 1)

            @block.scalar
            def _(act):
                act.preload_act_table_set("natural_log_exp_and_others")
                act.wait_ge(s("lr_loaded"), 16)
                act.activation(lr_w.hi[:, :, :, :], lr_raw[:, :, :, :], ACT.Copy).then_inc(s("lr_hi"), 1)
                act.wait_ge(s("ones_set"), 2)
                for r in range(2):
                    for g, (a, n) in enumerate(TOKEN_GROUPS):
                        act.wait_ge(s("low_summed"), r * 3 + g + 1)
                        act.activation(low[r][0:RANK, a:a + n], acc[g][0:RANK, 0:n], ACT.Copy)\
                            .then_inc(s("low_ready"), 1)

                def high(b, i, first):
                    act.wait_ge(s(f"w_loaded{b}"), i * 16 + 16)
                    if not first:
                        act.wait_ge(s(f"qk_summed2{b}"), i)
                    act.activation(w[b].hi[:, :, :], raw[:, :, :], ACT.Copy).then_inc(s(f"w_hi{b}"), 1)

                def chunk(b, i):
                    for g, (a, n) in enumerate(TOKEN_GROUPS):
                        act.wait_ge(s(f"qk_summed{g}{b}"), i + 1)
                        act.activation(qk[:, ds(i * 2 + b, 1), a:a + n].rearrange("p o n -> p (o n)"),
                                       acc[g][:, 0:n], ACT.Copy).then_inc(s(f"qk_ready{g}{b}"), 1)

                for b in range(2):
                    high(b, 0, True)
                for b in range(2):
                    chunk(b, 0)
                with act.Fori(1, pairs) as i:
                    for b in range(2):
                        high(b, i, False)
                    for b in range(2):
                        chunk(b, i)

                for n, (t, r) in enumerate(units):
                    b = n % 2
                    act.wait_ge(s("z_summed"), n + 1)
                    if n >= 2:
                        act.wait_ge(s("logs_ready"), n - 1)
                    act.activation(e[b][:, :], pz[b][:, :], ACT.Abs).then_inc(s("e_ready"), 1)
                    act.wait_ge(s("e_ready"), n + 1)
                    act.activation(e[b][:, :], e[b][:, :], ACT.Exp, scale=-1.0).then_inc(s("e_exp"), 1)
                    act.wait_ge(s("e_exp"), n + 1)
                    act.activation(e[b][:, :], e[b][:, :], ACT.Ln, bias=1.0).then_inc(s("e_log"), 1)

            @block.vector
            def _(dve):
                dve.wait_ge(s("lr_hi"), 1)
                dve.tensor_tensor(lr_w.lo[:, :, :, :], lr_raw[:, :, :, :], lr_w.hi[:, :, :, :].bitcast(F32),
                                  ALU.subtract).then_inc(s("lr_lo"), 1)

                def lows(b, i):
                    dve.wait_ge(s(f"w_hi{b}"), i + 1)
                    dve.tensor_tensor(w[b].lo[:, :, :], raw[:, :, :], w[b].hi[:, :, :].bitcast(F32),
                                      ALU.subtract).then_inc(s(f"w_lo{b}"), 1)

                for b in range(2):
                    lows(b, 0)
                with dve.Fori(1, pairs) as i:
                    for b in range(2):
                        lows(b, i)

                def take(n):
                    t, r = units[n]
                    dve.wait_ge(s("cum_summed"), n + 1)
                    dve.tensor_copy(cum[:, r, :, t * P:(t + 1) * P],
                                    pc[n % 2][:, :].rearrange("p (h n) -> p h n", h=HEADS)).then_inc(s("cum_ready"), 1)

                for n, (t, r) in enumerate(units):
                    b = n % 2
                    dve.wait_ge(s("e_ready"), n + 1)
                    if n >= 2:
                        dve.wait_ge(s("cum_summed"), n - 1)
                    dve.tensor_scalar(logs[b][:, :], pz[b][:, :], 0.0, None, ALU.min).then_inc(s("z_ready"), 1)
                    dve.wait_ge(s("z_ready"), n + 1)
                    dve.wait_ge(s("e_log"), n + 1)
                    dve.tensor_tensor(logs[b][:, :], logs[b][:, :], e[b][:, :], ALU.subtract).then_inc(s("logs_ready"), 1)
                    if n:
                        take(n - 1)
                take(len(units) - 1)
        ph.close()


def gla_scan(nc, d, qk, cum):
    with ExitStack() as ctx:
        ph = Phase(nc, ctx, "scan")
        s = ph.sem
        W = HEADS * P
        v = [[ph.sb(f"v{r}{b}", [P, HEADS * DV]) for b in range(2)] for r in range(2)]
        names = ("cr", "cl", "eq", "ek", "es", "el", "qi", "ki", "qs", "ks")
        t_ = {m: [ph.sb(f"{m}{r}", [P, HEADS, P]) for r in range(2)] for m in names}
        att = [ph.sb(f"att{r}", [P, HEADS, P]) for r in range(2)]
        kst = [ph.sb(f"kst{r}", [P, HEADS, P]) for r in range(2)]
        state = [ph.sb(f"state{r}", [P, HEADS, DV]) for r in range(2)]
        o = [ph.sb(f"o{r}", [P, HEADS * DV]) for r in range(2)]
        seen = ph.sb("seen", [P, 2, CHUNK], I32)
        ident = ph.sb("ident", [P, P])
        patt = ph.ps("patt", [P, 2, HEADS, CHUNK])
        pkst = ph.ps("pkst", [P, HEADS, P])
        po = [ph.ps(f"po{r}", [P, HEADS, DV]) for r in range(2)]
        pds = ph.ps("pds", [P, HEADS, DV])

        def tile(i, b, r, ta, tb):
            return i * 2 + (ta + b) if r == 0 else i * -2 + (tb - b)

        def after(eng, what, r, b, n, first, per=1):
            if b == 1:
                eng.wait_ge(s(f"{what}{r}0"), n * per)
            elif not first:
                eng.wait_ge(s(f"{what}{r}1"), (n - 1) * per)

        def order(r):
            return (0, 1) if r == 0 else (1, 0)

        with nc.Block() as block:
            @block.sync
            def _(sp):
                sp.dma_start(seen[:, :, :], d.seen).then_inc(s("tables"), 16)
                sp.dma_start(ident[:, :], d.ident).then_inc(s("tables"), 16)
                for st, ta, tb, pairs, before in SCAN:
                    with sp.Fori(0, pairs) as i:
                        n, first = i + (before + 1), before == 0
                        m, first_lat = i + before, before == 1
                        for b in range(2):
                            for r in range(2):
                                if before:
                                    sp.wait_ge(s(f"pds1{r}{b}"), (n - 1) * 2)
                                sp.dma_start(v[r][b][:, :], d.vd[ds(tile(i, b, r, ta, tb) * P, P), :])\
                                    .then_inc(s(f"v_loaded{r}{b}"), 16)

            @block.gpsimd
            def _(pool):
                for r in range(2):
                    pool.memset(att[r][:, :, :], 0.0).then_inc(s("zeroed"), 1)
                    pool.memset(state[r][:, :, :], 0.0).then_inc(s("zeroed"), 1)
                for st, ta, tb, pairs, before in SCAN:
                    if st == CTX:
                        continue
                    with pool.Fori(0, pairs) as i:
                        for b in range(2):
                            for r in range(2):
                                row = (tile(i, b, r, ta, tb) - CTX_TILES) * P
                                pool.wait_ge(s(f"o_ready{r}{b}"), i + before)
                                pool.dma_start(d.od[r, ds(row, P), :], o[r][:, :]).then_inc(s(f"o_stored{r}{b}"), 16)
                for b in range(2):
                    for r in range(2):
                        pool.wait_ge(s(f"o_stored{r}{b}"), 16 * (LAT_TILES // 2))

            @block.tensor
            def _(pe):
                pe.wait_ge(s("tables"), 32)
                for st, ta, tb, pairs, before in SCAN:
                    with pe.Fori(0, pairs) as i:
                        n, first = i + (before + 1), before == 0
                        m, first_lat = i + before, before == 1
                        for b in range(2):
                            if st == LAT:
                                for r in range(2):
                                    pe.wait_ge(s(f"qi{r}{b}"), m)
                                    pe.wait_ge(s(f"ki{r}{b}"), m)
                                    after(pe, "masked", 1, b, m, first_lat, 2)
                                    for h in range(HEADS):
                                        for c in range(2):
                                            at = slice(c * CHUNK, (c + 1) * CHUNK)
                                            last = pe.matmul(patt[at, r, h, :], t_["ki"][r][:, h, at],
                                                             t_["qi"][r][:, h, at], start=True, stop=True)
                                    last.then_inc(s(f"scored{r}{b}"), 1)
                            for r in range(2):
                                pe.wait_ge(s(f"ks{r}{b}"), n)
                                if r == 1:
                                    pe.wait_ge(s(f"kst0{b}"), n)
                                else:
                                    after(pe, "kst", 1, b, n, first)
                                for h in range(HEADS):
                                    last = pe.transpose(pkst[:, h, :], t_["ks"][r][:, h, :], ident[:, :])
                                last.then_inc(s(f"turned{r}{b}"), 1)
                            for j in range(2):
                                for r in range(2):
                                    c = order(r)[j]
                                    at = slice(c * CHUNK, (c + 1) * CHUNK)
                                    if j == 0:
                                        pe.wait_ge(s(f"v_loaded{r}{b}"), n * 16)
                                    if st == LAT:
                                        if j == 0:
                                            pe.wait_ge(s(f"masked{r}{b}"), m * 2)
                                            after(pe, "o_ready", r, b, m, first_lat)
                                            for h in range(HEADS):
                                                pe.matmul(po[r][:, h, :], att[r][:, h, :],
                                                          v[r][b][:, h * DV:(h + 1) * DV], start=h % 2 == 0, stop=False)
                                        for half in range(2):
                                            if j == 1:
                                                pe.wait_ge(s(f"state{half}{r}{b}"), n * 2 - 1)
                                            else:
                                                after(pe, f"state{half}", r, b, n, first, 2)
                                                pe.wait_ge(s(f"qs{r}{b}"), m)
                                        for h in range(HEADS):
                                            last = pe.matmul(po[r][at, h, :], t_["qs"][r][:, h, at],
                                                             state[r][:, h, :], start=False, stop=h % 2 == 1)
                                        if j == 1:
                                            last.then_inc(s(f"o_summed{r}{b}"), 1)
                                    if j == 0:
                                        pe.wait_ge(s(f"kst{r}{b}"), n)
                                    for half in range(2):
                                        if r == 1:
                                            pe.wait_ge(s(f"state{half}0{b}"), n * 2 - (1 - j))
                                        elif j == 1:
                                            pe.wait_ge(s(f"state{half}1{b}"), n * 2 - 1)
                                        else:
                                            after(pe, f"state{half}", 1, b, n, first, 2)
                                        for h in range(half * 2, half * 2 + 2):
                                            last = pe.matmul(pds[:, h, :], kst[r][at, h, :],
                                                             v[r][b][at, h * DV:(h + 1) * DV], start=True, stop=True)
                                        last.then_inc(s(f"pds{half}{r}{b}"), 1)

            @block.scalar
            def _(act):
                act.preload_act_table(ACT.Exp)
                for st, ta, tb, pairs, before in SCAN:
                    with act.Fori(0, pairs) as i:
                        n, first = i + (before + 1), before == 0
                        m, first_lat = i + before, before == 1
                        for b in range(2):
                            for r in range(2):
                                act.wait_ge(s(f"cl{r}{b}"), n)
                                after(act, "ks", r, b, n, first)
                                act.activation(t_["el"][r][:, :, :], t_["cl"][r][:, :, :], ACT.Exp)\
                                    .then_inc(s(f"el{r}{b}"), 1)
                                t = tile(i, b, r, ta, tb)
                                after(act, "state1", r, b, n, first, 2)
                                act.activation(t_["es"][r][:, :, :], cum[:, r, :, ds(t * P, P)], ACT.Exp)\
                                    .then_inc(s(f"es{r}{b}"), 1)
                                if st == LAT:
                                    act.wait_ge(s(f"cr{r}{b}"), m)
                                    act.activation(t_["eq"][r][:, :, :], t_["cr"][r][:, :, :], ACT.Exp)\
                                        .then_inc(s(f"eq{r}{b}"), 1)
                                    act.activation(t_["ek"][r][:, :, :], t_["cr"][r][:, :, :], ACT.Exp, scale=-1.0)\
                                        .then_inc(s(f"ek{r}{b}"), 1)
                            for r in range(2):
                                act.wait_ge(s(f"turned{r}{b}"), n)
                                after(act, "pds1", r, b, n, first, 2)
                                act.activation(kst[r][:, :, :], pkst[:, :, :], ACT.Copy).then_inc(s(f"kst{r}{b}"), 1)
                            if st == LAT:
                                for r in range(2):
                                    act.wait_ge(s(f"o_summed{r}{b}"), m)
                                    after(act, "o_stored", r, b, m, first_lat, 16)
                                    act.activation(o[r][:, :], po[r][:, :, :].rearrange("p h n -> p (h n)"), ACT.Copy)\
                                        .then_inc(s(f"o_ready{r}{b}"), 1)

            @block.vector
            def _(dve):
                dve.wait_ge(s("tables"), 32)
                dve.wait_ge(s("zeroed"), 4)

                def chunks(ap):
                    return ap.rearrange("p h (c n) -> p h c n", c=2)

                for st, ta, tb, pairs, before in SCAN:
                    with dve.Fori(0, pairs) as i:
                        n, first = i + (before + 1), before == 0
                        m, first_lat = i + before, before == 1
                        for b in range(2):
                            for r in range(2):
                                t = tile(i, b, r, ta, tb)
                                cv = chunks(cum[:, r, :, ds(t * P, P)])
                                shape = [P, HEADS, 2, CHUNK]
                                after(dve, "el", r, b, n, first)
                                dve.tensor_tensor(chunks(t_["cl"][r][:, :, :]),
                                                  cv[:, :, :, LAST[r]:LAST[r] + 1].to_broadcast(shape), cv,
                                                  ALU.subtract).then_inc(s(f"cl{r}{b}"), 1)
                                if st == LAT:
                                    after(dve, "ek", r, b, m, first_lat)
                                    dve.tensor_tensor(chunks(t_["cr"][r][:, :, :]), cv,
                                                      cv[:, :, :, REF[r]:REF[r] + 1].to_broadcast(shape),
                                                      ALU.subtract).then_inc(s(f"cr{r}{b}"), 1)
                            for r in range(2):
                                t = tile(i, b, r, ta, tb)
                                q = qk[:, 0:HEADS, ds(t * P, P)]
                                k = qk[:, HEADS:2 * HEADS, ds(t * P, P)]
                                dve.wait_ge(s(f"el{r}{b}"), n)
                                after(dve, "turned", r, b, n, first)
                                dve.tensor_tensor(t_["ks"][r][:, :, :], k, t_["el"][r][:, :, :], ALU.mult)\
                                    .then_inc(s(f"ks{r}{b}"), 1)
                                if st == LAT:
                                    dve.wait_ge(s(f"eq{r}{b}"), m)
                                    dve.scalar_tensor_tensor(t_["qi"][r][:, :, :], q, DK ** -0.5,
                                                             t_["eq"][r][:, :, :], ALU.mult, ALU.mult)\
                                        .then_inc(s(f"qi{r}{b}"), 1)
                                    dve.wait_ge(s(f"ek{r}{b}"), m)
                                    dve.tensor_tensor(t_["ki"][r][:, :, :], k, t_["ek"][r][:, :, :], ALU.mult)\
                                        .then_inc(s(f"ki{r}{b}"), 1)
                                dve.wait_ge(s(f"es{r}{b}"), n)
                                if st == LAT:
                                    after(dve, "o_summed", r, b, m, first_lat)
                                    dve.scalar_tensor_tensor(t_["qs"][r][:, :, :], q, DK ** -0.5,
                                                             t_["es"][r][:, :, :], ALU.mult, ALU.mult)\
                                        .then_inc(s(f"qs{r}{b}"), 1)
                            if st == LAT:
                                for r in range(2):
                                    dve.wait_ge(s(f"scored1{b}"), m)
                                    dve.sem_inc(s("score_tiles"), 1)
                                    for c in range(2):
                                        at = slice(c * CHUNK, (c + 1) * CHUNK)
                                        dve.copy_predicated(att[r][at, :, at],
                                                            seen[at, r:r + 1, :].to_broadcast([CHUNK, HEADS, CHUNK]),
                                                            patt[at, r, :, :]).then_inc(s(f"masked{r}{b}"), 1)
                            for j in range(2):
                                for r in range(2):
                                    c = order(r)[j]
                                    end = c * CHUNK + LAST[r]
                                    for half in range(2):
                                        dve.wait_ge(s(f"pds{half}{r}{b}"), n * 2 - (1 - j))
                                        if j == 1:
                                            dve.wait_ge(s(f"state{half}{r}{b}"), n * 2 - 1)
                                        else:
                                            after(dve, f"state{half}", r, b, n, first, 2)
                                        for h in range(half * 2, half * 2 + 2):
                                            last = dve.scalar_tensor_tensor(
                                                state[r][:, h, :], state[r][:, h, :], t_["es"][r][:, h, end:end + 1],
                                                pds[:, h, :], ALU.mult, ALU.add)
                                        last.then_inc(s(f"state{half}{r}{b}"), 1)
        ph.close()


def gla_output(nc, d):
    with ExitStack() as ctx:
        ph = Phase(nc, ctx, "wo")
        s = ph.sem
        raw = ph.sb("raw", [P, 2, D])
        w = Split(nc, ctx, "wo_w", [P, KC, D])
        ident = ph.sb("ident", [P, P])
        head_g = ph.sb("head_g", [P, D])
        res_gate = ph.sb("res_gate", [P, D])
        eps = ph.sb("eps", [P, 1])
        o = [[ph.sb(f"o{r}{b}", [P, HEADS, DV]) for b in range(2)] for r in range(2)]
        gate = [ph.sb(f"gate{b}", [P, HEADS, DV]) for b in range(2)]
        x = [ph.sb(f"x{b}", [P, D]) for b in range(2)]
        junk = ph.sb("junk", [P, HEADS, DV])
        stat = ph.sb("stat", [P, 2, 3, HEADS])
        ot = [Split(nc, ctx, f"wo_ot{b}", [P, KC, P]) for b in range(2)]
        y = [ph.sb(f"y{b}", [P, D]) for b in range(2)]
        pt = [ph.ps(f"pt{b}", [P, KC, P]) for b in range(2)]
        py = [ph.ps(f"py{b}", [P, D]) for b in range(2)]
        total = LAT_TILES // 2

        with nc.Block() as block:
            @block.sync
            def _(sp):
                sp.dma_start(ident[:, :], d.ident).then_inc(s("tables"), 16)
                sp.dma_start(head_g[:, :], d.head_g[0, :].partition_broadcast(P)).then_inc(s("tables"), 16)
                sp.dma_start(res_gate[:, :], d.mods[1, LAT, G1, :].partition_broadcast(P)).then_inc(s("tables"), 16)
                for k in range(KC):
                    if k >= 2:
                        sp.wait_ge(s("w_lo"), k - 1)
                    sp.dma_start(raw[:, k % 2, :], d.w_o[k * P:(k + 1) * P, :]).then_inc(s(f"w_loaded{k % 2}"), 16)
                for st, t0, pairs, before in LAT_STREAMS:
                    with sp.Fori(0, pairs) as i:
                        n = i + (before + 1)
                        for b in range(2):
                            row = (i * 2 + (t0 + b - CTX_TILES)) * P
                            if before:
                                sp.wait_ge(s(f"turned{b}"), n - 1)
                            for r in range(2):
                                sp.dma_start(o[r][b][:, :, :].rearrange("p h n -> p (h n)"), d.od[r, ds(row, P), :])\
                                    .then_inc(s(f"o_loaded{b}"), 16)
                            sp.dma_start(gate[b][:, :, :].rearrange("p h n -> p (h n)"), d.gd[ds(row, P), :])\
                                .then_inc(s(f"o_loaded{b}"), 16)
                            if before:
                                sp.wait_ge(s(f"stored{b}"), (n - 1) * 16)
                            sp.dma_start(x[b][:, :], d.xs[ds(row + CTX_LEN, P), :]).then_inc(s(f"x_loaded{b}"), 16)

            @block.gpsimd
            def _(pool):
                for st, t0, pairs, before in LAT_STREAMS:
                    with pool.Fori(0, pairs) as i:
                        for b in range(2):
                            pool.wait_ge(s(f"x_ready{b}"), i + (before + 1))
                            pool.dma_start(d.xs[ds((i * 2 + (t0 + b)) * P, P), :], x[b][:, :])\
                                .then_inc(s(f"stored{b}"), 16)
                for b in range(2):
                    pool.wait_ge(s(f"stored{b}"), 16 * total)

            @block.tensor
            def _(pe):
                pe.wait_ge(s("tables"), 48)
                pe.wait_ge(s("w_lo"), KC)
                for st, t0, pairs, before in LAT_STREAMS:
                    with pe.Fori(0, pairs) as i:
                        n = i + (before + 1)
                        for b in range(2):
                            pe.wait_ge(s(f"gated{b}"), n)
                            if before:
                                pe.wait_ge(s(f"ot_lo{b}"), n - 1)
                            for k in range(KC):
                                h, c = divmod(k * P, DV)
                                last = pe.transpose(pt[b][:, k, :], o[0][b][:, h, c:c + P], ident[:, :])
                            last.then_inc(s(f"turned{b}"), 1)
                        for b in range(2):
                            pe.wait_ge(s(f"ot_lo{b}"), n)
                            if before:
                                pe.wait_ge(s(f"y_gated{b}"), n - 1)
                            for h in range(2):
                                cols = slice(h * N, (h + 1) * N)
                                for k in range(KC):
                                    last = product3(pe, py[b][:, cols], ot[b].hi[:, k, :], ot[b].lo[:, k, :],
                                                    w.hi[:, k, cols], w.lo[:, k, cols], k == 0, k == KC - 1)
                            last.then_inc(s(f"y_ready{b}"), 1)

            @block.scalar
            def _(act):
                act.preload_act_table(ACT.Sqrt)
                for k in range(KC):
                    act.wait_ge(s(f"w_loaded{k % 2}"), 16 * (k // 2 + 1))
                    act.activation(w.hi[:, k, :], raw[:, k % 2, :], ACT.Copy).then_inc(s("w_hi"), 1)
                act.wait_ge(s("eps_set"), 1)
                for st, t0, pairs, before in LAT_STREAMS:
                    with act.Fori(0, pairs) as i:
                        n = i + (before + 1)
                        for b in range(2):
                            act.wait_ge(s(f"o_added{b}"), n)
                            for h in range(HEADS):
                                last = act.activation(junk[:, h, :], o[0][b][:, h, :], ACT.Square,
                                                      accum_out=stat[:, b, 0, h:h + 1])
                            last.then_inc(s(f"squares{b}"), 1)
                            act.wait_ge(s(f"squares{b}"), n)
                            if before:
                                act.wait_ge(s(f"rstd{b}"), n - 1)
                            act.activation(stat[:, b, 1, :], stat[:, b, 0, :], ACT.Sqrt, bias=eps[:, :],
                                           scale=1.0 / DV).then_inc(s(f"root{b}"), 1)
                        for b in range(2):
                            act.wait_ge(s(f"turned{b}"), n)
                            if before:
                                act.wait_ge(s(f"y_ready{b}"), n - 1)
                            act.activation(ot[b].hi[:, :, :], pt[b][:, :, :], ACT.Copy).then_inc(s(f"ot_hi{b}"), 1)

            @block.vector
            def _(dve):
                dve.memset(eps[:, :], EPS).then_inc(s("eps_set"), 1)
                for k in range(KC):
                    dve.wait_ge(s("w_hi"), k + 1)
                    dve.tensor_tensor(w.lo[:, k, :], raw[:, k % 2, :], w.hi[:, k, :].bitcast(F32), ALU.subtract)\
                        .then_inc(s("w_lo"), 1)
                dve.wait_ge(s("tables"), 48)
                for st, t0, pairs, before in LAT_STREAMS:
                    with dve.Fori(0, pairs) as i:
                        n = i + (before + 1)
                        for b in range(2):
                            dve.wait_ge(s(f"o_loaded{b}"), n * 48)
                            dve.tensor_tensor(o[0][b][:, :, :], o[0][b][:, :, :], o[1][b][:, :, :], ALU.add)\
                                .then_inc(s(f"o_added{b}"), 1)
                            dve.tensor_tensor(gate[b][:, :, :].rearrange("p h n -> p (h n)"),
                                              gate[b][:, :, :].rearrange("p h n -> p (h n)"), head_g[:, :], ALU.mult)\
                                .then_inc(s(f"gain{b}"), 1)
                        for b in range(2):
                            dve.wait_ge(s(f"root{b}"), n)
                            dve.reciprocal(stat[:, b, 2, :], stat[:, b, 1, :]).then_inc(s(f"rstd{b}"), 1)
                            dve.wait_ge(s(f"rstd{b}"), n)
                            dve.wait_ge(s(f"gain{b}"), n)
                            for h in range(HEADS):
                                last = dve.scalar_tensor_tensor(o[0][b][:, h, :], o[0][b][:, h, :],
                                                                stat[:, b, 2, h:h + 1], gate[b][:, h, :],
                                                                ALU.mult, ALU.mult)
                            last.then_inc(s(f"gated{b}"), 1)
                        for b in range(2):
                            dve.wait_ge(s(f"ot_hi{b}"), n)
                            dve.tensor_tensor(ot[b].lo[:, :, :], pt[b][:, :, :], ot[b].hi[:, :, :].bitcast(F32),
                                              ALU.subtract).then_inc(s(f"ot_lo{b}"), 1)
                        for b in range(2):
                            dve.wait_ge(s(f"y_ready{b}"), n)
                            dve.tensor_tensor(y[b][:, :], py[b][:, :], res_gate[:, :], ALU.mult)\
                                .then_inc(s(f"y_gated{b}"), 1)
                            dve.wait_ge(s(f"y_gated{b}"), n)
                            dve.wait_ge(s(f"x_loaded{b}"), n * 16)
                            dve.tensor_tensor(x[b][:, :], x[b][:, :], y[b][:, :], ALU.add)\
                                .then_inc(s(f"x_ready{b}"), 1)
        ph.close()

MAX_BLOCKS = 2 * TILES + EXPERTS
OUT_SHAPE = (1, SEQ, D)


def moe(nc, d, layer, streams, final):
    with ExitStack() as ctx:
        plan = Plan(nc, ctx, layer, TILES - streams[0][1])
        with ExitStack() as inner:
            ht = Split(nc, inner, f"ht_moe{layer}", [P, KC, TOK])
            normalise(nc, d, layer, 1, streams, ht, d.hd)
            route(nc, d, layer, streams, ht, plan)
        experts(nc, d, layer, plan)
        combine(nc, d, layer, streams, plan, final)


def conv_layer(nc, d, cs):
    with ExitStack() as ctx:
        vt = ctx.enter_context(nc.sbuf_tensor("taps_out", [P, KC, CONV_OUT], F32))
        vecs = ctx.enter_context(nc.sbuf_tensor("channel_vectors", [P, KC, VEC_ROWS], F32))
        with ExitStack() as inner:
            ht = Split(nc, inner, "ht_conv", [P, KC, TOK])
            normalise(nc, d, 0, 0, STREAMS, ht)
            conv_taps(nc, d, ht, vt, vecs, cs)
        conv_out(nc, d, vt, vecs)


def gla_layer(nc, d):
    with ExitStack() as ctx, ExitStack() as rows:
        ht = Split(nc, rows, "ht_gla", [P, KC, TOK], side="right")
        normalise(nc, d, 1, 0, STREAMS, ht)
        gla_values(nc, d, ht)
        qk = ctx.enter_context(nc.sbuf_tensor("qk", [P, 2 * HEADS, TOK], F32))
        cum = ctx.enter_context(nc.sbuf_tensor("cum", [P, 2, HEADS, TOK], F32))
        gla_keys(nc, d, ht, qk, cum)
        rows.close()
        gla_scan(nc, d, qk, cum)
    gla_output(nc, d)


def program(nc, d):
    Phase.pool_dma = []
    with ExitStack() as ctx:
        cs = ctx.enter_context(nc.sbuf_tensor("silu_c", [P, KC, 2], F32))
        modulation(nc, d, cs)
        conv_layer(nc, d, cs)
    moe(nc, d, 0, STREAMS, False)
    gla_layer(nc, d)
    moe(nc, d, 1, LAT_STREAMS, True)


class Dram:

    def __init__(self, nc, a, out):
        def scratch(name, shape, dt=F32):
            return nc.dram_tensor("scratch_" + name, shape, dt, kind="Internal").ap()

        self.x, self.c, self.ctx, self.c_ctx = a["in_x"], a["in_c"], a["in_ctx"], a["in_c_ctx"]
        self.ada_w, self.ada_b, self.norm_g, self.final_g = a["in_ada_w"], a["in_ada_b"], a["in_norm_g"], a["in_final_g"]
        self.pw1_w, self.pw1_b = a["in_conv_pw1_w"][0], a["in_conv_pw1_b"]
        self.dw_w, self.dw_b = a["in_conv_dw_w"][0], a["in_conv_dw_b"]
        self.ln_g, self.ln_b = a["in_conv_ln_g"], a["in_conv_ln_b"]
        self.pw2_w, self.pw2_b = a["in_conv_pw2_w"][0], a["in_conv_pw2_b"]
        self.w_in, self.gk_up, self.gk_b = a["in_gla_w_in"][0], a["in_gla_gk_up"][0], a["in_gla_gk_b"][0]
        self.head_g, self.w_o = a["in_gla_head_g"], a["in_gla_w_o"][0]
        self.wg, self.bg, self.wr, self.br = a["in_moe_wg"], a["in_moe_bg"], a["in_moe_wr"], a["in_moe_br"]
        self.w1, self.w3, self.w2 = a["in_moe_w1"], a["in_moe_w3"], a["in_moe_w2"]
        self.pos_row, self.pos_col, self.ident = a["const_pos_row"], a["const_pos_col"], a["const_ident"]
        self.mean_w, self.ones, self.before = a["const_mean_w"], a["const_ones"], a["const_before"]
        self.iota, self.token = a["const_iota"], a["const_token"]
        self.cums, self.seen = a["const_cums"], a["const_seen"]
        self.out = out if len(out.shape) == 2 else out[0]
        self.xs = scratch("residual", (TOK, D))
        self.mods = scratch("modulation", (2, 2, 6, D))
        self.hd = scratch("experts_in", (TOK, D))
        self.vd = scratch("gla_values", (TOK, D))
        self.gd = scratch("gla_gates", (SEQ, D))
        self.od = scratch("gla_out", (2, SEQ, D))
        self.yd = scratch("experts_out", (MAX_BLOCKS * BLK, D))


_INS = ['x', 'c', 'ctx', 'c_ctx', 'ada_w', 'ada_b', 'norm_g', 'final_g', 'conv_pw1_w', 'conv_pw1_b', 'conv_dw_w',
        'conv_dw_b', 'conv_ln_g', 'conv_ln_b', 'conv_pw2_w', 'conv_pw2_b', 'gla_w_in', 'gla_gk_up', 'gla_gk_b',
        'gla_head_g', 'gla_w_o', 'moe_wg', 'moe_bg', 'moe_wr', 'moe_br', 'moe_w1', 'moe_w3', 'moe_w2']


def shape_tables():
    quarter = D // 4
    omega = (1.0 / (10000.0 ** (np.arange(quarter, dtype=np.float32) / np.float32(quarter)))).astype(np.float32)
    ar = np.arange(SEQ // GRID_W, dtype=np.float32)[:, None] * omega
    ac = np.arange(GRID_W, dtype=np.float32)[:, None] * omega
    k = np.arange(P)
    same = (k[:, None] // CHUNK) == (k[None, :] // CHUNK)
    return {
        'pos_row': np.concatenate([np.sin(ar), np.cos(ar)], axis=1).astype(np.float32),
        'pos_col': np.concatenate([np.sin(ac), np.cos(ac)], axis=1).astype(np.float32),
        'ident': np.eye(P, dtype=np.float32),
        'mean_w': np.full((P, P), 1.0 / D, np.float32),
        'ones': np.ones((P, P), np.float32),
        'before': (k[:, None] < k[None, :]).astype(np.float32),
        'iota': np.broadcast_to(np.arange(P, dtype=np.float32), (P, P)).copy(),
        'token': (np.arange(TILES, dtype=np.float32)[None, :] * P + k[:, None].astype(np.float32)).astype(np.float32),
        'cums': np.stack([(same & (k[:, None] <= k[None, :])).astype(np.float32) / 16.0,
                          (same & (k[:, None] >= k[None, :])).astype(np.float32) / 16.0], axis=1),
        'seen': np.stack([np.tile((k[:CHUNK, None] <= k[None, :CHUNK]), (2, 1)),
                          np.tile((k[:CHUNK, None] >= k[None, :CHUNK]), (2, 1))], axis=1).astype(np.int32),
    }


def kernel(**inputs):
    import concourse.bacc as _bacc
    from concourse.bass_utils import run_bass_kernel_spmd as _run

    nc = _bacc.Bacc("TRN2", target_bir_lowering=False, num_devices=1)
    arrays, args = {}, {}
    for name in _INS:
        arrays["in_" + name] = np.ascontiguousarray(inputs[name])
    for name, table in shape_tables().items():
        arrays["const_" + name] = np.ascontiguousarray(table)
    for name, a in arrays.items():
        args[name] = nc.dram_tensor(name, a.shape, mybir.dt.from_np(a.dtype), kind="ExternalInput").ap()
    out = nc.dram_tensor("out", OUT_SHAPE, F32, kind="ExternalOutput").ap()
    program(nc, Dram(nc, args, out))
    r = _run(nc, [arrays], core_ids=[0])
    return r.results[0]["out"]
```

```python
import concourse.bass as bass
from concourse import mybir
import numpy as np
from contextlib import ExitStack

F32 = mybir.dt.float32
F32R = mybir.dt.float32r
I32 = mybir.dt.int32
U32 = mybir.dt.uint32
ACT = mybir.ActivationFunctionType
ALU = mybir.AluOpType
AX = mybir.AxisListType
ds = bass.ds

P = 128
D = 1024
KC = D // P
SEQ, CTX_LEN, GRID_W = 1024, 256, 64
TOK = SEQ + CTX_LEN
TILES = TOK // P
CTX_TILES = CTX_LEN // P
N = 512
EPS = 1e-6
TAPS, PAD = 31, 15
HEADS, DK, DV, CHUNK, RANK = 4, 128, 256, 64, 16
GLA_IN = 2 * HEADS * DK + 2 * HEADS * DV + 2 * RANK
GROUPS, PER_GROUP, EXPERTS, FF, BLK = 4, 8, 32, 512, 128
LAT, CTX = 0, 1
SH1, SC1, G1, SH2, SC2, G2 = range(6)
STREAMS = [(CTX, 0, CTX_TILES // 2, 0), (LAT, CTX_TILES, (TILES - CTX_TILES) // 2, CTX_TILES // 2)]
LAT_STREAMS = [(LAT, CTX_TILES, 1, 0), (LAT, CTX_TILES + 2, (TILES - CTX_TILES) // 2 - 1, 1)]
GAP = PAD + CTX_LEN + PAD
CONV_GROUPS = [(0, CTX_LEN, PAD), (CTX_LEN, N, GAP), (CTX_LEN + N, N, GAP + N)]
CONV_W = GAP + SEQ + PAD
CONV_OUT = GAP + SEQ - PAD
VEC_ROWS = TAPS + 5
V_DWB, V_LNG, V_LNB, V_BA, V_BG = range(TAPS, VEC_ROWS)


class Phase:
    POOL_DMA = ("stored", "h_stored", "o_stored", "gathered")
    pool_dma = []

    def __init__(self, nc, ctx, name):
        self.pool_used = 0
        self.nc, self.ctx, self.name, self.sems = nc, ctx, name, {}

    def sb(self, name, shape, dt=F32):
        return self.ctx.enter_context(self.nc.sbuf_tensor(f"{self.name}_{name}", shape, dt))

    def ps(self, name, shape, dt=F32):
        return self.ctx.enter_context(self.nc.psum_tensor(f"{self.name}_{name}", shape, dt))

    def sem(self, name):
        if name not in self.sems and name.rstrip("01234567") in self.POOL_DMA:
            if self.pool_used == len(self.pool_dma):
                self.pool_dma.append(self.nc.alloc_semaphore(f"pool_dma{self.pool_used}"))
            self.sems[name] = self.pool_dma[self.pool_used]
            self.pool_used += 1
        if name not in self.sems:
            self.sems[name] = self.ctx.enter_context(self.nc.semaphore(f"{self.name}_{name}"))
        return self.sems[name]

    def close(self):
        numbers = sorted(sem.num for sem in self.sems.values())
        with self.nc.Block() as block:
            @block.gpsimd
            def _(pool):
                for sem in self.pool_dma[:self.pool_used]:
                    pool.dma_reset(range(sem.num, sem.num + 1))
                start = numbers[0]
                for at, num in enumerate(numbers):
                    if at + 1 == len(numbers) or numbers[at + 1] != num + 1:
                        pool.sem_clear(range(start, num + 1))
                        start = numbers[min(at + 1, len(numbers) - 1)]


def chain(ph, eng, name):
    done = [0]

    def link(ins):
        done[0] += 1
        ins.then_inc(ph.sem(name), 1)
        eng.wait_ge(ph.sem(name), done[0])
    return link


def product3(pe, out, xh, xl, wh, wl, start, stop):
    pe.matmul(out, xh, wh, start=start, stop=False)
    pe.matmul(out, xh, wl, start=False, stop=False)
    return pe.matmul(out, xl, wh, start=False, stop=stop)


class Split:

    def __init__(self, nc, ctx, name, shape, side="left"):
        self.hi = ctx.enter_context(nc.sbuf_tensor(name + "_hi", shape, F32R, side=side))
        self.lo = ctx.enter_context(nc.sbuf_tensor(name + "_lo", shape, F32R, side=side))


class SquareWeights:
    SLOTS = 4

    def __init__(self, ph, nc, ctx, name, dram):
        self.ph, self.dram = ph, dram
        self.raw = ph.sb("w_raw", [P, self.SLOTS, D])
        self.w = Split(nc, ctx, name, [P, KC, D])

    def load(self, sp):
        s = self.ph.sem
        for k in range(KC):
            if k >= self.SLOTS:
                sp.wait_ge(s(f"w_lo{k % 2}"), (k - self.SLOTS) // 2 + 1)
            sp.dma_start(self.raw[:, k % self.SLOTS, :], self.dram[k * P:(k + 1) * P, :])\
                .then_inc(s(f"w_loaded{k % self.SLOTS}"), 16)

    def high(self, act):
        s = self.ph.sem
        for k in range(KC):
            act.wait_ge(s(f"w_loaded{k % self.SLOTS}"), 16 * (k // self.SLOTS + 1))
            act.activation(self.w.hi[:, k, :], self.raw[:, k % self.SLOTS, :], ACT.Copy).then_inc(s("w_hi"), 1)

    def low(self, eng, odd):
        s = self.ph.sem
        for k in range(odd, KC, 2):
            eng.wait_ge(s("w_hi"), k + 1)
            eng.tensor_tensor(self.w.lo[:, k, :], self.raw[:, k % self.SLOTS, :], self.w.hi[:, k, :].bitcast(F32),
                              ALU.subtract).then_inc(s(f"w_lo{odd}"), 1)

    def wait(self, pe):
        for odd in range(2):
            pe.wait_ge(self.ph.sem(f"w_lo{odd}"), KC // 2)


def modulation(nc, d, cs):
    with ExitStack() as ctx:
        ph = Phase(nc, ctx, "ada")
        s = ph.sem
        rows = (SH1, SC1)
        craw = ph.sb("craw", [P, 2, KC])
        w = [ph.sb(f"w{m}", [P, KC, D]) for m in rows]
        row = ph.sb("row", [2, len(rows), D])
        bias = ph.sb("bias", [2, len(rows), D])
        acc = [ph.ps(f"acc{m}", [P, D]) for m in rows]
        xin = [ph.sb(f"xin{b}", [P, D]) for b in range(4)]
        pos_row = [ph.sb(f"pos_row{b}", [P, N]) for b in range(4)]
        pos_col = ph.sb("pos_col", [P, N])
        lat_tiles = TILES - CTX_TILES

        with nc.Block() as block:
            @block.sync
            def _(sp):
                for k, src in enumerate((d.c[0, :], d.c_ctx)):
                    sp.dma_start(craw[:, k, :], src.rearrange("(p k) -> p k", k=KC)).then_inc(s("c_loaded"), 16)
                for m in rows:
                    for h in range(2):
                        cols = slice(h * N, (h + 1) * N)
                        sp.dma_start(w[m][:, :, cols], d.ada_w[0, :, m * D + h * N:m * D + (h + 1) * N]
                                     .rearrange("(p k) n -> p k n", k=KC)).then_inc(s(f"w_loaded{m}{h}"), 16)
                sp.dma_start(bias[:, :, :].rearrange("o m n -> o (m n)"),
                             d.ada_b[0, 0:len(rows) * D].partition_broadcast(2)).then_inc(s("b_loaded"), 16)
                for t in range(lat_tiles):
                    sp.wait_ge(s("x_added"), 2 * (t + 1))
                    sp.dma_start(d.xs[CTX_LEN + t * P:CTX_LEN + (t + 1) * P, :], xin[t % 4][:, :])\
                        .then_inc(s(f"x_stored{t % 4}"), 16)
                sp.wait_ge(s("rows_done"), len(rows))
                for k, stream in enumerate((LAT, CTX)):
                    sp.dma_start(d.mods[0, stream, 0:len(rows), :], row[k:k + 1, :, :]).then_inc(s("mods_stored"), 16)
                sp.wait_ge(s("mods_stored"), 32)
                for b in range(4):
                    sp.wait_ge(s(f"x_stored{b}"), 16 * (lat_tiles // 4))

            @block.scalar
            def _(act):
                act.wait_ge(s("c_loaded"), 32)
                act.activation(cs[:, :, :].rearrange("p k s -> p s k"), craw[:, :, :], ACT.Silu)\
                    .then_inc(s("c_ready"), 1)
                act.dma_start(d.xs[0:CTX_LEN, :], d.ctx[0, :, :]).then_inc(s("ctx_copied"), 16)
                for h in range(P // GRID_W):
                    act.dma_start(pos_col[h * GRID_W:(h + 1) * GRID_W, :], d.pos_col).then_inc(s("col_loaded"), 16)
                for t in range(lat_tiles):
                    b = t % 4
                    if t >= 4:
                        act.wait_ge(s(f"x_stored{b}"), 16 * (t // 4))
                    act.dma_start(xin[b][:, :], d.x[0, t * P:(t + 1) * P, :]).then_inc(s(f"x_loaded{b}"), 16)
                    for h in range(P // GRID_W):
                        r = t * (P // GRID_W) + h
                        act.dma_start(pos_row[b][h * GRID_W:(h + 1) * GRID_W, :],
                                      d.pos_row[r, :].partition_broadcast(GRID_W)).then_inc(s(f"x_loaded{b}"), 16)
                act.wait_ge(s("ctx_copied"), 16)

            @block.tensor
            def _(pe):
                pe.wait_ge(s("c_ready"), 1)
                for m in rows:
                    for h in range(2):
                        pe.wait_ge(s(f"w_loaded{m}{h}"), 16)
                        for k in range(KC):
                            last = pe.matmul(acc[m][0:2, h * N:(h + 1) * N], cs[:, k, :],
                                             w[m][:, k, h * N:(h + 1) * N], start=k == 0, stop=k == KC - 1)
                    last.then_inc(s("acc_ready"), 1)

            @block.vector
            def _(dve):
                dve.wait_ge(s("col_loaded"), 32)
                for t in range(lat_tiles):
                    b = t % 4
                    dve.wait_ge(s(f"x_loaded{b}"), 48 * (t // 4 + 1))
                    for half, table in ((0, pos_row[b]), (1, pos_col)):
                        cols = slice(half * N, (half + 1) * N)
                        dve.tensor_tensor(xin[b][:, cols], xin[b][:, cols], table[:, :], ALU.add)\
                            .then_inc(s("x_added"), 1)
                dve.wait_ge(s("b_loaded"), 16)
                for m in rows:
                    dve.wait_ge(s("acc_ready"), m + 1)
                    dve.tensor_tensor(row[:, m, :], acc[m][0:2, :], bias[:, m, :], ALU.add).then_inc(s("rows_done"), 1)
        ph.close()


def norm_stage(ph, d, layer, which, streams, ht, hd):
    s = ph.sem
    x = [ph.sb(f"x{b}", [P, D]) for b in range(2)]
    h = [ph.sb(f"h{b}", [P, D]) for b in range(2)]
    junk = ph.sb("junk", [P, D])
    stat = ph.sb("stat", [P, 2, 4])
    eps = ph.sb("eps", [P, 1])
    scale = ph.sb("scale", [P, 2, D])
    shift = ph.sb("shift", [P, 2, D])
    gain = ph.sb("gain", [P, D])
    ident = ph.sb("ident", [P, P])
    pt = [ph.ps(f"pt{b}", [P, KC, P]) for b in range(2)]
    sh_row, sc_row = (SH1, SC1) if which == 0 else (SH2, SC2)
    total = sum(pairs for _, _, pairs, _ in streams)
    used = sorted({st for st, _, _, _ in streams}, reverse=True)

    def sync(sp):
        for st, t0, pairs, before in streams:
            with sp.Fori(0, pairs) as i:
                for b in range(2):
                    row = (i * 2 + (t0 + b)) * P
                    if before:
                        sp.wait_ge(s(f"scaled{b}"), i + before)
                    sp.dma_start(x[b][:, :], d.xs[ds(row, P), :]).then_inc(s(f"x_loaded{b}"), 16)

    def pool(pl):
        if hd is None:
            return
        for st, t0, pairs, before in streams:
            with pl.Fori(0, pairs) as i:
                for b in range(2):
                    row = (i * 2 + (t0 + b)) * P
                    pl.wait_ge(s(f"h_ready{b}"), i + (before + 1))
                    pl.dma_start(hd[ds(row, P), :], h[b][:, :]).then_inc(s(f"h_stored{b}"), 16)
        for b in range(2):
            pl.wait_ge(s(f"h_stored{b}"), 16 * sum(p for _, _, p, _ in streams))

    def scalar(act):
        act.dma_start(gain[:, :], d.norm_g[layer, which, :].partition_broadcast(P)).then_inc(s("gain_loaded"), 16)
        for st in used:
            act.dma_start(scale[:, st, :], d.mods[layer, st, sc_row, :].partition_broadcast(P))\
                .then_inc(s(f"rows_loaded{st}"), 16)
            act.dma_start(shift[:, st, :], d.mods[layer, st, sh_row, :].partition_broadcast(P))\
                .then_inc(s(f"rows_loaded{st}"), 16)
            if st == used[0]:
                act.dma_start(ident[:, :], d.ident).then_inc(s("ident"), 16)
        act.preload_act_table(ACT.Sqrt)
        act.wait_ge(s("eps_set"), 1)

        def root(b, n):
            act.wait_ge(s(f"x_loaded{b}"), n * 16)
            act.activation(junk[:, :], x[b][:, :], ACT.Square, accum_out=stat[:, b, 0:1])\
                .then_inc(s(f"squares{b}"), 1)
            act.wait_ge(s(f"squares{b}"), n)
            act.activation(stat[:, b, 1:2], stat[:, b, 0:1], ACT.Sqrt, bias=eps[:, :], scale=1.0 / D)\
                .then_inc(s(f"root{b}"), 1)

        def high(b, n, tile):
            act.wait_ge(s(f"t_ready{b}"), n)
            act.activation(ht.hi[:, :, ds(tile * P, P)], pt[b][:, :, :], ACT.Copy).then_inc(s(f"ht_hi{b}"), 1)

        for st, t0, pairs, before in streams:
            with act.Fori(0, pairs) as i:
                n, tile = i + (before + 1), i * 2 + t0
                root(0, n)
                if before:
                    high(1, n - 1, tile - 1)
                root(1, n)
                high(0, n, tile)
        high(1, total, TILES - 1)

    def vector(dve):
        dve.memset(eps[:, :], EPS).then_inc(s("eps_set"), 1)
        dve.wait_ge(s("gain_loaded"), 16)

        def full_scale(st):
            dve.wait_ge(s(f"rows_loaded{st}"), 32)
            dve.scalar_tensor_tensor(scale[:, st, :], scale[:, st, :], 1.0, gain[:, :], ALU.add, ALU.mult)\
                .then_inc(s("scale_ready"), 1)
            dve.wait_ge(s("scale_ready"), used.index(st) + 1)

        def norm(b, n, st, before):
            dve.wait_ge(s(f"root{b}"), n)
            dve.reciprocal(stat[:, b, 2:3], stat[:, b, 1:2]).then_inc(s(f"rstd{b}"), 1)
            dve.wait_ge(s(f"rstd{b}"), n)
            if before:
                dve.wait_ge(s(f"t_ready{b}"), n - 1)
                if hd is not None:
                    dve.wait_ge(s(f"h_stored{b}"), (n - 1) * 16)
            dve.scalar_tensor_tensor(h[b][:, :], x[b][:, :], stat[:, b, 2:3], scale[:, st, :],
                                     ALU.mult, ALU.mult).then_inc(s(f"scaled{b}"), 1)
            dve.wait_ge(s(f"scaled{b}"), n)
            dve.tensor_tensor(h[b][:, :], h[b][:, :], shift[:, st, :], ALU.add).then_inc(s(f"h_ready{b}"), 1)

        def low(b, n, tile):
            dve.wait_ge(s(f"ht_hi{b}"), n)
            dve.tensor_tensor(ht.lo[:, :, ds(tile * P, P)], pt[b][:, :, :],
                              ht.hi[:, :, ds(tile * P, P)].bitcast(F32), ALU.subtract).then_inc(s(f"ht_lo{b}"), 1)

        for at, (st, t0, pairs, before) in enumerate(streams):
            if at == 0 or st != streams[at - 1][0]:
                full_scale(st)
            with dve.Fori(0, pairs) as i:
                n, tile = i + (before + 1), i * 2 + t0
                norm(0, n, st, before)
                if before:
                    low(1, n - 1, tile - 1)
                norm(1, n, st, before)
                low(0, n, tile)
        low(1, total, TILES - 1)

    def tensor(pe):
        pe.wait_ge(s("ident"), 16)
        for st, t0, pairs, before in streams:
            with pe.Fori(0, pairs) as i:
                n = i + (before + 1)
                for b in range(2):
                    pe.wait_ge(s(f"h_ready{b}"), n)
                    if before:
                        pe.wait_ge(s(f"ht_lo{b}"), n - 1)
                    for k in range(KC):
                        last = pe.transpose(pt[b][:, k, :], h[b][:, k * P:(k + 1) * P], ident[:, :])
                    last.then_inc(s(f"t_ready{b}"), 1)

    return sync, pool, scalar, vector, tensor


def normalise(nc, d, layer, which, streams, ht, hd=None):
    with ExitStack() as ctx:
        ph = Phase(nc, ctx, f"norm{layer}{which}")
        sync, pool, scalar, vector, tensor = norm_stage(ph, d, layer, which, streams, ht, hd)
        with nc.Block() as block:
            block.sync(sync)
            block.gpsimd(pool)
            block.scalar(scalar)
            block.vector(vector)
            block.tensor(tensor)
        ph.close()


ADA_UNITS = [(0, 0, 2, 0, 2 * D), (0, 0, 2, 1, 2 * D), (0, 1, 3, 0, 0), (1, 1, 3, 1, 0), (1, 1, 3, 2, 0)]


def conv_taps(nc, d, ht, vt, vecs, cs):
    with ExitStack() as ctx:
        ph = Phase(nc, ctx, "taps")
        s = ph.sem
        raw = [ph.sb(f"raw{b}", [P, KC, 2, P]) for b in range(2)]
        w = Split(nc, ctx, "taps_w", [P, KC, 2, P])
        ada_w = [ph.sb(f"ada_w{h}", [P, KC // 2, N]) for h in range(2)]
        ada_b = ph.sb("ada_b", [2, N])
        ada_sum = ph.sb("ada_sum", [2, N])
        ada_row = ph.sb("ada_row", [2, N])
        ada_acc = ph.ps("ada_acc", [P, N])
        rows = ph.sb("rows", [VEC_ROWS, D])
        ident = ph.sb("ident", [P, P])
        vec = [ph.sb(f"vec{b}", [P, VEC_ROWS]) for b in range(2)]
        sg = [ph.sb(f"sg{g}", [P, N]) for g in range(3)]
        u = [ph.sb(f"u{b}", [P, CONV_W]) for b in range(2)]
        acc = [ph.sb(f"acc{b}", [P, CONV_OUT]) for b in range(2)]
        za = [ph.ps(f"za{g}", [P, N]) for g in range(3)]
        zg = [ph.ps(f"zg{g}", [P, N]) for g in range(3)]
        pv = ph.ps("pv", [P, KC, VEC_ROWS])
        pairs = KC // 2

        with nc.Block() as block:
            @block.sync
            def _(sp):
                sp.dma_start(ident[:, :], d.ident).then_inc(s("rows_loaded"), 16)
                for r0, src in ((0, d.dw_w), (V_DWB, d.dw_b), (V_LNG, d.ln_g), (V_LNB, d.ln_b)):
                    n = src.shape[0]
                    sp.dma_start(rows[r0:r0 + n, :], src).then_inc(s("rows_loaded"), 16)
                sp.dma_start(rows[V_BA:V_BG + 1, :], d.pw1_b.rearrange("o (h n) -> (o h) n", h=2))\
                    .then_inc(s("rows_loaded"), 16)

                def load(b, i):
                    for h in range(2):
                        src = d.pw1_w[:, ds((i * 2 + b) * P + h * D, P)].rearrange("(k p) n -> p k n", p=P)
                        sp.dma_start(raw[b][:, :, h, :], src).then_inc(s(f"w_loaded{b}"), 16)

                def load_unit(j, i, first):
                    _, l, per, at, c0 = ADA_UNITS[j]
                    u = i * len(ADA_UNITS) + j
                    col = (i * per + at) * N + c0
                    for h in range(2):
                        if not (first and j == 0):
                            sp.wait_ge(s(f"ada_used{h}"), u)
                        half = slice(h * (KC // 2), (h + 1) * (KC // 2))
                        sp.dma_start(ada_w[h][:, :, :], d.ada_w[l, :, ds(col, N)]
                                     .rearrange("(p k) n -> p k n", k=KC)[:, half, :]).then_inc(s(f"ada_loaded{h}"), 16)
                    if not (first and j == 0):
                        sp.wait_ge(s("ada_out"), u)
                    sp.dma_start(ada_b[:, :], d.ada_b[l, ds(col, N)].partition_broadcast(2))\
                        .then_inc(s("ada_b_loaded"), 16)

                def pair(i, first, last):
                    for b in range(2):
                        for j, unit in enumerate(ADA_UNITS):
                            if unit[0] == b:
                                load_unit(j, i, first)
                        if not last:
                            sp.wait_ge(s(f"w_lo{b}"), i + 1)
                            load(b, i + 1)

                for b in range(2):
                    load(b, 0)
                pair(0, True, False)
                with sp.Fori(1, pairs - 1) as i:
                    pair(i, False, False)
                pair(pairs - 1, False, True)

            @block.gpsimd
            def _(pool):
                for b in range(2):
                    pool.memset(u[b][:, :], 0.0).then_inc(s("u_zero"), 1)

                def low(b, i):
                    pool.wait_ge(s(f"w_hi{b}"), i + 1)
                    pool.tensor_tensor(w.lo[:, :, :, :], raw[b][:, :, :, :], w.hi[:, :, :, :].bitcast(F32),
                                       ALU.subtract).then_inc(s(f"w_lo{b}"), 1)

                def gate(b, i):
                    for g, (t0, n, c0) in enumerate(CONV_GROUPS):
                        pool.wait_ge(s(f"sig_ready{g}{b}"), i + 1)
                        pool.wait_ge(s(f"a_ready{g}{b}"), i + 1)
                        pool.tensor_tensor(u[b][:, c0:c0 + n], u[b][:, c0:c0 + n], sg[g][:, 0:n], ALU.mult)\
                            .then_inc(s(f"u_ready{g}{b}"), 1)

                def units_out(b, i, first):
                    for j, (when, l, per, at, c0) in enumerate(ADA_UNITS):
                        if when != b:
                            continue
                        u = i * len(ADA_UNITS) + j
                        pool.wait_ge(s("ada_b_loaded"), (u + 1) * 16)
                        pool.wait_ge(s("ada_taken"), u + 1)
                        if not (first and j == 0):
                            pool.wait_ge(s("stored"), u * 16)
                        pool.tensor_tensor(ada_row[:, :], ada_sum[:, :], ada_b[:, :], ALU.add)\
                            .then_inc(s("ada_out"), 1)
                        pool.wait_ge(s("ada_out"), u + 1)
                        pool.dma_start(d.mods[l].rearrange("s m n -> s (m n)")[:, ds((i * per + at) * N + c0, N)],
                                       ada_row[:, :]).then_inc(s("stored"), 16)

                low(0, 0)
                gate(0, 0)
                low(1, 0)
                units_out(0, 0, True)
                gate(1, 0)
                with pool.Fori(1, pairs) as i:
                    low(0, i)
                    units_out(1, i - 1, False)
                    gate(0, i)
                    low(1, i)
                    units_out(0, i, False)
                    gate(1, i)
                units_out(1, pairs - 1, False)
                pool.wait_ge(s("stored"), 16 * pairs * len(ADA_UNITS))

            @block.tensor
            def _(pe):
                pe.wait_ge(s("rows_loaded"), 96)
                for k in range(KC):
                    last = pe.transpose(pv[:, k, :], rows[:, k * P:(k + 1) * P], ident[0:VEC_ROWS, 0:VEC_ROWS])
                last.then_inc(s("pv_ready"), 1)

                def chunk(b, i, first):
                    pe.wait_ge(s(f"w_lo{b}"), i + 1)
                    for g, (t0, n, _) in enumerate(CONV_GROUPS):
                        if not (first and b == 0):
                            pe.wait_ge(s(f"a_ready{g}{1 - b}"), i + b)
                        for h, z in ((1, zg[g]), (0, za[g])):
                            for k in range(KC):
                                last = product3(pe, z[:, 0:n], w.hi[:, k, h, :], w.lo[:, k, h, :],
                                                ht.hi[:, k, t0:t0 + n], ht.lo[:, k, t0:t0 + n], k == 0, k == KC - 1)
                        last.then_inc(s(f"z_ready{g}{b}"), 1)

                def units(b, i, first):
                    for j, unit in enumerate(ADA_UNITS):
                        if unit[0] != b:
                            continue
                        u = i * len(ADA_UNITS) + j
                        if not (first and j == 0):
                            pe.wait_ge(s("ada_taken"), u)
                        for h in range(2):
                            pe.wait_ge(s(f"ada_loaded{h}"), (u + 1) * 16)
                            for k in range(KC // 2):
                                last = pe.matmul(ada_acc[0:2, :], cs[:, h * (KC // 2) + k, :], ada_w[h][:, k, :],
                                                 start=h == 0 and k == 0, stop=h == 1 and k == KC // 2 - 1)
                            last.then_inc(s(f"ada_used{h}"), 1)

                for b in range(2):
                    chunk(b, 0, True)
                    units(b, 0, True)
                with pe.Fori(1, pairs) as i:
                    for b in range(2):
                        chunk(b, i, False)
                        units(b, i, False)

            @block.scalar
            def _(act):
                act.preload_act_table(ACT.Sigmoid)
                act.wait_ge(s("u_zero"), 2)

                def high(b, i, first):
                    act.wait_ge(s(f"w_loaded{b}"), i * 32 + 32)
                    if not (first and b == 0):
                        act.wait_ge(s(f"z_ready2{1 - b}"), i + b)
                    act.activation(w.hi[:, :, :, :], raw[b][:, :, :, :], ACT.Copy).then_inc(s(f"w_hi{b}"), 1)

                def take_units(b, i, first):
                    for j, unit in enumerate(ADA_UNITS):
                        if unit[0] != b:
                            continue
                        u = i * len(ADA_UNITS) + j
                        act.wait_ge(s("ada_used1"), u + 1)
                        if not (first and j == 0):
                            act.wait_ge(s("ada_out"), u)
                        act.activation(ada_sum[:, :], ada_acc[0:2, :], ACT.Copy).then_inc(s("ada_taken"), 1)

                def chunk(b, i, first):
                    act.wait_ge(s(f"vec_ready{b}"), i + 1)
                    if not first:
                        act.wait_ge(s("taps_summed"), i * 2 + (b - 1))
                    for g, (t0, n, c0) in enumerate(CONV_GROUPS):
                        act.wait_ge(s(f"z_ready{g}{b}"), i + 1)
                        if not (first and b == 0):
                            act.wait_ge(s(f"u_ready{g}{1 - b}"), i + b)
                        act.activation(sg[g][:, 0:n], zg[g][:, 0:n], ACT.Sigmoid, bias=vec[b][:, V_BG:V_BG + 1])\
                            .then_inc(s(f"sig_ready{g}{b}"), 1)
                        act.activation(u[b][:, c0:c0 + n], za[g][:, 0:n], ACT.Identity, bias=vec[b][:, V_BA:V_BA + 1])\
                            .then_inc(s(f"a_ready{g}{b}"), 1)

                high(0, 0, True)
                chunk(0, 0, True)
                high(1, 0, True)
                take_units(0, 0, True)
                chunk(1, 0, True)
                with act.Fori(1, pairs) as i:
                    high(0, i, False)
                    take_units(1, i - 1, False)
                    chunk(0, i, False)
                    high(1, i, False)
                    take_units(0, i, False)
                    chunk(1, i, False)
                take_units(1, pairs - 1, False)

            @block.vector
            def _(dve):
                dve.wait_ge(s("pv_ready"), 1)
                dve.tensor_copy(vecs[:, :, :], pv[:, :, :]).then_inc(s("vecs_ready"), 1)
                dve.wait_ge(s("vecs_ready"), 1)

                def vector(b, i):
                    dve.tensor_copy(vec[b][:, :], vecs[:, ds(i * 2 + b, 1), :].rearrange("p o v -> p (o v)"))\
                        .then_inc(s(f"vec_ready{b}"), 1)

                def chunk(b, i, first=False, last=False):
                    n = i + 1
                    if b == 0:
                        vector(1, i)
                    elif not last:
                        vector(0, i + 1)
                    dve.wait_ge(s(f"vec_ready{b}"), n)
                    for g in range(3):
                        dve.wait_ge(s(f"u_ready{g}{b}"), n)
                    if not (first and b == 0):
                        dve.wait_ge(s("taps_summed"), i * 2 + b)
                    dve.tensor_scalar(acc[0][:, :], u[b][:, 0:CONV_OUT], vec[b][:, 0:1], vec[b][:, V_DWB:V_DWB + 1],
                                      ALU.mult, ALU.add).then_inc(s(f"tap0{b}"), 1)
                    dve.tensor_scalar(acc[1][:, :], u[b][:, 1:1 + CONV_OUT], vec[b][:, 1:2], None, ALU.mult)\
                        .then_inc(s(f"tap1{b}"), 1)
                    for k in range(2, TAPS):
                        q = k % 2
                        dve.wait_ge(s(f"tap{q}{b}"), i * len(range(q, TAPS, 2)) + k // 2)
                        dve.scalar_tensor_tensor(acc[q][:, :], u[b][:, k:k + CONV_OUT], vec[b][:, k:k + 1],
                                                 acc[q][:, :], ALU.mult, ALU.add).then_inc(s(f"tap{q}{b}"), 1)
                    for q in range(2):
                        dve.wait_ge(s(f"tap{q}{b}"), n * len(range(q, TAPS, 2)))
                    dve.tensor_tensor(vt[:, ds(i * 2 + b, 1), :].rearrange("p o n -> p (o n)"), acc[0][:, :],
                                      acc[1][:, :], ALU.add).then_inc(s("taps_summed"), 1)

                vector(0, 0)
                for b in range(2):
                    chunk(b, 0, first=True)
                with dve.Fori(1, pairs - 1) as i:
                    for b in range(2):
                        chunk(b, i)
                for b in range(2):
                    chunk(b, pairs - 1, last=True)
                dve.wait_ge(s("taps_summed"), KC)
        ph.close()


AHEAD = [(CTX, 0, 1, 0, None), (LAT, CTX_TILES, 1, 1, CTX), (LAT, CTX_TILES + 2, TILES // 2 - 2, 2, LAT)]


def conv_out(nc, d, vt, vecs):
    with ExitStack() as ctx:
        ph = Phase(nc, ctx, "pw2")
        s = ph.sem
        weights = SquareWeights(ph, nc, ctx, "pw2_w", d.pw2_w)
        w = weights.w
        mean_w = ph.sb("mean_w", [P, P])
        bias = ph.sb("bias", [P, D])
        gate = ph.sb("gate", [P, 2, D])
        eps = ph.sb("eps", [P, 1])
        dev = [ph.sb(f"dev{b}", [P, KC, P]) for b in range(2)]
        sq = [ph.sb(f"sq{b}", [P, KC, P]) for b in range(2)]
        root = ph.sb("root", [P, 2, P])
        rstd = ph.sb("rstd", [P, 2, P])
        act_t = [Split(nc, ctx, f"pw2_act{b}", [P, KC, P]) for b in range(2)]
        x = [ph.sb(f"x{b}", [P, D]) for b in range(2)]
        y = [ph.sb(f"y{b}", [P, D]) for b in range(2)]
        mean = [ph.ps(f"mean{b}", [P, N]) for b in range(2)]
        var = [ph.ps(f"var{b}", [P, N]) for b in range(2)]
        py = [ph.ps(f"py{b}", [P, D]) for b in range(2)]

        def vcol(i, b, t0):
            return (i * 2 + (t0 + b)) * P + (0 if t0 < CTX_TILES else GAP - PAD - CTX_LEN)

        with nc.Block() as block:
            @block.sync
            def _(sp):
                sp.dma_start(mean_w[:, :], d.mean_w).then_inc(s("tables"), 16)
                sp.dma_start(bias[:, :], d.pw2_b[0, :].partition_broadcast(P)).then_inc(s("tables"), 16)
                for st in (LAT, CTX):
                    sp.dma_start(gate[:, st, :], d.mods[0, st, G1, :].partition_broadcast(P)).then_inc(s("tables"), 16)
                weights.load(sp)
                for st, t0, pairs, before in STREAMS:
                    with sp.Fori(0, pairs) as i:
                        for b in range(2):
                            if before:
                                sp.wait_ge(s(f"stored{b}"), (i + before) * 16)
                            sp.dma_start(x[b][:, :], d.xs[ds((i * 2 + (t0 + b)) * P, P), :])\
                                .then_inc(s(f"x_loaded{b}"), 16)

            @block.gpsimd
            def _(pool):
                weights.low(pool, 1)
                for st, t0, pairs, before in STREAMS:
                    with pool.Fori(0, pairs) as i:
                        for b in range(2):
                            pool.wait_ge(s(f"x_ready{b}"), i + (before + 1))
                            pool.dma_start(d.xs[ds((i * 2 + (t0 + b)) * P, P), :], x[b][:, :])\
                                .then_inc(s(f"stored{b}"), 16)
                for b in range(2):
                    pool.wait_ge(s(f"stored{b}"), 16 * (TILES // 2))

            @block.tensor
            def _(pe):
                def average(what, b, i, t0):
                    for k in range(KC):
                        if what == "mean":
                            out, src = mean[b], vt[:, k, ds(vcol(i, b, t0), P)]
                        else:
                            out, src = var[b], sq[b][:, k, :]
                        last = pe.matmul(out[:, 0:P], mean_w[:, :], src, start=k == 0, stop=k == KC - 1)
                    last.then_inc(s(f"{what}_ready{b}"), 1)

                def product(b, n, before):
                    pe.wait_ge(s(f"act_lo{b}"), n)
                    if before:
                        pe.wait_ge(s(f"biased{b}"), n - 1)
                    for h in range(2):
                        for k in range(KC):
                            cols = slice(h * N, (h + 1) * N)
                            last = product3(pe, py[b][:, cols], act_t[b].hi[:, k, :], act_t[b].lo[:, k, :],
                                            w.hi[:, k, cols], w.lo[:, k, cols], k == 0, k == KC - 1)
                    last.then_inc(s(f"y_ready{b}"), 1)

                pe.wait_ge(s("tables"), 64)
                for st, t0, pairs, before, prev in AHEAD:
                    with pe.Fori(0, pairs) as i:
                        n = i + (before + 1)
                        for b in range(2):
                            if before:
                                pe.wait_ge(s(f"dev_ready{b}"), n - 1)
                            average("mean", b, i, t0)
                        if before == 1:
                            weights.wait(pe)
                        if before:
                            product(0, n - 1, before - 1)
                        for b in range(2):
                            pe.wait_ge(s(f"sq_ready{b}"), n)
                            if before:
                                pe.wait_ge(s(f"root_ready{b}"), n - 1)
                            average("var", b, i, t0)
                        if before:
                            product(1, n - 1, before - 1)
                for b in range(2):
                    product(b, TILES // 2, 1)

            @block.scalar
            def _(act):
                weights.high(act)
                act.wait_ge(s("eps_set"), 1)
                for st, t0, pairs, before, prev in AHEAD:
                    with act.Fori(0, pairs) as i:
                        n = i + (before + 1)
                        for b in range(2):
                            act.wait_ge(s(f"dev_ready{b}"), n)
                            if before:
                                act.wait_ge(s(f"act_lo{b}"), n - 1)
                            act.activation(sq[b][:, :, :], dev[b][:, :, :], ACT.Square).then_inc(s(f"sq_ready{b}"), 1)
                        for b in range(2):
                            act.wait_ge(s(f"var_ready{b}"), n)
                            if before:
                                act.wait_ge(s(f"rstd_ready{b}"), n - 1)
                            act.activation(root[:, b, :], var[b][:, 0:P], ACT.Sqrt, bias=eps[:, :])\
                                .then_inc(s(f"root_ready{b}"), 1)
                        for b in range(2):
                            act.wait_ge(s(f"scaled{b}"), n)
                            for k in range(KC):
                                last = act.activation(sq[b][:, k, :], dev[b][:, k, :], ACT.Silu,
                                                      scale=vecs[:, k, V_LNG:V_LNG + 1],
                                                      bias=vecs[:, k, V_LNB:V_LNB + 1])
                            last.then_inc(s(f"act_ready{b}"), 1)
                        for b in range(2):
                            act.wait_ge(s(f"act_ready{b}"), n)
                            if before:
                                act.wait_ge(s(f"y_ready{b}"), n - 1)
                            act.activation(act_t[b].hi[:, :, :], sq[b][:, :, :], ACT.Copy).then_inc(s(f"act_hi{b}"), 1)

            @block.vector
            def _(dve):
                def low(b, n):
                    dve.wait_ge(s(f"act_hi{b}"), n)
                    dve.tensor_tensor(act_t[b].lo[:, :, :], sq[b][:, :, :], act_t[b].hi[:, :, :].bitcast(F32),
                                      ALU.subtract).then_inc(s(f"act_lo{b}"), 1)

                def add(b, n, st):
                    dve.wait_ge(s(f"y_ready{b}"), n)
                    dve.tensor_tensor(y[b][:, :], py[b][:, :], bias[:, :], ALU.add).then_inc(s(f"biased{b}"), 1)
                    dve.wait_ge(s(f"biased{b}"), n)
                    dve.tensor_tensor(y[b][:, :], y[b][:, :], gate[:, st, :], ALU.mult).then_inc(s(f"gated{b}"), 1)
                    dve.wait_ge(s(f"gated{b}"), n)
                    dve.wait_ge(s(f"x_loaded{b}"), n * 16)
                    dve.tensor_tensor(x[b][:, :], x[b][:, :], y[b][:, :], ALU.add).then_inc(s(f"x_ready{b}"), 1)

                dve.memset(eps[:, :], EPS).then_inc(s("eps_set"), 1)
                weights.low(dve, 0)
                dve.wait_ge(s("tables"), 64)
                for st, t0, pairs, before, prev in AHEAD:
                    with dve.Fori(0, pairs) as i:
                        n = i + (before + 1)
                        for b in range(2):
                            dve.wait_ge(s(f"mean_ready{b}"), n)
                            if before:
                                dve.wait_ge(s(f"act_ready{b}"), n - 1)
                            dve.tensor_tensor(dev[b][:, :, :], vt[:, :, ds(vcol(i, b, t0), P)],
                                              mean[b][:, 0:P].unsqueeze(1).to_broadcast([P, KC, P]), ALU.subtract)\
                                .then_inc(s(f"dev_ready{b}"), 1)
                        if before:
                            add(0, n - 1, prev)
                        for b in range(2):
                            dve.wait_ge(s(f"root_ready{b}"), n)
                            dve.reciprocal(rstd[:, b, :], root[:, b, :]).then_inc(s(f"rstd_ready{b}"), 1)
                            dve.wait_ge(s(f"rstd_ready{b}"), n)
                            dve.tensor_tensor(dev[b][:, :, :], dev[b][:, :, :],
                                              rstd[:, b:b + 1, :].to_broadcast([P, KC, P]), ALU.mult)\
                                .then_inc(s(f"scaled{b}"), 1)
                        low(0, n)
                        if before:
                            add(1, n - 1, prev)
                        low(1, n)
                for b in range(2):
                    add(b, TILES // 2, LAT)
        ph.close()


def route(nc, d, layer, streams, ht, plan):
    t0 = streams[0][1]
    nt = TILES - t0
    nb = plan.blocks
    width = GROUPS + EXPERTS
    with ExitStack() as ctx:
        ph = Phase(nc, ctx, f"route{layer}")
        s = ph.sem
        raw = ph.sb("raw", [P, KC, width])
        w = Split(nc, ctx, f"route{layer}_w", [P, KC, width])
        bias = ph.sb("bias", [width, 1])
        next_e = ph.sb("next_e", [1, EXPERTS])
        ident = ph.sb("ident", [P, P])
        before = ph.sb("before", [P, P])
        ones = ph.sb("ones", [P, P])
        iota = ph.sb("iota", [P, P])
        token = ph.sb("token", [P, TILES])
        lt = ph.sb("lt", [width, TOK])
        lg = ph.sb("lg", [P, nt, width])
        gm = ph.sb("gm", [P, nt])
        ga = ph.sb("ga", [P, nt, GROUPS])
        gsel = ph.sb("gsel", [P, nt, GROUPS])
        gw = ph.sb("gw", [P, nt])
        inner = [ph.sb(f"inner{j}", [P, nt, EXPERTS]) for j in range(2)]
        cand = ph.sb("cand", [P, nt, EXPERTS])
        least = ph.sb("least", [P, nt])
        top = ph.sb("top", [P, 2, nt])
        hot = ph.sb("hot", [P, 2, nt, EXPERTS])
        both = ph.sb("both", [P, nt, EXPERTS])
        sofar = ph.sb("sofar", [P, nt + 1, EXPERTS])
        rank = ph.sb("rank", [P, nt, EXPERTS])
        picked = ph.sb("picked", [P, 2, nt, EXPERTS])
        mine = ph.sb("mine", [P, 2, nt])
        first = ph.sb("first", [P, 2, nt])
        over = ph.sb("over", [P, 2, nt])
        steps = ph.sb("steps", [P, nt])
        more = ph.sb("more", [P, 2 * nt * nt + EXPERTS * nt])
        need = ph.sb("need", [P, EXPERTS])
        ends = [ph.sb(f"ends{j}", [P, EXPERTS]) for j in range(2)]
        passed = ph.sb("passed", [1, nb, EXPERTS])
        blk = ph.sb("blk", [1, nb + 2])
        fresh = ph.sb("fresh", [1, nb])
        in_slot = ph.sb("in_slot", [P, 2 * nt, P])
        in_blk = ph.sb("in_blk", [P, 2 * nt, nb + 1])
        pl = [ph.ps(f"pl{g}", [P, N]) for g in range(3)]
        pt = ph.ps("pt", [P, nt, width])
        pr = ph.ps("pr", [P, nt * EXPERTS])
        pa = ph.ps("pa", [P, nt * EXPERTS])
        pi = ph.ps("pi", [P, nb + 1])
        groups = [(a, min(N, TOK - a)) for a in range(t0 * P, TOK, N)]

        with nc.Block() as block:
            @block.sync
            def _(sp):
                for dst, src in ((raw[:, :, 0:GROUPS], d.wg[layer].rearrange("(k p) n -> p k n", p=P)),
                                 (raw[:, :, GROUPS:width], d.wr[layer].rearrange("(k p) n -> p k n", p=P)),
                                 (bias[0:GROUPS, :], d.bg[layer, :].unsqueeze(1)),
                                 (bias[GROUPS:width, :], d.br[layer, :].unsqueeze(1)),
                                 (next_e[:, :], d.next_expert),
                                 (ident[:, :], d.ident), (before[:, :], d.before), (ones[:, :], d.ones),
                                 (iota[:, :], d.iota), (token[:, :], d.token)):
                    sp.dma_start(dst, src).then_inc(s("loaded"), 16)

            @block.tensor
            def _(pe):
                pe.wait_ge(s("loaded"), 160)
                pe.wait_ge(s("w_lo"), 1)
                for g, (a, n) in enumerate(groups):
                    for k in range(KC):
                        last = product3(pe, pl[g][0:width, 0:n], w.hi[:, k, :], w.lo[:, k, :],
                                        ht.hi[:, k, a:a + n], ht.lo[:, k, a:a + n], k == 0, k == KC - 1)
                    last.then_inc(s("logits"), 1)
                pe.wait_ge(s("biased"), len(groups))
                for t in range(nt):
                    last = pe.transpose(pt[:, t, :], lt[:, (t0 + t) * P:(t0 + t + 1) * P], ident[0:width, 0:width])
                last.then_inc(s("turned"), 1)
                pe.wait_ge(s("chosen"), 1)
                pe.matmul(pr[:, :], before[:, :], both[:, :, :].rearrange("p t e -> p (t e)"), start=True, stop=True)
                pe.matmul(pa[:, :], ones[:, :], both[:, :, :].rearrange("p t e -> p (t e)"), start=True, stop=True)\
                    .then_inc(s("counted"), 1)
                pe.wait_ge(s("hot_slots"), 4)
                for j in range(2 * nt):
                    last = pe.matmul(pi[:, :], in_slot[:, j, :], in_blk[:, j, :], start=j == 0, stop=j == 2 * nt - 1)
                last.then_inc(s("slots_done"), 1)

            @block.scalar
            def _(act):
                act.preload_act_table(ACT.Exp)
                act.wait_ge(s("loaded"), 160)
                act.activation(w.hi[:, :, :], raw[:, :, :], ACT.Copy).then_inc(s("w_hi"), 1)
                for g, (a, n) in enumerate(groups):
                    act.wait_ge(s("logits"), g + 1)
                    act.activation(lt[:, a:a + n], pl[g][0:width, 0:n], ACT.Identity, bias=bias[:, :])\
                        .then_inc(s("biased"), 1)
                act.wait_ge(s("group_shifted"), 1)
                act.activation(ga[:, :, :], ga[:, :, :], ACT.Exp).then_inc(s("group_exp"), 1)
                act.wait_ge(s("top_gap"), 1)
                act.activation(top[:, 1, :], top[:, 1, :], ACT.Exp).then_inc(s("top_exp"), 1)

            @block.vector
            def _(dve):
                link = chain(ph, dve, "step")

                def over_rows(ap, n):
                    return ap.unsqueeze(2).to_broadcast([P, nt, n])

                def along(n):
                    return iota[:, 0:n].unsqueeze(1).to_broadcast([P, nt, n])

                def first_max(values, n, biggest, hot_out):
                    link(dve.tensor_reduce(biggest, values, AX.X, ALU.max))
                    link(dve.tensor_tensor(cand[:, :, 0:n], values, over_rows(biggest, n), ALU.is_equal))
                    link(dve.scalar_tensor_tensor(cand[:, :, 0:n], cand[:, :, 0:n], -100.0, along(n), ALU.mult, ALU.add))
                    link(dve.tensor_reduce(least[:, :], cand[:, :, 0:n], AX.X, ALU.min))
                    link(dve.tensor_tensor(hot_out, cand[:, :, 0:n], over_rows(least[:, :], n), ALU.is_equal))

                dve.wait_ge(s("w_hi"), 1)
                dve.tensor_tensor(w.lo[:, :, :], raw[:, :, :], w.hi[:, :, :].bitcast(F32), ALU.subtract)\
                    .then_inc(s("w_lo"), 1)
                dve.wait_ge(s("turned"), 1)
                link(dve.tensor_copy(lg[:, :, 0:GROUPS], pt[:, :, 0:GROUPS]))
                link(dve.tensor_copy(lg[:, :, GROUPS:width].rearrange("p t (e g) -> p t e g", g=GROUPS),
                                     pt[:, :, GROUPS:width].rearrange("p t (g e) -> p t e g", g=GROUPS)))
                first_max(lg[:, :, 0:GROUPS], GROUPS, gm[:, :], gsel[:, :, :])
                dve.tensor_tensor(ga[:, :, :], lg[:, :, 0:GROUPS], over_rows(gm[:, :], GROUPS), ALU.subtract)\
                    .then_inc(s("group_shifted"), 1)
                def by_group(ap):
                    return ap.rearrange("p t (e g) -> p t e g", g=GROUPS)
                sel = gsel[:, :, :].unsqueeze(2).to_broadcast([P, nt, PER_GROUP, GROUPS])
                link(dve.tensor_tensor(by_group(inner[0][:, :, :]), by_group(lg[:, :, GROUPS:width]), sel, ALU.mult))
                link(dve.tensor_scalar(gsel[:, :, :], gsel[:, :, :], 1.0, 1e30, ALU.subtract, ALU.mult))
                link(dve.tensor_tensor(by_group(inner[0][:, :, :]), by_group(inner[0][:, :, :]), sel, ALU.add))
                first_max(inner[0][:, :, :], EXPERTS, top[:, 0, :], hot[:, 0, :, :])
                link(dve.scalar_tensor_tensor(inner[1][:, :, :], hot[:, 0, :, :], -2e30, inner[0][:, :, :],
                                              ALU.mult, ALU.add))
                first_max(inner[1][:, :, :], EXPERTS, top[:, 1, :], hot[:, 1, :, :])
                dve.tensor_tensor(both[:, :, :], hot[:, 0, :, :], hot[:, 1, :, :], ALU.add).then_inc(s("chosen"), 1)
                dve.tensor_tensor(top[:, 1, :], top[:, 1, :], top[:, 0, :], ALU.subtract).then_inc(s("top_gap"), 1)
                dve.wait_ge(s("group_exp"), 1)
                link(dve.tensor_reduce(gw[:, :], ga[:, :, :], AX.X, ALU.add))
                link(dve.reciprocal(gw[:, :], gw[:, :]))
                dve.wait_ge(s("top_exp"), 1)
                link(dve.tensor_scalar(top[:, 0, :], top[:, 1, :], 1.0, None, ALU.add))
                link(dve.reciprocal(top[:, 0, :], top[:, 0, :]))
                link(dve.tensor_tensor(plan.weight[:, 0, :], top[:, 0, :], gw[:, :], ALU.mult))
                link(dve.tensor_tensor(plan.weight[:, 1, :], plan.weight[:, 0, :], top[:, 1, :], ALU.mult))
                dve.wait_ge(s("counted"), 1)
                link(dve.memset(sofar[:, 0, :], 0.0))
                for t in range(nt):
                    link(dve.tensor_tensor(sofar[:, t + 1, :], sofar[:, t, :], pa[:, t * EXPERTS:(t + 1) * EXPERTS],
                                           ALU.add))
                link(dve.tensor_tensor(rank[:, :, :].rearrange("p t e -> p (t e)"), pr[:, :],
                                       sofar[:, 0:nt, :].rearrange("p t e -> p (t e)"), ALU.add))
                link(dve.tensor_scalar(steps[:, :], iota[:, 0:nt], float(BLK), None, ALU.mult))
                taken = more[:, 2 * nt * nt:].rearrange("p (e t) -> p e t", t=nt)
                link(dve.tensor_tensor(taken, sofar[:, nt, :].unsqueeze(2).to_broadcast([P, EXPERTS, nt]),
                                       steps[:, :].unsqueeze(1).to_broadcast([P, EXPERTS, nt]), ALU.is_gt))
                link(dve.tensor_reduce(need[:, :], taken, AX.X, ALU.add))
                link(dve.tensor_copy(ends[0][:, :], need[:, :]))
                for j in range(5):
                    a, b, step = ends[j % 2], ends[(j + 1) % 2], 1 << j
                    link(dve.tensor_copy(b[:, 0:step], a[:, 0:step]))
                    link(dve.tensor_tensor(b[:, step:], a[:, step:], a[:, 0:EXPERTS - step], ALU.add))
                end = ends[1]
                link(dve.tensor_tensor(need[:, :], end[:, :], need[:, :], ALU.subtract))
                for j in range(2):
                    link(dve.tensor_tensor(picked[:, j, :, :], hot[:, j, :, :], rank[:, :, :], ALU.mult))
                link(dve.tensor_reduce(mine[:, :, :], picked[:, :, :, :], AX.X, ALU.add))
                for j in range(2):
                    link(dve.tensor_tensor(picked[:, j, :, :], hot[:, j, :, :],
                                           need[:, :].unsqueeze(1).to_broadcast([P, nt, EXPERTS]), ALU.mult))
                link(dve.tensor_reduce(first[:, :, :], picked[:, :, :, :], AX.X, ALU.add))
                for j in range(2):
                    full = more[:, j * nt * nt:j * nt * nt + nt * (nt - 1)].rearrange("p (t k) -> p t k", k=nt - 1)
                    link(dve.tensor_tensor(full, over_rows(mine[:, j, :], nt - 1),
                                           steps[:, 1:nt].unsqueeze(1).to_broadcast([P, nt, nt - 1]), ALU.is_ge))
                    link(dve.tensor_reduce(over[:, j, :], full, AX.X, ALU.add))
                link(dve.tensor_tensor(first[:, :, :], first[:, :, :], over[:, :, :], ALU.add))
                link(dve.scalar_tensor_tensor(mine[:, :, :], over[:, :, :], -float(BLK), mine[:, :, :],
                                              ALU.mult, ALU.add))
                link(dve.scalar_tensor_tensor(plan.slot[:, :, :], first[:, :, :], float(BLK), mine[:, :, :],
                                              ALU.mult, ALU.add))
                for j in range(2):
                    q = slice(j * nt, (j + 1) * nt)
                    dve.tensor_tensor(in_slot[:, q, :], along(P), over_rows(mine[:, j, :], P), ALU.is_equal)\
                        .then_inc(s("hot_slots"), 1)
                    link(dve.tensor_tensor(in_blk[:, q, :], along(nb + 1), over_rows(first[:, j, :], nb + 1),
                                           ALU.is_equal))
                    dve.tensor_tensor(in_blk[:, q, :], in_blk[:, q, :], over_rows(token[:, t0:TILES], nb + 1),
                                      ALU.mult).then_inc(s("hot_slots"), 1)
                link(dve.tensor_tensor(passed[:, :, :], iota[0:1, 0:nb].unsqueeze(2).to_broadcast([1, nb, EXPERTS]),
                                       end[0:1, :].unsqueeze(1).to_broadcast([1, nb, EXPERTS]), ALU.is_ge))
                link(dve.tensor_tensor(passed[:, :, :], passed[:, :, :],
                                       next_e[:, :].unsqueeze(1).to_broadcast([1, nb, EXPERTS]), ALU.mult))
                link(dve.tensor_reduce(blk[:, 0:nb], passed[:, :, :], AX.X, ALU.add))
                link(dve.memset(fresh[:, :], 1.0))
                link(dve.tensor_tensor(fresh[:, 1:nb], blk[:, 1:nb], blk[:, 0:nb - 1], ALU.not_equal))
                link(dve.tensor_copy(plan.fresh[:, :], fresh[:, :]))
                link(dve.tensor_copy(blk[:, nb:nb + 1], end[0:1, EXPERTS - 1:EXPERTS]))
                link(dve.tensor_scalar(blk[:, nb + 1:nb + 2], end[0:1, EXPERTS - 1:EXPERTS], 1.0, None, ALU.subtract))
                link(dve.tensor_copy(plan.block[:, :], blk[:, :]))
                dve.wait_ge(s("slots_done"), 1)
                link(dve.tensor_scalar(plan.taken[:, :], pi[:, :], 1.0, None, ALU.min))
                link(dve.tensor_scalar(plan.token[:, :], pi[:, :], 1.0, 0.0, ALU.subtract, ALU.max))
        ph.close()


class Plan:
    def __init__(self, nc, ctx, layer, tiles):
        self.blocks = 2 * tiles + EXPERTS
        self.fewest = 2 * tiles
        def sb(name, shape, dt):
            return ctx.enter_context(nc.sbuf_tensor(f"plan{layer}_{name}", shape, dt))
        self.slot = sb("slot", [P, 2, tiles], I32)
        self.weight = sb("weight", [P, 2, tiles], F32)
        self.token = sb("token", [P, self.blocks + 1], I32)
        self.taken = sb("taken", [P, self.blocks + 1], I32)
        self.block = sb("block", [1, self.blocks + 2], I32)
        self.fresh = sb("fresh", [1, self.blocks], I32)


def experts(nc, d, layer, plan):
    FC = FF // P
    nb = plan.blocks
    with ExitStack() as ctx:
        ph = Phase(nc, ctx, f"moe{layer}")
        s = ph.sem
        shapes = {"w1": [P, KC, FF], "w3": [P, KC, FF], "w2": [P, FC, D]}
        SLOTS = {"w1": 2, "w3": 2, "w2": 1}
        raw = {m: [ph.sb(f"{m}_raw{p}", sh) for p in range(SLOTS[m])] for m, sh in shapes.items()}
        hi = {m: ph.sb(f"{m}_hi", sh, F32R) for m, sh in shapes.items()}
        lo = {m: ph.sb(f"{m}_lo", sh, F32R) for m, sh in shapes.items()}
        half = {m: sh[1] // 2 for m, sh in shapes.items()}
        dram = {"w1": d.w1, "w3": d.w3, "w2": d.w2}
        ident = ph.sb("ident", [P, P])
        idx = ph.sb("idx", [P, 1], I32)
        xg = ph.sb("xg", [P, D])
        xt_hi = ph.sb("xt_hi", [P, KC, P], F32R)
        xt_lo = ph.sb("xt_lo", [P, KC, P], F32R)
        sil = ph.sb("sil", [P, FF])
        a = ph.sb("a", [P, FF])
        at_hi = ph.sb("at_hi", [P, FC, P], F32R)
        at_lo = ph.sb("at_lo", [P, FC, P], F32R)
        y = ph.sb("y", [P, D])
        zero = ph.sb("zero", [P, D])
        pxt = ph.ps("pxt", [P, KC, P])
        pg = ph.ps("pg", [P, FF])
        pu = ph.ps("pu", [P, FF])
        pat = ph.ps("pat", [P, FC, P])
        py = ph.ps("py", [P, D])

        def blocks(eng, body, tail=None, otherwise=None):
            count = eng.value_load(plan.block[0:1, nb:nb + 1], min_val=plan.fewest, max_val=nb)
            for k in range(2):
                body(k, k)
            with eng.Fori(1, nb // 2) as i:
                for p in range(2):
                    k = i * 2 + p
                    with eng.If(k < count):
                        body(k, 2, i, p)
                    if otherwise:
                        with eng.If(k >= count):
                            otherwise(k)
            if tail:
                tail(count, eng.value_load(plan.block[0:1, nb + 1:nb + 2], min_val=plan.fewest - 1, max_val=nb - 1))

        def by_expert(eng, k, least, fresh, kept):
            if least == 0:
                fresh()
                return
            new = eng.value_load(plan.fresh[0:1, ds(k, 1)], min_val=0, max_val=1)
            with eng.If(new > 0):
                fresh()
            with eng.If(new < 1):
                kept()

        HALF = BLK // 2

        def by_rows(eng, k, transfer):
            wide = eng.value_load(plan.taken[HALF:HALF + 1, ds(k, 1)], min_val=0, max_val=1)
            with eng.If(wide > 0):
                transfer(BLK)
            with eng.If(wide < 1):
                transfer(HALF)

        with nc.Block() as block:
            @block.sync
            def _(sp):
                sp.dma_start(ident[:, :], d.ident).then_inc(s("ident"), 16)

                def bring(mats, k, least, p=0):
                    def free(m, h):
                        if SLOTS[m] == 1 and least:
                            sp.wait_ge(s(f"{m}_lo{h}"), k)
                        elif SLOTS[m] == 2 and least == 2:
                            sp.wait_ge(s(f"{m}_lo{h}"), k - 1)

                    def fresh():
                        e = sp.value_load(plan.block[0:1, ds(k, 1)], min_val=0, max_val=EXPERTS - 1)
                        for m in mats:
                            for h in range(2):
                                cut = slice(h * half[m], (h + 1) * half[m])
                                free(m, h)
                                sp.dma_start(raw[m][p][:, cut, :],
                                             dram[m][layer, ds(e, 1), h * half[m] * P:(h + 1) * half[m] * P, :]
                                             .rearrange("o (k p) n -> p (o k) n", p=P)).then_inc(s(f"{m}_raw{h}{p}"), 16)

                    def kept():
                        for m in mats:
                            for h in range(2):
                                free(m, h)
                                sp.sem_inc(s(f"{m}_raw{h}{p}"), 16)

                    by_expert(sp, k, least, fresh, kept)

                def body(b, least, i=0, p=None):
                    bring(("w1", "w3"), b, least, b if p is None else p)
                    if least:
                        bring(("w2",), b - 1, least - 1)

                def unused(k):
                    sp.dma_start(d.yd[ds(k * BLK, BLK), :], zero[:, :]).then_inc(s("covered"), 16)

                sp.wait_ge(s("zero_set"), 1)
                blocks(sp, body, lambda count, last: bring(("w2",), last, 1), None if layer else unused)

            @block.gpsimd
            def _(pool):
                def gather(k, n):
                    pool.tensor_copy(idx[:, :], plan.token[:, ds(k, 1)]).then_inc(s("idx_ready"), 1)
                    pool.wait_ge(s("idx_ready"), n + 1)
                    pool.sem_inc(s("gathers"), 1)

                    def transfer(rows):
                        pool.indirect_dma_start(xg[0:rows, :], None, d.hd[:, :],
                                                bass.IndirectOffsetOnAxis(idx[0:rows, :], 0))\
                            .then_inc(s("gathered"), 16)

                    by_rows(pool, k, transfer)

                def ahead(k, least, i=0, p=0):
                    pool.wait_ge(s("xt_turned"), k + 1)
                    gather(k + 1, k + 1)

                def finish(count, last):
                    pool.wait_ge(s("gathered"), count * 16 + 16)
                    pool.wait_ge(s("y_stored"), count * 16 + 16)
                    if layer == 0:
                        pool.wait_ge(s("covered"), nb * 16)

                pool.memset(zero[:, :], 0.0).then_inc(s("zero_set"), 1)
                pool.memset(xg[:, :], 0.0).then_inc(s("xg_zeroed"), 1)
                pool.wait_ge(s("xg_zeroed"), 1)
                gather(0, 0)
                blocks(pool, ahead, finish)

            @block.tensor
            def _(pe):
                def turn_x(n):
                    pe.wait_ge(s("gathered"), n * 16)
                    for k in range(KC):
                        last = pe.transpose(pxt[:, k, :], xg[:, k * P:(k + 1) * P], ident[:, :])
                    last.then_inc(s("xt_turned"), 1)

                def out_product(n, before, least):
                    pe.wait_ge(s("at_lo"), n)
                    if least:
                        pe.wait_ge(s("y_out"), before)
                    for h in range(2):
                        pe.wait_ge(s(f"w2_lo{h}"), n)
                        for c in range(2):
                            for k in range(h * half["w2"], (h + 1) * half["w2"]):
                                cols = slice(c * N, (c + 1) * N)
                                last = product3(pe, py[:, cols], at_hi[:, k, :], at_lo[:, k, :],
                                                hi["w2"][:, k, cols], lo["w2"][:, k, cols], k == 0, k == FC - 1)
                    last.then_inc(s("w2_done"), 1)

                def body(b, least, i=0, p=None):
                    n = b + 1
                    p = b if p is None else p
                    pe.wait_ge(s("xt_hi"), n)
                    pe.wait_ge(s("xt_lo"), n)
                    for w, out, used in (("w1", pg, "sil_ready"), ("w3", pu, "a_ready")):
                        if least:
                            pe.wait_ge(s(used), b)
                        for h in range(2):
                            pe.wait_ge(s(f"{w}_lo{h}"), n)
                            for k in range(h * half[w], (h + 1) * half[w]):
                                last = product3(pe, out[:, :], xt_hi[:, k, :], xt_lo[:, k, :], hi[w][:, k, :],
                                                lo[w][:, k, :], k == 0, k == KC - 1)
                        last.then_inc(s(f"{w}_done"), 1)
                    turn_x(n + 1)
                    if least:
                        out_product(b, b - 1, least - 1)
                    pe.wait_ge(s("a_ready"), n)
                    for k in range(FC):
                        last = pe.transpose(pat[:, k, :], a[:, k * P:(k + 1) * P], ident[:, :])
                    last.then_inc(s("at_turned"), 1)

                pe.wait_ge(s("ident"), 16)
                turn_x(1)
                blocks(pe, body, lambda count, last: out_product(count, last, 1))

            @block.scalar
            def _(act):
                act.preload_act_table(ACT.Silu)

                def high(m, n, before, least, p=0, loads=None):
                    for h in range(2):
                        cut = slice(h * half[m], (h + 1) * half[m])
                        act.wait_ge(s(f"{m}_raw{h}{p}"), (n if loads is None else loads) * 16)
                        if h == 0 and least:
                            act.wait_ge(s(f"{m}_done"), before)
                        act.activation(hi[m][:, cut, :], raw[m][p][:, cut, :], ACT.Copy).then_inc(s(f"{m}_hi{h}"), 1)

                def skip(m):
                    for h in range(2):
                        act.sem_inc(s(f"{m}_hi{h}"), 1)

                def put_out(n, k):
                    act.wait_ge(s("w2_done"), n)
                    act.wait_ge(s("y_stored"), n * 16)
                    act.activation(y[:, :], py[:, :], ACT.Copy).then_inc(s("y_out"), 1)
                    act.wait_ge(s("y_out"), n)

                    def transfer(rows):
                        act.dma_start(d.yd[ds(k * BLK, rows), :], y[0:rows, :]).then_inc(s("y_stored"), 16)

                    if layer:
                        by_rows(act, k, transfer)
                    else:
                        transfer(BLK)

                def x_high(n):
                    act.wait_ge(s("xt_turned"), n)
                    act.activation(xt_hi[:, :, :], pxt[:, :, :], ACT.Copy).then_inc(s("xt_hi"), 1)

                def before_out(n, k, least):
                    act.wait_ge(s("at_turned"), n)
                    act.activation(at_hi[:, :, :], pat[:, :, :], ACT.Copy).then_inc(s("at_hi"), 1)
                    by_expert(act, k, least, lambda: high("w2", n, k, least), lambda: skip("w2"))

                def body(b, least, i=0, p=None):
                    n = b + 1
                    p = b if p is None else p

                    def fresh():
                        high("w1", n, b, least, p, i + 1)
                        x_high(n)
                        high("w3", n, b, least, p, i + 1)

                    def kept():
                        skip("w1")
                        x_high(n)
                        skip("w3")

                    by_expert(act, b, least, fresh, kept)
                    if least > 1:
                        put_out(b - 1, b - 2)
                    if least:
                        before_out(b, b - 1, least - 1)
                    act.wait_ge(s("w1_done"), n)
                    if least:
                        act.wait_ge(s("a_ready"), b)
                    act.activation(sil[:, :], pg[:, :], ACT.Silu).then_inc(s("sil_ready"), 1)

                def tail(count, last):
                    put_out(last, last - 1)
                    before_out(count, last, 1)
                    put_out(count, last)

                blocks(act, body, tail)

            @block.vector
            def _(dve):
                def low(m, n, p=0, halves=(0, 1)):
                    for h in halves:
                        cut = slice(h * half[m], (h + 1) * half[m])
                        dve.wait_ge(s(f"{m}_hi{h}"), n)
                        dve.tensor_tensor(lo[m][:, cut, :], raw[m][p][:, cut, :], hi[m][:, cut, :].bitcast(F32),
                                          ALU.subtract).then_inc(s(f"{m}_lo{h}"), 1)

                def skip(m, n):
                    for h in range(2):
                        dve.wait_ge(s(f"{m}_hi{h}"), n)
                        dve.sem_inc(s(f"{m}_lo{h}"), 1)

                def x_low(n):
                    dve.wait_ge(s("xt_hi"), n)
                    dve.tensor_tensor(xt_lo[:, :, :], pxt[:, :, :], xt_hi[:, :, :].bitcast(F32), ALU.subtract)\
                        .then_inc(s("xt_lo"), 1)

                def before_out(n, k, least):
                    dve.wait_ge(s("at_hi"), n)
                    dve.tensor_tensor(at_lo[:, :, :], pat[:, :, :], at_hi[:, :, :].bitcast(F32), ALU.subtract)\
                        .then_inc(s("at_lo"), 1)
                    by_expert(dve, k, least, lambda: low("w2", n), lambda: skip("w2", n))

                def body(b, least, i=0, p=None):
                    n = b + 1
                    p = b if p is None else p
                    if layer == 0:
                        dve.sem_inc(s("covered"), 16)

                    def fresh():
                        low("w1", n, p, (0,))
                        x_low(n)
                        low("w1", n, p, (1,))
                        low("w3", n, p)

                    def kept():
                        skip("w1", n)
                        x_low(n)
                        skip("w3", n)

                    by_expert(dve, b, least, fresh, kept)
                    if least:
                        before_out(b, b - 1, least - 1)
                    dve.wait_ge(s("sil_ready"), n)
                    dve.wait_ge(s("w3_done"), n)
                    if least:
                        dve.wait_ge(s("at_turned"), b)
                    dve.tensor_tensor(a[:, :], sil[:, :], pu[:, :], ALU.mult).then_inc(s("a_ready"), 1)

                dve.sem_inc(s("y_stored"), 16)
                blocks(dve, body, lambda count, last: before_out(count, last, 1))
        ph.close()


def combine(nc, d, layer, streams, plan, ht):
    final = ht is None
    first_tile = streams[0][1]
    tiles = range(TILES - first_tile)
    XB, YB = 4, 3
    with ExitStack() as ctx:
        ph = Phase(nc, ctx, f"comb{layer}")
        s = ph.sem
        x = [ph.sb(f"x{b}", [P, D]) for b in range(XB)]
        y = [[ph.sb(f"y{j}{b}", [P, D]) for b in range(YB)] for j in range(2)]
        mix = [ph.sb(f"mix{b}", [P, D]) for b in range(2)]
        gate = ph.sb("gate", [P, 2, D])
        junk = ph.sb("junk", [P, D])
        stat = ph.sb("stat", [P, len(tiles), 3])
        eps = ph.sb("eps", [P, 1])
        gain = ph.sb("gain", [P, D])
        if not final:
            h = [ph.sb(f"h{b}", [P, D]) for b in range(2)]
            scale = ph.sb("scale", [P, 2, D])
            shift = ph.sb("shift", [P, 2, D])
            ident = ph.sb("ident", [P, P])
            pt = [ph.ps(f"pt{b}", [P, KC, P]) for b in range(2)]
        used = (CTX, LAT) if first_tile == 0 else (LAT,)

        def stream(t):
            return CTX if first_tile + t < CTX_TILES else LAT

        def starts(t):
            return t == 0 or stream(t) != stream(t - 1)

        def lagging(body, lag):
            return lambda t: body(t - lag) if t - lag in tiles else None

        def run(*stages):
            stages = [lagging(body, lag) for body, lag in stages]
            for t in range(len(tiles) + 3):
                for stage in stages:
                    stage(t)

        with nc.Block() as block:
            @block.sync
            def _(sp):
                def load(t):
                    if t >= XB:
                        sp.wait_ge(s("normed"), t - XB + 1)
                        sp.wait_ge(s(f"x_stored{t % XB}"), 16 * (t // XB))
                    row = (first_tile + t) * P
                    sp.dma_start(x[t % XB][:, :], d.xs[row:row + P, :]).then_inc(s(f"x_loaded{t % XB}"), 16)

                def store(t):
                    sp.wait_ge(s("normed" if final else "x_added"), t + 1)
                    row = t * P
                    sp.dma_start((d.out if final else d.xs)[row:row + P, :], x[t % XB][:, :])\
                        .then_inc(s(f"x_stored{t % XB}"), 16)

                for t in range(2):
                    load(t)
                for t in tiles:
                    if t + 2 in tiles:
                        load(t + 2)
                    store(t)
                for b in range(XB):
                    sp.wait_ge(s(f"x_stored{b}"), 16 * len(tiles[b::XB]))

            @block.gpsimd
            def _(pool):
                def gather(t):
                    b = t % YB
                    for j in range(2):
                        if t >= YB:
                            pool.wait_ge(s("first_in" if j == 0 else "second_in"), t - YB + 1)
                        pool.indirect_dma_start(y[j][b][:, :], None, d.yd[:, :],
                                                bass.IndirectOffsetOnAxis(plan.slot[:, j, t:t + 1], 0))\
                            .then_inc(s(f"gathered{j}{b}"), 16)

                def gated(t):
                    if starts(t):
                        pool.wait_ge(s(f"gate_loaded{stream(t)}"), 16)
                    pool.wait_ge(s("second_in"), t + 1)
                    pool.tensor_tensor(mix[t % 2][:, :], mix[t % 2][:, :], gate[:, stream(t), :], ALU.mult)\
                        .then_inc(s("gated"), 1)

                for t in range(YB):
                    gather(t)
                for t in tiles:
                    gated(t)
                    if t + YB in tiles:
                        gather(t + YB)

            @block.tensor
            def _(pe):
                if final:
                    return
                pe.wait_ge(s("ident"), 16)
                for t in tiles:
                    pe.wait_ge(s("h_ready"), t + 1)
                    if t >= 2:
                        pe.wait_ge(s("ht_lo"), t - 1)
                    for k in range(KC):
                        last = pe.transpose(pt[t % 2][:, k, :], h[t % 2][:, k * P:(k + 1) * P], ident[:, :])
                    last.then_inc(s("turned"), 1)

            @block.scalar
            def _(act):
                for st in used:
                    act.dma_start(gate[:, st, :], d.mods[layer, st, G2, :].partition_broadcast(P))\
                        .then_inc(s(f"gate_loaded{st}"), 16)
                    if st == used[0]:
                        row = d.final_g if final else d.norm_g[layer + 1, 0, :]
                        act.dma_start(gain[:, :], row.partition_broadcast(P)).then_inc(s("gain_loaded"), 16)
                    if not final:
                        act.dma_start(scale[:, st, :], d.mods[layer + 1, st, SC1, :].partition_broadcast(P))\
                            .then_inc(s(f"rows_loaded{st}"), 16)
                        act.dma_start(shift[:, st, :], d.mods[layer + 1, st, SH1, :].partition_broadcast(P))\
                            .then_inc(s(f"rows_loaded{st}"), 16)
                if not final:
                    act.dma_start(ident[:, :], d.ident).then_inc(s("ident"), 16)
                act.preload_act_table(ACT.Sqrt)
                act.wait_ge(s("eps_set"), 1)

                def first(t):
                    act.wait_ge(s(f"gathered0{t % YB}"), 16 * (t // YB + 1))
                    if t >= 2:
                        act.wait_ge(s("x_added"), t - 1)
                    act.activation(mix[t % 2][:, :], y[0][t % YB][:, :], ACT.Copy, scale=plan.weight[:, 0, t:t + 1])\
                        .then_inc(s("first_in"), 1)

                def high(t):
                    act.wait_ge(s("turned"), t + 1)
                    cols = slice(t * P, (t + 1) * P)
                    act.activation(ht.hi[:, :, cols], pt[t % 2][:, :, :], ACT.Copy).then_inc(s("ht_hi"), 1)

                def root(t):
                    act.wait_ge(s("x_added"), t + 1)
                    act.activation(junk[:, :], x[t % XB][:, :], ACT.Square, accum_out=stat[:, t, 0:1])\
                        .then_inc(s("squares"), 1)
                    act.wait_ge(s("squares"), t + 1)
                    act.activation(stat[:, t, 1:2], stat[:, t, 0:1], ACT.Sqrt, bias=eps[:, :], scale=1.0 / D)\
                        .then_inc(s("root"), 1)

                if final:
                    run((first, 0), (root, 1))
                else:
                    run((first, 0), (high, 3), (root, 1))

            @block.vector
            def _(dve):
                dve.memset(eps[:, :], EPS).then_inc(s("eps_set"), 1)

                def second(t):
                    dve.wait_ge(s(f"gathered1{t % YB}"), 16 * (t // YB + 1))
                    dve.wait_ge(s("first_in"), t + 1)
                    dve.scalar_tensor_tensor(mix[t % 2][:, :], y[1][t % YB][:, :], plan.weight[:, 1, t:t + 1],
                                             mix[t % 2][:, :], ALU.mult, ALU.add).then_inc(s("second_in"), 1)

                def add(t):
                    dve.wait_ge(s(f"x_loaded{t % XB}"), 16 * (t // XB + 1))
                    dve.wait_ge(s("gated"), t + 1)
                    dve.tensor_tensor(x[t % XB][:, :], x[t % XB][:, :], mix[t % 2][:, :], ALU.add)\
                        .then_inc(s("x_added"), 1)

                def low(t):
                    dve.wait_ge(s("ht_hi"), t + 1)
                    cols = slice(t * P, (t + 1) * P)
                    dve.tensor_tensor(ht.lo[:, :, cols], pt[t % 2][:, :, :], ht.hi[:, :, cols].bitcast(F32),
                                      ALU.subtract).then_inc(s("ht_lo"), 1)

                def norm(t):
                    if t == 0:
                        dve.wait_ge(s("gain_loaded"), 16)
                    if starts(t) and not final:
                        st = stream(t)
                        dve.wait_ge(s(f"rows_loaded{st}"), 32)
                        dve.scalar_tensor_tensor(scale[:, st, :], scale[:, st, :], 1.0, gain[:, :], ALU.add, ALU.mult)\
                            .then_inc(s("scale_ready"), 1)
                        dve.wait_ge(s("scale_ready"), used.index(st) + 1)
                    dve.wait_ge(s("root"), t + 1)
                    dve.reciprocal(stat[:, t, 2:3], stat[:, t, 1:2]).then_inc(s("rstd"), 1)
                    dve.wait_ge(s("rstd"), t + 1)
                    if final:
                        dve.scalar_tensor_tensor(x[t % XB][:, :], x[t % XB][:, :], stat[:, t, 2:3], gain[:, :],
                                                 ALU.mult, ALU.mult).then_inc(s("normed"), 1)
                        return
                    if t >= 2:
                        dve.wait_ge(s("turned"), t - 1)
                    dve.scalar_tensor_tensor(h[t % 2][:, :], x[t % XB][:, :], stat[:, t, 2:3],
                                             scale[:, stream(t), :], ALU.mult, ALU.mult).then_inc(s("normed"), 1)
                    dve.wait_ge(s("normed"), t + 1)
                    dve.tensor_tensor(h[t % 2][:, :], h[t % 2][:, :], shift[:, stream(t), :], ALU.add)\
                        .then_inc(s("h_ready"), 1)

                if final:
                    run((second, 0), (norm, 2), (add, 1))
                else:
                    run((second, 0), (add, 1), (low, 3), (norm, 1))
        ph.close()


QK, VG = 2 * HEADS * DK, 2 * HEADS * DV
LAT_TILES = TILES - CTX_TILES
TOKEN_GROUPS = [(0, CTX_LEN), (CTX_LEN, N), (CTX_LEN + N, N)]
SCAN = [(CTX, 0, CTX_TILES - 1, 1, 0, TILES - 1), (LAT, CTX_TILES, TILES - 1, 1, 1, TILES - 3),
        (LAT, CTX_TILES + 2, TILES - 3, LAT_TILES // 2 - 2, 2, TILES - 5),
        (LAT, TILES - 2, CTX_TILES + 1, 1, LAT_TILES // 2, None)]


class Step:

    def __init__(self, stream, b, n, forward, backward, first, first_lat):
        self.lat, self.b, self.n, self.m = stream == LAT, b, n, n - 1
        self.tile, self.first, self.first_lat = (forward, backward), first, first_lat


def scan_steps(i, segment):
    stream, ta, tb, pairs, before, behind = segment
    n = i + (before + 1)
    steps = [Step(stream, b, n, i * 2 + (ta + b), i * -2 + (tb - b), before == 0 and b == 0, before == 1 and b == 0)
             for b in range(2)]
    after = None if behind is None else Step(LAT, 0, n + 1, i * 2 + (ta + 2), i * -2 + behind, False, before == 0)
    return [(steps[0], steps[1]), (steps[1], after)]


LAST = {0: CHUNK - 1, 1: 0}
REF = {0: CHUNK // 2, 1: CHUNK // 2 - 1}


def gla_values(nc, d, ht):
    with ExitStack() as ctx:
        ph = Phase(nc, ctx, "glav")
        s = ph.sem
        raw = ph.sb("raw", [P, KC, N])
        w = [Split(nc, ctx, f"glav_w{b}", [P, KC, N]) for b in range(2)]
        out = [ph.sb(f"out{b}", [P, N]) for b in range(4)]
        acc = [ph.ps(f"acc{b}", [P, N]) for b in range(4)]
        jobs = [("v", 0, 0), ("v", 1, 0), ("gate", 0, CTX_TILES), ("gate", 1, CTX_TILES)]
        steps = [(g, t) for g, job in enumerate(jobs) for t in range(job[2], TILES)]

        with nc.Block() as block:
            @block.sync
            def _(sp):
                def load(g):
                    c0 = QK + g * N
                    if g:
                        sp.wait_ge(s("w_lo"), g)
                    sp.dma_start(raw[:, :, :], d.w_in[:, c0:c0 + N].rearrange("(k p) n -> p k n", p=P))\
                        .then_inc(s("w_loaded"), 16)
                for g in range(len(jobs)):
                    load(g)

            @block.gpsimd
            def _(pool):
                for n, (g, t) in enumerate(steps):
                    kind, half, t0 = jobs[g]
                    dst, row = (d.vd, t * P) if kind == "v" else (d.gd, (t - CTX_TILES) * P)
                    pool.wait_ge(s("out_ready"), n + 1)
                    pool.dma_start(dst[row:row + P, half * N:(half + 1) * N], out[n % 4][:, :])\
                        .then_inc(s(f"stored{n % 4}"), 16)
                for b in range(4):
                    pool.wait_ge(s(f"stored{b}"), 16 * len(range(b, len(steps), 4)))

            @block.tensor
            def _(pe):
                for n, (g, t) in enumerate(steps):
                    if t == jobs[g][2]:
                        pe.wait_ge(s("w_lo"), g + 1)
                    if n >= 4:
                        pe.wait_ge(s("out_ready"), n - 3)
                    cols = slice(t * P, (t + 1) * P)
                    for k in range(KC):
                        last = product3(pe, acc[n % 4][:, :], ht.hi[:, k, cols], ht.lo[:, k, cols],
                                        w[g % 2].hi[:, k, :], w[g % 2].lo[:, k, :], k == 0, k == KC - 1)
                    last.then_inc(s("acc_ready"), 1)

            @block.scalar
            def _(act):
                act.preload_act_table(ACT.Silu)
                starts = [min(n for n, (g, _) in enumerate(steps) if g == q) for q in range(len(jobs))]

                def high(g):
                    act.wait_ge(s("w_loaded"), 16 * (g + 1))
                    if g >= 2:
                        act.wait_ge(s("acc_ready"), starts[g - 1])
                    act.activation(w[g % 2].hi[:, :, :], raw[:, :, :], ACT.Copy).then_inc(s("w_hi"), 1)

                high(0)
                for n, (g, t) in enumerate(steps):
                    if n == starts[g] and g + 1 < len(jobs):
                        high(g + 1)
                    act.wait_ge(s("acc_ready"), n + 1)
                    if n >= 4:
                        act.wait_ge(s(f"stored{n % 4}"), 16 * (n // 4))
                    act.activation(out[n % 4][:, :], acc[n % 4][:, :], ACT.Copy if jobs[g][0] == "v" else ACT.Silu)\
                        .then_inc(s("out_ready"), 1)

            @block.vector
            def _(dve):
                for g in range(len(jobs)):
                    dve.wait_ge(s("w_hi"), g + 1)
                    dve.tensor_tensor(w[g % 2].lo[:, :, :], raw[:, :, :], w[g % 2].hi[:, :, :].bitcast(F32),
                                      ALU.subtract).then_inc(s("w_lo"), 1)
        ph.close()


def gla_keys(nc, d, ht, qk, cum):
    with ExitStack() as ctx:
        ph = Phase(nc, ctx, "glak")
        s = ph.sem
        raw = ph.sb("raw", [P, KC, P])
        w = [Split(nc, ctx, f"glak_w{b}", [P, KC, P]) for b in range(2)]
        lr_raw = ph.sb("lr_raw", [P, KC, 2, RANK])
        lr_w = Split(nc, ctx, "glak_lrw", [P, KC, 2, RANK])
        low = [ph.sb(f"low{r}", [RANK + 1, TOK]) for r in range(2)]
        up = [ph.sb(f"up{r}", [RANK + 1, HEADS * DK]) for r in range(2)]
        cums = ph.sb("cums", [P, 2, P])
        e = [ph.sb(f"e{b}", [P, HEADS * DK]) for b in range(2)]
        logs = [ph.sb(f"logs{b}", [P, HEADS * DK]) for b in range(2)]
        acc = [ph.ps(f"acc{g}", [P, N]) for g in range(3)]
        pz = [ph.ps(f"pz{b}", [P, N]) for b in range(2)]
        pc = [ph.ps(f"pc{b}", [P, N]) for b in range(2)]
        chunks = QK // P
        pairs = chunks // 2
        units = [(t, r) for t in range(TILES) for r in range(2)]

        with nc.Block() as block:
            @block.sync
            def _(sp):
                sp.dma_start(lr_raw[:, :, :, :].rearrange("p k r n -> p k (r n)"),
                             d.w_in[:, QK + VG:GLA_IN].rearrange("(k p) n -> p k n", p=P)).then_inc(s("lr_loaded"), 16)
                for r in range(2):
                    sp.dma_start(up[r][0:RANK, :], d.gk_up[r]).then_inc(s("up_loaded"), 16)
                    sp.dma_start(up[r][RANK:RANK + 1, :], d.gk_b[r:r + 1, :]).then_inc(s("up_loaded"), 16)
                sp.dma_start(cums[:, :, :], d.cums).then_inc(s("up_loaded"), 16)

                def load(b, i):
                    sp.dma_start(raw[:, :, :], d.w_in[:, ds((i * 2 + b) * P, P)].rearrange("(k p) n -> p k n", p=P))\
                        .then_inc(s(f"w_loaded{b}"), 16)

                load(0, 0)
                sp.wait_ge(s("w_lo0"), 1)
                load(1, 0)
                with sp.Fori(1, pairs) as i:
                    for b in range(2):
                        sp.wait_ge(s(f"w_lo{1 - b}"), i + b)
                        load(b, i)

            @block.gpsimd
            def _(pool):
                for r in range(2):
                    pool.memset(low[r][:, :], 1.0).then_inc(s("ones_set"), 1)

            @block.tensor
            def _(pe):
                pe.wait_ge(s("lr_lo"), 1)
                for r in range(2):
                    for g, (a, n) in enumerate(TOKEN_GROUPS):
                        if r:
                            pe.wait_ge(s("low_ready"), g + 1)
                        for k in range(KC):
                            last = product3(pe, acc[g][0:RANK, 0:n], lr_w.hi[:, k, r, :], lr_w.lo[:, k, r, :],
                                            ht.hi[:, k, a:a + n], ht.lo[:, k, a:a + n], k == 0, k == KC - 1)
                        last.then_inc(s("low_summed"), 1)

                def chunk(b, i, first):
                    pe.wait_ge(s(f"w_lo{b}"), i + 1)
                    for g, (a, n) in enumerate(TOKEN_GROUPS):
                        if first and b == 0:
                            pe.wait_ge(s("low_ready"), len(TOKEN_GROUPS) + g + 1)
                        else:
                            pe.wait_ge(s(f"qk_ready{g}{1 - b}"), i + b)
                        for k in range(KC):
                            last = product3(pe, acc[g][:, 0:n], w[b].hi[:, k, :], w[b].lo[:, k, :],
                                            ht.hi[:, k, a:a + n], ht.lo[:, k, a:a + n], k == 0, k == KC - 1)
                        last.then_inc(s(f"qk_summed{g}{b}"), 1)

                for b in range(2):
                    chunk(b, 0, True)
                with pe.Fori(1, pairs) as i:
                    for b in range(2):
                        chunk(b, i, False)

                pe.wait_ge(s("up_loaded"), 80)

                def sums(n):
                    t, r = units[n]
                    pe.wait_ge(s("logs_ready"), n + 1)
                    if n >= 2:
                        pe.wait_ge(s("cum_ready"), n - 1)
                    for h in range(HEADS):
                        last = pe.matmul(pc[n % 2][:, h * P:(h + 1) * P], logs[n % 2][:, h * DK:(h + 1) * DK],
                                         cums[:, r, :], start=True, stop=True)
                    last.then_inc(s("cum_summed"), 1)

                for n, (t, r) in enumerate(units):
                    if n >= 2:
                        pe.wait_ge(s("e_ready"), n - 1)
                        pe.wait_ge(s("z_ready"), n - 1)
                    pe.matmul(pz[n % 2][:, :], low[r][:, t * P:(t + 1) * P], up[r][:, :], start=True, stop=True)\
                        .then_inc(s("z_summed"), 1)
                    if n:
                        sums(n - 1)
                sums(len(units) - 1)

            @block.scalar
            def _(act):
                act.preload_act_table_set("natural_log_exp_and_others")
                act.wait_ge(s("lr_loaded"), 16)
                act.activation(lr_w.hi[:, :, :, :], lr_raw[:, :, :, :], ACT.Copy).then_inc(s("lr_hi"), 1)
                act.wait_ge(s("ones_set"), 2)
                for r in range(2):
                    for g, (a, n) in enumerate(TOKEN_GROUPS):
                        act.wait_ge(s("low_summed"), r * 3 + g + 1)
                        act.activation(low[r][0:RANK, a:a + n], acc[g][0:RANK, 0:n], ACT.Copy)\
                            .then_inc(s("low_ready"), 1)

                def high(b, i, first):
                    act.wait_ge(s(f"w_loaded{b}"), i * 16 + 16)
                    if not first:
                        act.wait_ge(s(f"qk_summed2{b}"), i)
                    act.activation(w[b].hi[:, :, :], raw[:, :, :], ACT.Copy).then_inc(s(f"w_hi{b}"), 1)

                def chunk(b, i):
                    for g, (a, n) in enumerate(TOKEN_GROUPS):
                        act.wait_ge(s(f"qk_summed{g}{b}"), i + 1)
                        act.activation(qk[:, ds(i * 2 + b, 1), a:a + n].rearrange("p o n -> p (o n)"),
                                       acc[g][:, 0:n], ACT.Copy).then_inc(s(f"qk_ready{g}{b}"), 1)

                for b in range(2):
                    high(b, 0, True)
                for b in range(2):
                    chunk(b, 0)
                with act.Fori(1, pairs) as i:
                    for b in range(2):
                        high(b, i, False)
                    for b in range(2):
                        chunk(b, i)

                for n, (t, r) in enumerate(units):
                    b = n % 2
                    act.wait_ge(s("z_summed"), n + 1)
                    if n >= 2:
                        act.wait_ge(s("logs_ready"), n - 1)
                    act.activation(e[b][:, :], pz[b][:, :], ACT.Abs).then_inc(s("e_ready"), 1)
                    act.wait_ge(s("e_ready"), n + 1)
                    act.activation(e[b][:, :], e[b][:, :], ACT.Exp, scale=-1.0).then_inc(s("e_exp"), 1)
                    act.wait_ge(s("e_exp"), n + 1)
                    act.activation(e[b][:, :], e[b][:, :], ACT.Ln, bias=1.0).then_inc(s("e_log"), 1)

            @block.vector
            def _(dve):
                dve.wait_ge(s("lr_hi"), 1)
                dve.tensor_tensor(lr_w.lo[:, :, :, :], lr_raw[:, :, :, :], lr_w.hi[:, :, :, :].bitcast(F32),
                                  ALU.subtract).then_inc(s("lr_lo"), 1)

                def lows(b, i):
                    dve.wait_ge(s(f"w_hi{b}"), i + 1)
                    dve.tensor_tensor(w[b].lo[:, :, :], raw[:, :, :], w[b].hi[:, :, :].bitcast(F32),
                                      ALU.subtract).then_inc(s(f"w_lo{b}"), 1)

                for b in range(2):
                    lows(b, 0)
                with dve.Fori(1, pairs) as i:
                    for b in range(2):
                        lows(b, i)

                def take(n):
                    t, r = units[n]
                    dve.wait_ge(s("cum_summed"), n + 1)
                    dve.tensor_copy(cum[:, r, :, t * P:(t + 1) * P],
                                    pc[n % 2][:, :].rearrange("p (h n) -> p h n", h=HEADS)).then_inc(s("cum_ready"), 1)

                for n, (t, r) in enumerate(units):
                    b = n % 2
                    dve.wait_ge(s("e_ready"), n + 1)
                    if n >= 2:
                        dve.wait_ge(s("cum_summed"), n - 1)
                    dve.tensor_scalar(logs[b][:, :], pz[b][:, :], 0.0, None, ALU.min).then_inc(s("z_ready"), 1)
                    dve.wait_ge(s("z_ready"), n + 1)
                    dve.wait_ge(s("e_log"), n + 1)
                    dve.tensor_tensor(logs[b][:, :], logs[b][:, :], e[b][:, :], ALU.subtract).then_inc(s("logs_ready"), 1)
                    if n:
                        take(n - 1)
                take(len(units) - 1)
        ph.close()


def gla_scan(nc, d, qk, cum):
    with ExitStack() as ctx:
        ph = Phase(nc, ctx, "scan")
        s = ph.sem
        v = [[ph.sb(f"v{r}{b}", [P, HEADS * DV]) for b in range(2)] for r in range(2)]
        names = ("cr", "cl", "eq", "ek", "el", "qi", "ki", "ks")
        t_ = {m: [ph.sb(f"{m}{r}", [P, HEADS, P]) for r in range(2)] for m in names}
        qs, es = ([[ph.sb(f"{m}{r}{b}", [P, HEADS, P]) for b in range(2)] for r in range(2)] for m in ("qs", "es"))
        att = [ph.sb(f"att{r}", [P, HEADS, P]) for r in range(2)]
        kst = [ph.sb(f"kst{r}", [P, HEADS, P]) for r in range(2)]
        state = [ph.sb(f"state{r}", [P, HEADS, DV]) for r in range(2)]
        o = [ph.sb(f"o{r}", [P, HEADS * DV]) for r in range(2)]
        seen = ph.sb("seen", [P, 2, CHUNK], I32)
        ident = ph.sb("ident", [P, P])
        patt = ph.ps("patt", [P, 2, HEADS, CHUNK])
        pkst = ph.ps("pkst", [P, HEADS, P])
        po = [ph.ps(f"po{r}", [P, HEADS, DV]) for r in range(2)]
        pds = ph.ps("pds", [P, HEADS, DV])

        def after(eng, what, r, st, per=1):
            if st.b == 1:
                eng.wait_ge(s(f"{what}{r}0"), st.n * per)
            elif not st.first:
                eng.wait_ge(s(f"{what}{r}1"), (st.n - 1) * per)

        def after_lat(eng, what, r, st, per=1):
            if st.b == 1:
                eng.wait_ge(s(f"{what}{r}0"), st.m * per)
            elif not st.first_lat:
                eng.wait_ge(s(f"{what}{r}1"), (st.m - 1) * per)

        def every_step(eng, body):
            for segment in SCAN:
                with eng.Fori(0, segment[3]) as i:
                    for now, then in scan_steps(i, segment):
                        body(now, then, segment[4])

        FIRST = Step(CTX, 0, 1, 0, CTX_TILES - 1, True, False)

        def order(r):
            return (0, 1) if r == 0 else (1, 0)

        def chunks(ap):
            return ap.rearrange("p h (c n) -> p h c n", c=2)

        WHOLE = [P, HEADS, 2, CHUNK]

        with nc.Block() as block:
            @block.sync
            def _(sp):
                sp.dma_start(seen[:, :, :], d.seen).then_inc(s("tables"), 16)
                sp.dma_start(ident[:, :], d.ident).then_inc(s("tables"), 16)

                def body(st, then, before):
                    for r in range(2):
                        if before:
                            sp.wait_ge(s(f"pds1{r}{st.b}"), (st.n - 1) * 2)
                        sp.dma_start(v[r][st.b][:, :], d.vd[ds(st.tile[r] * P, P), :])\
                            .then_inc(s(f"v_loaded{r}{st.b}"), 16)

                every_step(sp, body)

            @block.gpsimd
            def _(pool):
                for r in range(2):
                    pool.memset(att[r][:, :, :], 0.0).then_inc(s("zeroed"), 1)
                    pool.memset(state[r][:, :, :], 0.0).then_inc(s("zeroed"), 1)

                def keys(st):
                    for r in range(2):
                        cv = chunks(cum[:, r, :, ds(st.tile[r] * P, P)])
                        after(pool, "el", r, st)
                        pool.tensor_tensor(chunks(t_["cl"][r][:, :, :]),
                                           cv[:, :, :, LAST[r]:LAST[r] + 1].to_broadcast(WHOLE), cv,
                                           ALU.subtract).then_inc(s(f"cl{r}{st.b}"), 1)
                    for r in range(2):
                        pool.wait_ge(s(f"el{r}{st.b}"), st.n)
                        after(pool, "turned", r, st)
                        pool.tensor_tensor(t_["ks"][r][:, :, :], qk[:, HEADS:2 * HEADS, ds(st.tile[r] * P, P)],
                                           t_["el"][r][:, :, :], ALU.mult).then_inc(s(f"ks{r}{st.b}"), 1)

                def body(st, then, before):
                    if then:
                        keys(then)
                    if st.lat:
                        for r in range(2):
                            pool.wait_ge(s(f"o_ready{r}{st.b}"), st.m)
                            pool.dma_start(d.od[r, ds((st.tile[r] - CTX_TILES) * P, P), :], o[r][:, :])\
                                .then_inc(s(f"o_stored{r}{st.b}"), 16)

                keys(FIRST)
                every_step(pool, body)
                for b in range(2):
                    for r in range(2):
                        pool.wait_ge(s(f"o_stored{r}{b}"), 16 * (LAT_TILES // 2))

            @block.tensor
            def _(pe):
                pe.wait_ge(s("tables"), 32)

                def body(st, then, before):
                    n, m, b = st.n, st.m, st.b
                    if st.lat:
                        for r in range(2):
                            pe.wait_ge(s(f"qi{r}{b}"), m)
                            pe.wait_ge(s(f"ki{r}{b}"), m)
                            after_lat(pe, "masked", 1, st, 2)
                            for h in range(HEADS):
                                for c in range(2):
                                    at = slice(c * CHUNK, (c + 1) * CHUNK)
                                    last = pe.matmul(patt[at, r, h, :], t_["ki"][r][:, h, at],
                                                     t_["qi"][r][:, h, at], start=True, stop=True)
                            last.then_inc(s(f"scored{r}{b}"), 1)
                    for r in range(2):
                        pe.wait_ge(s(f"ks{r}{b}"), n)
                        if r == 1:
                            pe.wait_ge(s(f"kst0{b}"), n)
                        else:
                            after(pe, "kst", 1, st)
                        for h in range(HEADS):
                            last = pe.transpose(pkst[:, h, :], t_["ks"][r][:, h, :], ident[:, :])
                        last.then_inc(s(f"turned{r}{b}"), 1)
                    for j in range(2):
                        for r in range(2):
                            c = order(r)[j]
                            at = slice(c * CHUNK, (c + 1) * CHUNK)
                            if j == 0:
                                pe.wait_ge(s(f"v_loaded{r}{b}"), n * 16)
                            if st.lat:
                                if j == 0:
                                    pe.wait_ge(s(f"masked{r}{b}"), m * 2)
                                    after_lat(pe, "o_ready", r, st)
                                    for h in range(HEADS):
                                        pe.matmul(po[r][:, h, :], att[r][:, h, :],
                                                  v[r][b][:, h * DV:(h + 1) * DV], start=h % 2 == 0, stop=False)
                                for half in range(2):
                                    if j == 1:
                                        pe.wait_ge(s(f"state{half}{r}{b}"), n * 2 - 1)
                                    else:
                                        after(pe, f"state{half}", r, st, 2)
                                        pe.wait_ge(s(f"qs{r}{b}"), m)
                                for h in range(HEADS):
                                    last = pe.matmul(po[r][at, h, :], qs[r][b][:, h, at],
                                                     state[r][:, h, :], start=False, stop=h % 2 == 1)
                                if j == 1:
                                    last.then_inc(s(f"o_summed{r}{b}"), 1)
                            if j == 0:
                                pe.wait_ge(s(f"kst{r}{b}"), n)
                            for half in range(2):
                                if r == 1:
                                    pe.wait_ge(s(f"state{half}0{b}"), n * 2 - (1 - j))
                                elif j == 1:
                                    pe.wait_ge(s(f"state{half}1{b}"), n * 2 - 1)
                                else:
                                    after(pe, f"state{half}", 1, st, 2)
                                for h in range(half * 2, half * 2 + 2):
                                    last = pe.matmul(pds[:, h, :], kst[r][at, h, :],
                                                     v[r][b][at, h * DV:(h + 1) * DV], start=True, stop=True)
                                last.then_inc(s(f"pds{half}{r}{b}"), 1)

                every_step(pe, body)

            @block.scalar
            def _(act):
                act.preload_act_table(ACT.Exp)

                def exponentials(st, before):
                    b = st.b
                    for r in range(2):
                        act.wait_ge(s(f"cl{r}{b}"), st.n)
                        after(act, "ks", r, st)
                        act.activation(t_["el"][r][:, :, :], t_["cl"][r][:, :, :], ACT.Exp)\
                            .then_inc(s(f"el{r}{b}"), 1)
                        if before:
                            act.wait_ge(s(f"state1{r}{b}"), (st.n - 1) * 2)
                        act.activation(es[r][b][:, :, :], cum[:, r, :, ds(st.tile[r] * P, P)], ACT.Exp)\
                            .then_inc(s(f"es{r}{b}"), 1)
                        if st.lat:
                            act.wait_ge(s(f"cr{r}{b}"), st.m)
                            act.activation(t_["eq"][r][:, :, :], t_["cr"][r][:, :, :], ACT.Exp)\
                                .then_inc(s(f"eq{r}{b}"), 1)
                            act.activation(t_["ek"][r][:, :, :], t_["cr"][r][:, :, :], ACT.Exp, scale=-1.0)\
                                .then_inc(s(f"ek{r}{b}"), 1)

                def body(st, then, before):
                    b = st.b
                    for r in range(2):
                        act.wait_ge(s(f"turned{r}{b}"), st.n)
                        after(act, "pds1", r, st, 2)
                        act.activation(kst[r][:, :, :], pkst[:, :, :], ACT.Copy).then_inc(s(f"kst{r}{b}"), 1)
                    if then:
                        exponentials(then, before or then.b == 0)
                    if st.lat:
                        for r in range(2):
                            act.wait_ge(s(f"o_summed{r}{b}"), st.m)
                            after_lat(act, "o_stored", r, st, 16)
                            act.activation(o[r][:, :], po[r][:, :, :].rearrange("p h n -> p (h n)"), ACT.Copy)\
                                .then_inc(s(f"o_ready{r}{b}"), 1)

                exponentials(FIRST, 0)
                every_step(act, body)

            @block.vector
            def _(dve):
                dve.wait_ge(s("tables"), 32)
                dve.wait_ge(s("zeroed"), 4)

                def from_reference(st):
                    for r in range(2):
                        cv = chunks(cum[:, r, :, ds(st.tile[r] * P, P)])
                        after_lat(dve, "ek", r, st)
                        dve.tensor_tensor(chunks(t_["cr"][r][:, :, :]), cv,
                                          cv[:, :, :, REF[r]:REF[r] + 1].to_broadcast(WHOLE),
                                          ALU.subtract).then_inc(s(f"cr{r}{st.b}"), 1)

                def products(st, r, before):
                    b = st.b
                    q = qk[:, 0:HEADS, ds(st.tile[r] * P, P)]
                    k = qk[:, HEADS:2 * HEADS, ds(st.tile[r] * P, P)]
                    dve.wait_ge(s(f"eq{r}{b}"), st.m)
                    dve.scalar_tensor_tensor(t_["qi"][r][:, :, :], q, DK ** -0.5, t_["eq"][r][:, :, :],
                                             ALU.mult, ALU.mult).then_inc(s(f"qi{r}{b}"), 1)
                    dve.wait_ge(s(f"ek{r}{b}"), st.m)
                    dve.tensor_tensor(t_["ki"][r][:, :, :], k, t_["ek"][r][:, :, :], ALU.mult)\
                        .then_inc(s(f"ki{r}{b}"), 1)
                    dve.wait_ge(s(f"es{r}{b}"), st.n)
                    if before:
                        dve.wait_ge(s(f"o_summed{r}{b}"), st.m - 1)
                    dve.scalar_tensor_tensor(qs[r][b][:, :, :], q, DK ** -0.5, es[r][b][:, :, :],
                                             ALU.mult, ALU.mult).then_inc(s(f"qs{r}{b}"), 1)

                def decay(st, j, r):
                    end = order(r)[j] * CHUNK + LAST[r]
                    dve.wait_ge(s(f"es{r}{st.b}"), st.n)
                    for half in range(2):
                        dve.wait_ge(s(f"pds{half}{r}{st.b}"), st.n * 2 - (1 - j))
                        if j == 1:
                            dve.wait_ge(s(f"state{half}{r}{st.b}"), st.n * 2 - 1)
                        else:
                            after(dve, f"state{half}", r, st, 2)
                        for h in range(half * 2, half * 2 + 2):
                            last = dve.scalar_tensor_tensor(state[r][:, h, :], state[r][:, h, :],
                                                            es[r][st.b][:, h, end:end + 1], pds[:, h, :],
                                                            ALU.mult, ALU.add)
                        last.then_inc(s(f"state{half}{r}{st.b}"), 1)

                def body(st, then, before):
                    if st.lat:
                        for r in range(2):
                            dve.wait_ge(s(f"scored1{st.b}"), st.m)
                            dve.sem_inc(s("score_tiles"), 1)
                            for c in range(2):
                                at = slice(c * CHUNK, (c + 1) * CHUNK)
                                dve.copy_predicated(att[r][at, :, at],
                                                    seen[at, r:r + 1, :].to_broadcast([CHUNK, HEADS, CHUNK]),
                                                    patt[at, r, :, :]).then_inc(s(f"masked{r}{st.b}"), 1)
                    ahead = then is not None and then.lat
                    if ahead:
                        from_reference(then)
                    for r in range(2):
                        decay(st, 0, r)
                    for r in range(2):
                        if ahead:
                            products(then, r, before > 1 or (before == 1 and then.b == 0))
                        decay(st, 1, r)

                every_step(dve, body)
        ph.close()


PAIRS_AHEAD = [(CTX_TILES, 1, 0), (CTX_TILES + 2, 1, 1), (CTX_TILES + 4, LAT_TILES // 2 - 2, 2)]


def gla_output(nc, d):
    with ExitStack() as ctx:
        ph = Phase(nc, ctx, "wo")
        s = ph.sem
        weights = SquareWeights(ph, nc, ctx, "wo_w", d.w_o)
        w = weights.w
        ident = ph.sb("ident", [P, P])
        head_g = ph.sb("head_g", [P, D])
        res_gate = ph.sb("res_gate", [P, D])
        eps = ph.sb("eps", [P, 1])
        o = [[ph.sb(f"o{r}{b}", [P, HEADS, DV]) for b in range(2)] for r in range(2)]
        gate = [ph.sb(f"gate{b}", [P, HEADS, DV]) for b in range(2)]
        x = [ph.sb(f"x{b}", [P, D]) for b in range(2)]
        junk = ph.sb("junk", [P, HEADS, DV])
        stat = ph.sb("stat", [P, 2, 3, HEADS])
        ot = [Split(nc, ctx, f"wo_ot{b}", [P, KC, P]) for b in range(2)]
        y = [ph.sb(f"y{b}", [P, D]) for b in range(2)]
        pt = [ph.ps(f"pt{b}", [P, KC, P]) for b in range(2)]
        py = [ph.ps(f"py{b}", [P, D]) for b in range(2)]
        total = LAT_TILES // 2

        with nc.Block() as block:
            @block.sync
            def _(sp):
                sp.dma_start(ident[:, :], d.ident).then_inc(s("tables"), 16)
                sp.dma_start(head_g[:, :], d.head_g[0, :].partition_broadcast(P)).then_inc(s("tables"), 16)
                sp.dma_start(res_gate[:, :], d.mods[1, LAT, G1, :].partition_broadcast(P)).then_inc(s("tables"), 16)
                weights.load(sp)

                def load_x(b, n, row, before):
                    if before:
                        sp.wait_ge(s(f"stored{b}"), (n - 1) * 16)
                    sp.dma_start(x[b][:, :], d.xs[ds(row, P), :]).then_inc(s(f"x_loaded{b}"), 16)

                for t0, pairs, before in PAIRS_AHEAD:
                    with sp.Fori(0, pairs) as i:
                        n = i + (before + 1)
                        for b in range(2):
                            row = (i * 2 + (t0 + b - CTX_TILES)) * P
                            if before:
                                sp.wait_ge(s(f"turned{b}"), n - 1)
                            for r in range(2):
                                sp.dma_start(o[r][b][:, :, :].rearrange("p h n -> p (h n)"), d.od[r, ds(row, P), :])\
                                    .then_inc(s(f"o_loaded{b}"), 16)
                            sp.dma_start(gate[b][:, :, :].rearrange("p h n -> p (h n)"), d.gd[ds(row, P), :])\
                                .then_inc(s(f"o_loaded{b}"), 16)
                        for b in range(2):
                            if before:
                                load_x(b, n - 1, (i * 2 + (t0 + b - 2)) * P, before - 1)
                for b in range(2):
                    load_x(b, total, (TILES - 2 + b) * P, 1)

            @block.gpsimd
            def _(pool):
                weights.low(pool, 1)
                for st, t0, pairs, before in LAT_STREAMS:
                    with pool.Fori(0, pairs) as i:
                        for b in range(2):
                            pool.wait_ge(s(f"x_ready{b}"), i + (before + 1))
                            pool.dma_start(d.xs[ds((i * 2 + (t0 + b)) * P, P), :], x[b][:, :])\
                                .then_inc(s(f"stored{b}"), 16)
                for b in range(2):
                    pool.wait_ge(s(f"stored{b}"), 16 * total)

            @block.tensor
            def _(pe):
                def product(b, n, before):
                    pe.wait_ge(s(f"ot_lo{b}"), n)
                    if before:
                        pe.wait_ge(s(f"y_gated{b}"), n - 1)
                    for h in range(2):
                        cols = slice(h * N, (h + 1) * N)
                        for k in range(KC):
                            last = product3(pe, py[b][:, cols], ot[b].hi[:, k, :], ot[b].lo[:, k, :],
                                            w.hi[:, k, cols], w.lo[:, k, cols], k == 0, k == KC - 1)
                    last.then_inc(s(f"y_ready{b}"), 1)

                pe.wait_ge(s("tables"), 48)
                for t0, pairs, before in PAIRS_AHEAD:
                    with pe.Fori(0, pairs) as i:
                        n = i + (before + 1)
                        if before == 1:
                            weights.wait(pe)
                        if before:
                            product(0, n - 1, before - 1)
                        for b in range(2):
                            pe.wait_ge(s(f"gated{b}"), n)
                            if before:
                                pe.wait_ge(s(f"ot_lo{b}"), n - 1)
                            for k in range(KC):
                                h, c = divmod(k * P, DV)
                                last = pe.transpose(pt[b][:, k, :], o[0][b][:, h, c:c + P], ident[:, :])
                            last.then_inc(s(f"turned{b}"), 1)
                        if before:
                            product(1, n - 1, before - 1)
                for b in range(2):
                    product(b, total, 1)

            @block.scalar
            def _(act):
                act.preload_act_table(ACT.Sqrt)
                weights.high(act)
                act.wait_ge(s("eps_set"), 1)
                for t0, pairs, before in PAIRS_AHEAD:
                    with act.Fori(0, pairs) as i:
                        n = i + (before + 1)
                        for b in range(2):
                            act.wait_ge(s(f"o_added{b}"), n)
                            for h in range(HEADS):
                                last = act.activation(junk[:, h, :], o[0][b][:, h, :], ACT.Square,
                                                      accum_out=stat[:, b, 0, h:h + 1])
                            last.then_inc(s(f"squares{b}"), 1)
                            act.wait_ge(s(f"squares{b}"), n)
                            if before:
                                act.wait_ge(s(f"rstd{b}"), n - 1)
                            act.activation(stat[:, b, 1, :], stat[:, b, 0, :], ACT.Sqrt, bias=eps[:, :],
                                           scale=1.0 / DV).then_inc(s(f"root{b}"), 1)
                        for b in range(2):
                            act.wait_ge(s(f"turned{b}"), n)
                            if before:
                                act.wait_ge(s(f"y_ready{b}"), n - 1)
                            act.activation(ot[b].hi[:, :, :], pt[b][:, :, :], ACT.Copy).then_inc(s(f"ot_hi{b}"), 1)

            @block.vector
            def _(dve):
                def low(b, n):
                    dve.wait_ge(s(f"ot_hi{b}"), n)
                    dve.tensor_tensor(ot[b].lo[:, :, :], pt[b][:, :, :], ot[b].hi[:, :, :].bitcast(F32),
                                      ALU.subtract).then_inc(s(f"ot_lo{b}"), 1)

                def add(b, n):
                    dve.wait_ge(s(f"y_ready{b}"), n)
                    dve.tensor_tensor(y[b][:, :], py[b][:, :], res_gate[:, :], ALU.mult).then_inc(s(f"y_gated{b}"), 1)
                    dve.wait_ge(s(f"y_gated{b}"), n)
                    dve.wait_ge(s(f"x_loaded{b}"), n * 16)
                    dve.tensor_tensor(x[b][:, :], x[b][:, :], y[b][:, :], ALU.add).then_inc(s(f"x_ready{b}"), 1)

                dve.memset(eps[:, :], EPS).then_inc(s("eps_set"), 1)
                weights.low(dve, 0)
                dve.wait_ge(s("tables"), 48)
                for t0, pairs, before in PAIRS_AHEAD:
                    with dve.Fori(0, pairs) as i:
                        n = i + (before + 1)
                        for b in range(2):
                            dve.wait_ge(s(f"o_loaded{b}"), n * 48)
                            dve.tensor_tensor(o[0][b][:, :, :], o[0][b][:, :, :], o[1][b][:, :, :], ALU.add)\
                                .then_inc(s(f"o_added{b}"), 1)
                            dve.tensor_tensor(gate[b][:, :, :].rearrange("p h n -> p (h n)"),
                                              gate[b][:, :, :].rearrange("p h n -> p (h n)"), head_g[:, :], ALU.mult)\
                                .then_inc(s(f"gain{b}"), 1)
                        for b in range(2):
                            dve.wait_ge(s(f"root{b}"), n)
                            dve.reciprocal(stat[:, b, 2, :], stat[:, b, 1, :]).then_inc(s(f"rstd{b}"), 1)
                            dve.wait_ge(s(f"rstd{b}"), n)
                            dve.wait_ge(s(f"gain{b}"), n)
                            for h in range(HEADS):
                                last = dve.scalar_tensor_tensor(o[0][b][:, h, :], o[0][b][:, h, :],
                                                                stat[:, b, 2, h:h + 1], gate[b][:, h, :],
                                                                ALU.mult, ALU.mult)
                            last.then_inc(s(f"gated{b}"), 1)
                        if before:
                            add(0, n - 1)
                        low(0, n)
                        if before:
                            add(1, n - 1)
                        low(1, n)
                for b in range(2):
                    add(b, total)
        ph.close()

MAX_BLOCKS = 2 * TILES + EXPERTS
OUT_SHAPE = (1, SEQ, D)


def moe(nc, d, layer, streams, rows=None):
    with ExitStack() as ctx:
        plan = Plan(nc, ctx, layer, TILES - streams[0][1])
        with ExitStack() as inner:
            ht = Split(nc, inner, f"ht_moe{layer}", [P, KC, TOK])
            normalise(nc, d, layer, 1, streams, ht, d.hd)
            route(nc, d, layer, streams, ht, plan)
        experts(nc, d, layer, plan)
        ht_next = rows and Split(nc, rows, f"ht_next{layer}", [P, KC, TOK], side="right")
        combine(nc, d, layer, streams, plan, ht_next)
    return ht_next


def conv_layer(nc, d, cs):
    with ExitStack() as ctx:
        vt = ctx.enter_context(nc.sbuf_tensor("taps_out", [P, KC, CONV_OUT], F32))
        vecs = ctx.enter_context(nc.sbuf_tensor("channel_vectors", [P, KC, VEC_ROWS], F32))
        with ExitStack() as inner:
            ht = Split(nc, inner, "ht_conv", [P, KC, TOK])
            normalise(nc, d, 0, 0, STREAMS, ht)
            conv_taps(nc, d, ht, vt, vecs, cs)
        conv_out(nc, d, vt, vecs)


def gla_layer(nc, d, rows, ht):
    with ExitStack() as ctx:
        gla_values(nc, d, ht)
        qk = ctx.enter_context(nc.sbuf_tensor("qk", [P, 2 * HEADS, TOK], F32))
        cum = ctx.enter_context(nc.sbuf_tensor("cum", [P, 2, HEADS, TOK], F32))
        gla_keys(nc, d, ht, qk, cum)
        rows.close()
        gla_scan(nc, d, qk, cum)
    gla_output(nc, d)


def program(nc, d):
    Phase.pool_dma = []
    with ExitStack() as ctx:
        cs = ctx.enter_context(nc.sbuf_tensor("silu_c", [P, KC, 2], F32))
        modulation(nc, d, cs)
        conv_layer(nc, d, cs)
    with ExitStack() as rows:
        ht = moe(nc, d, 0, STREAMS, rows)
        gla_layer(nc, d, rows, ht)
    moe(nc, d, 1, LAT_STREAMS)


class Dram:

    def __init__(self, nc, a, out):
        def scratch(name, shape, dt=F32):
            return nc.dram_tensor("scratch_" + name, shape, dt, kind="Internal").ap()

        self.x, self.c, self.ctx, self.c_ctx = a["in_x"], a["in_c"], a["in_ctx"], a["in_c_ctx"]
        self.ada_w, self.ada_b, self.norm_g, self.final_g = a["in_ada_w"], a["in_ada_b"], a["in_norm_g"], a["in_final_g"]
        self.pw1_w, self.pw1_b = a["in_conv_pw1_w"][0], a["in_conv_pw1_b"]
        self.dw_w, self.dw_b = a["in_conv_dw_w"][0], a["in_conv_dw_b"]
        self.ln_g, self.ln_b = a["in_conv_ln_g"], a["in_conv_ln_b"]
        self.pw2_w, self.pw2_b = a["in_conv_pw2_w"][0], a["in_conv_pw2_b"]
        self.w_in, self.gk_up, self.gk_b = a["in_gla_w_in"][0], a["in_gla_gk_up"][0], a["in_gla_gk_b"][0]
        self.head_g, self.w_o = a["in_gla_head_g"], a["in_gla_w_o"][0]
        self.wg, self.bg, self.wr, self.br = a["in_moe_wg"], a["in_moe_bg"], a["in_moe_wr"], a["in_moe_br"]
        self.w1, self.w3, self.w2 = a["in_moe_w1"], a["in_moe_w3"], a["in_moe_w2"]
        self.pos_row, self.pos_col, self.ident = a["const_pos_row"], a["const_pos_col"], a["const_ident"]
        self.mean_w, self.ones, self.before = a["const_mean_w"], a["const_ones"], a["const_before"]
        self.iota, self.token, self.next_expert = a["const_iota"], a["const_token"], a["const_next_expert"]
        self.cums, self.seen = a["const_cums"], a["const_seen"]
        self.out = out if len(out.shape) == 2 else out[0]
        self.xs = scratch("residual", (TOK, D))
        self.mods = scratch("modulation", (2, 2, 6, D))
        self.hd = scratch("experts_in", (TOK, D))
        self.vd = scratch("gla_values", (TOK, D))
        self.gd = scratch("gla_gates", (SEQ, D))
        self.od = scratch("gla_out", (2, SEQ, D))
        self.yd = scratch("experts_out", (MAX_BLOCKS * BLK, D))


_INS = ['x', 'c', 'ctx', 'c_ctx', 'ada_w', 'ada_b', 'norm_g', 'final_g', 'conv_pw1_w', 'conv_pw1_b', 'conv_dw_w',
        'conv_dw_b', 'conv_ln_g', 'conv_ln_b', 'conv_pw2_w', 'conv_pw2_b', 'gla_w_in', 'gla_gk_up', 'gla_gk_b',
        'gla_head_g', 'gla_w_o', 'moe_wg', 'moe_bg', 'moe_wr', 'moe_br', 'moe_w1', 'moe_w3', 'moe_w2']


def shape_tables():
    quarter = D // 4
    omega = (1.0 / (10000.0 ** (np.arange(quarter, dtype=np.float32) / np.float32(quarter)))).astype(np.float32)
    ar = np.arange(SEQ // GRID_W, dtype=np.float32)[:, None] * omega
    ac = np.arange(GRID_W, dtype=np.float32)[:, None] * omega
    k = np.arange(P)
    same = (k[:, None] // CHUNK) == (k[None, :] // CHUNK)
    order = np.arange(EXPERTS).reshape(GROUPS, PER_GROUP).T.reshape(-1)
    return {
        'next_expert': np.diff(order, append=order[-1:]).astype(np.float32)[None, :],
        'pos_row': np.concatenate([np.sin(ar), np.cos(ar)], axis=1).astype(np.float32),
        'pos_col': np.concatenate([np.sin(ac), np.cos(ac)], axis=1).astype(np.float32),
        'ident': np.eye(P, dtype=np.float32),
        'mean_w': np.full((P, P), 1.0 / D, np.float32),
        'ones': np.ones((P, P), np.float32),
        'before': (k[:, None] < k[None, :]).astype(np.float32),
        'iota': np.broadcast_to(np.arange(P, dtype=np.float32), (P, P)).copy(),
        'token': (np.arange(TILES, dtype=np.float32)[None, :] * P + k[:, None].astype(np.float32) + 1).astype(np.float32),
        'cums': np.stack([(same & (k[:, None] <= k[None, :])).astype(np.float32) / 16.0,
                          (same & (k[:, None] >= k[None, :])).astype(np.float32) / 16.0], axis=1),
        'seen': np.stack([np.tile((k[:CHUNK, None] <= k[None, :CHUNK]), (2, 1)),
                          np.tile((k[:CHUNK, None] >= k[None, :CHUNK]), (2, 1))], axis=1).astype(np.int32),
    }


def kernel(**inputs):
    import concourse.bacc as _bacc
    from concourse.bass_utils import run_bass_kernel_spmd as _run

    nc = _bacc.Bacc("TRN2", target_bir_lowering=False, num_devices=1)
    arrays, args = {}, {}
    for name in _INS:
        arrays["in_" + name] = np.ascontiguousarray(inputs[name])
    for name, table in shape_tables().items():
        arrays["const_" + name] = np.ascontiguousarray(table)
    for name, a in arrays.items():
        args[name] = nc.dram_tensor(name, a.shape, mybir.dt.from_np(a.dtype), kind="ExternalInput").ap()
    out = nc.dram_tensor("out", OUT_SHAPE, F32, kind="ExternalOutput").ap()
    program(nc, Dram(nc, args, out))
    r = _run(nc, [arrays], core_ids=[0])
    return r.results[0]["out"]
```
